# Optimizing a Trainium2 kernel written in Bass

```python
import jax
import jax.numpy as jnp
from jax import lax
import numpy as np
import math
import jax, jax.numpy as jnp

D_MODEL = 1024
BATCH = 1
SEQ = 1024
DEPTH = 1

GRID_W = 64
CTX_LEN = 256
EPS = 1e-6
HG_HEADS = 4
HG_DIM = 128
HG_WIDTH = HG_HEADS * HG_DIM
CHUNK = 32
ATT_HEADS = 8
ATT_KV_HEADS = 2
HEAD_DIM = 64
ATT_WIDTH = ATT_HEADS * HEAD_DIM
KV_WIDTH = ATT_KV_HEADS * HEAD_DIM
WINDOW = 128
BLOCK = 128
ROPE_THETA = 10000.0
D_FF = ((8 * D_MODEL + 3 * 256 - 1) // (3 * 256)) * 256
CTX_COLS = 3 * HG_WIDTH + 2 * KV_WIDTH
IN_COLS = CTX_COLS + 2 * HG_WIDTH + ATT_WIDTH + 2 * D_MODEL


def _rmsnorm(x, w):
    xf = x.astype(jnp.float32)
    y = xf * lax.rsqrt(jnp.mean(xf * xf, axis=-1, keepdims=True) + EPS)
    return (y * w.astype(jnp.float32)).astype(x.dtype)

def _modulate(x, w, shift, scale):
    return _rmsnorm(x, w) * (1.0 + scale) + shift

def _heads(t, n_heads, head_dim):
    return t.reshape(t.shape[0], t.shape[1], n_heads, head_dim)

def _split_ctx_side(p):
    a, b, c_, d = HG_WIDTH, 2 * HG_WIDTH, 3 * HG_WIDTH, 3 * HG_WIDTH + KV_WIDTH
    return p[..., :a], p[..., a:b], p[..., b:c_], p[..., c_:d], p[..., d:CTX_COLS]

def _split_query_side(p):
    a = CTX_COLS + HG_WIDTH
    b = a + HG_WIDTH
    c_ = b + ATT_WIDTH
    return p[..., CTX_COLS:a], p[..., a:b], p[..., b:c_], p[..., c_:IN_COLS]

def _gla_chunkwise(q, k, v, log_f, s0):
    b_, s_, h_, dk = k.shape
    dv = v.shape[-1]
    n = s_ // CHUNK

    def chunks(t):
        return t.astype(jnp.float32).reshape(b_, n, CHUNK, h_, t.shape[-1]).transpose(0, 3, 1, 2, 4)

    k, v, log_f = chunks(k), chunks(v), chunks(log_f)
    cum = jnp.cumsum(log_f, axis=3)
    cum_last = cum[:, :, :, -1:, :]
    u = jnp.einsum('bhnck,bhncv->bhnkv', k * jnp.exp(cum_last - cum), v)
    decay = jnp.exp(cum_last[:, :, :, 0, :])

    def step(state, inp):
        d, un = inp
        return d[..., None] * state + un, state

    s_final, s_start = lax.scan(step, s0.astype(jnp.float32),
                                (jnp.moveaxis(decay, 2, 0), jnp.moveaxis(u, 2, 0)))
    if q is None:
        return None, s_final
    s_start = jnp.moveaxis(s_start, 0, 2)
    qd = chunks(q) * jnp.exp(cum)
    scores = jnp.einsum('bhnck,bhnsk->bhncs', qd, k * jnp.exp(-cum))
    lower_tri = jnp.tril(jnp.ones((CHUNK, CHUNK), dtype=bool))
    scores = jnp.where(lower_tri, scores, 0.0)
    o = (jnp.einsum('bhncs,bhnsv->bhncv', scores, v)
         + jnp.einsum('bhnck,bhnkv->bhncv', qd, s_start))
    o = o.transpose(0, 2, 3, 1, 4).reshape(b_, s_, h_, dv)
    return o, s_final

def _hgrn_query(q_raw):
    return _heads(jax.nn.silu(q_raw.astype(jnp.float32)) * HG_DIM ** -0.5, HG_HEADS, HG_DIM)

def _hgrn_direction(q, f_logit, inp, lb, s0, reverse):
    f = lb + (1.0 - lb) * jax.nn.sigmoid(f_logit.astype(jnp.float32))
    log_f = _heads(jnp.log(f), HG_HEADS, HG_DIM)
    k = _heads(1.0 - f, HG_HEADS, HG_DIM)
    v = _heads(inp, HG_HEADS, HG_DIM)
    if reverse:
        q = None if q is None else jnp.flip(q, 1)
        k, v, log_f = jnp.flip(k, 1), jnp.flip(v, 1), jnp.flip(log_f, 1)
    o, s = _gla_chunkwise(q, k, v, log_f, s0)
    if reverse and o is not None:
        o = jnp.flip(o, 1)
    return o, s

def _hgrn_readout(o, g_raw, norm_w, dtype):
    g = _heads(g_raw, HG_HEADS, HG_DIM).astype(jnp.float32)
    y = _rmsnorm(o, norm_w) * jax.nn.silu(g)
    return y.reshape(o.shape[0], o.shape[1], HG_WIDTH).astype(dtype)

def _rope_1d(t, pos):
    d = t.shape[-1]
    inv_freq = ROPE_THETA ** (-jnp.arange(0, d, 2, dtype=jnp.float32) / d)
    ang = pos.astype(jnp.float32)[:, None] * inv_freq[None, :]
    cos = jnp.cos(ang)[None, :, None, :]
    sin = jnp.sin(ang)[None, :, None, :]
    tf = t.astype(jnp.float32)
    t1, t2 = tf[..., : d // 2], tf[..., d // 2:]
    return jnp.concatenate([t1 * cos - t2 * sin, t1 * sin + t2 * cos], axis=-1)

def _axial_rope(t, rows, cols):
    half = t.shape[-1] // 2
    return jnp.concatenate([_rope_1d(t[..., :half], rows), _rope_1d(t[..., half:], cols)],
                           axis=-1).astype(t.dtype)

def _window_attention(q, k, v, kc, vc, sinks):
    b_, s_, hq, dh = q.shape
    hkv = k.shape[2]
    grp = hq // hkv
    nb = s_ // BLOCK
    f32 = jnp.float32
    qb = q.astype(f32).reshape(b_, nb, BLOCK, hkv, grp, dh) * dh ** -0.5

    def band(t):
        tp = jnp.pad(t.astype(f32), ((0, 0), (BLOCK, BLOCK), (0, 0), (0, 0)))
        tp = tp.reshape(b_, nb + 2, BLOCK, hkv, dh)
        return jnp.concatenate([tp[:, :-2], tp[:, 1:-1], tp[:, 2:]], axis=2)

    kw, vw = band(k), band(v)
    s_loc = jnp.einsum('bnqhgd,bnkhd->bnhgqk', qb, kw)
    qi = jnp.arange(BLOCK)[:, None]
    kj = jnp.arange(3 * BLOCK)[None, :]
    k_pos = (jnp.arange(nb)[:, None, None] - 1) * BLOCK + kj[None]
    valid = (jnp.abs(kj - BLOCK - qi) <= WINDOW)[None] & (k_pos >= 0) & (k_pos < s_)
    s_loc = jnp.where(valid[None, :, None, None], s_loc, -jnp.inf)
    s_ctx = jnp.einsum('bnqhgd,blhd->bnhgql', qb, kc.astype(f32))
    sink = jnp.broadcast_to(sinks.astype(f32).reshape(1, 1, hkv, grp, 1, 1), s_loc.shape[:-1] + (1,))
    p = jax.nn.softmax(jnp.concatenate([s_loc, s_ctx, sink], axis=-1), axis=-1)
    n_loc = 3 * BLOCK
    n_ctx = kc.shape[1]
    o = (jnp.einsum('bnhgqk,bnkhd->bnqhgd', p[..., :n_loc], vw)
         + jnp.einsum('bnhgql,blhd->bnqhgd', p[..., n_loc:n_loc + n_ctx], vc.astype(f32)))
    return o.reshape(b_, s_, hq * dh).astype(v.dtype)

def _context_attention(qc, kc, vc, sinks):
    b_, l_, hq, dh = qc.shape
    hkv = kc.shape[2]
    grp = hq // hkv
    f32 = jnp.float32
    qg = qc.astype(f32).reshape(b_, l_, hkv, grp, dh) * dh ** -0.5
    s = jnp.einsum('blhgd,bmhd->bhglm', qg, kc.astype(f32))
    sink = jnp.broadcast_to(sinks.astype(f32).reshape(1, hkv, grp, 1, 1), s.shape[:-1] + (1,))
    p = jax.nn.softmax(jnp.concatenate([s, sink], axis=-1), axis=-1)
    o = jnp.einsum('bhglm,bmhd->blhgd', p[..., :l_], vc.astype(f32))
    return o.reshape(b_, l_, hq * dh).astype(vc.dtype)

def _merge(y_hg, y_at, gates, w_bh, w_ba, w_o):
    g_hg, g_at = jnp.split(gates, 2, axis=-1)
    mixed = jax.nn.sigmoid(g_hg) * (y_hg @ w_bh) + jax.nn.sigmoid(g_at) * (y_at @ w_ba)
    return mixed @ w_o

def _swiglu(h, w_gate, w_up, w_down):
    return (jax.nn.silu(h @ w_gate) * (h @ w_up)) @ w_down

def first_inputs(seed: int = 0) -> dict:
    key = jax.random.key(seed)
    ks = jax.random.split(key, 20)
    f32 = jnp.float32

    def nrm(k, shape, scale):
        return jax.random.normal(k, shape, f32) * scale

    return {
        'x': nrm(ks[0], (BATCH, SEQ, D_MODEL), 1.0),
        'c': nrm(ks[1], (BATCH, D_MODEL), 1.0),
        'ctx': nrm(ks[2], (BATCH, CTX_LEN, D_MODEL), 1.0),
        'c_ctx': nrm(ks[3], (D_MODEL,), 1.0),
        'w_ada': nrm(ks[4], (DEPTH, D_MODEL, 6 * D_MODEL), 0.5 * D_MODEL ** -0.5),
        'b_ada': nrm(ks[5], (DEPTH, 6 * D_MODEL), 0.02),
        'norm_mix_w': 1.0 + nrm(ks[6], (DEPTH, D_MODEL), 0.02),
        'norm_ffn_w': 1.0 + nrm(ks[7], (DEPTH, D_MODEL), 0.02),
        'w_in': nrm(ks[8], (DEPTH, D_MODEL, IN_COLS), D_MODEL ** -0.5),
        'hgrn_lb_logits': nrm(ks[9], (2, DEPTH + 1, HG_WIDTH), 0.5),
        'hgrn_norm_w': 1.0 + nrm(ks[10], (DEPTH, HG_DIM), 0.02),
        'q_norm_w': 1.0 + nrm(ks[11], (DEPTH, HEAD_DIM), 0.02),
        'k_norm_w': 1.0 + nrm(ks[12], (DEPTH, HEAD_DIM), 0.02),
        'attn_sinks': nrm(ks[13], (DEPTH, ATT_HEADS), 0.5),
        'w_branch_hgrn': nrm(ks[14], (DEPTH, HG_WIDTH, D_MODEL), HG_WIDTH ** -0.5),
        'w_branch_attn': nrm(ks[15], (DEPTH, ATT_WIDTH, D_MODEL), ATT_WIDTH ** -0.5),
        'w_out': nrm(ks[16], (DEPTH, D_MODEL, D_MODEL), D_MODEL ** -0.5),
        'w_ffn_gate': nrm(ks[17], (DEPTH, D_MODEL, D_FF), D_MODEL ** -0.5),
        'w_ffn_up': nrm(ks[18], (DEPTH, D_MODEL, D_FF), D_MODEL ** -0.5),
        'w_ffn_down': nrm(ks[19], (DEPTH, D_FF, D_MODEL), D_FF ** -0.5),
    }

def first_block(x, c, ctx, c_ctx, w_ada, b_ada, norm_mix_w, norm_ffn_w, w_in, hgrn_lb_logits,
              hgrn_norm_w, q_norm_w, k_norm_w, attn_sinks, w_branch_hgrn, w_branch_attn,
              w_out, w_ffn_gate, w_ffn_up, w_ffn_down):
    n_lat = x.shape[1]
    ROWS = n_lat // GRID_W
    rows = jnp.repeat(jnp.arange(ROWS), GRID_W)
    cols = jnp.tile(jnp.arange(GRID_W), ROWS)
    lower_bounds = jnp.cumsum(jax.nn.softmax(hgrn_lb_logits.astype(jnp.float32), axis=1), axis=1)

    for layer in range(DEPTH):
        last = layer == DEPTH - 1
        mod = jax.nn.silu(c) @ w_ada[layer] + b_ada[layer]
        mod_c = jax.nn.silu(c_ctx) @ w_ada[layer] + b_ada[layer]
        sh1, sc1, g1, sh2, sc2, g2 = [m[:, None, :] for m in jnp.split(mod, 6, axis=-1)]
        csh1, csc1, cg1, csh2, csc2, cg2 = jnp.split(mod_c, 6, axis=-1)
        lb_fwd, lb_bwd = lower_bounds[0, layer], lower_bounds[1, layer]

        h = _modulate(x, norm_mix_w[layer], sh1, sc1)
        hc = _modulate(ctx, norm_mix_w[layer], csh1, csc1)
        p = h @ w_in[layer]
        pc = hc @ (w_in[layer, :, :CTX_COLS] if last else w_in[layer])

        cf_fwd, cf_bwd, c_inp, c_k, c_v = _split_ctx_side(pc)
        s0 = jnp.zeros((ctx.shape[0], HG_HEADS, HG_DIM, HG_DIM), jnp.float32)
        c_q_hg = None if last else _hgrn_query(_split_query_side(pc)[0])
        co_fwd, cs_fwd = _hgrn_direction(c_q_hg, cf_fwd, c_inp, lb_fwd, s0, False)
        co_bwd, cs_bwd = _hgrn_direction(c_q_hg, cf_bwd, c_inp, lb_bwd, s0, True)
        ck = _rmsnorm(_heads(c_k, ATT_KV_HEADS, HEAD_DIM), k_norm_w[layer])
        cv = _heads(c_v, ATT_KV_HEADS, HEAD_DIM)

        f_fwd, f_bwd, inp, k_raw, v_raw = _split_ctx_side(p)
        q_hg_raw, g_hg, q_raw, gates = _split_query_side(p)
        q_hg = _hgrn_query(q_hg_raw)
        o_fwd, _ = _hgrn_direction(q_hg, f_fwd, inp, lb_fwd, cs_fwd, False)
        o_bwd, _ = _hgrn_direction(q_hg, f_bwd, inp, lb_bwd, cs_bwd, True)
        y_hg = _hgrn_readout(o_fwd + o_bwd, g_hg, hgrn_norm_w[layer], x.dtype)
        q = _axial_rope(_rmsnorm(_heads(q_raw, ATT_HEADS, HEAD_DIM), q_norm_w[layer]), rows, cols)
        k = _axial_rope(_rmsnorm(_heads(k_raw, ATT_KV_HEADS, HEAD_DIM), k_norm_w[layer]), rows, cols)
        y_at = _window_attention(q, k, _heads(v_raw, ATT_KV_HEADS, HEAD_DIM), ck, cv, attn_sinks[layer])
        x_new = x + g1 * _merge(y_hg, y_at, gates, w_branch_hgrn[layer], w_branch_attn[layer], w_out[layer])
        x_new = x_new + g2 * _swiglu(_modulate(x_new, norm_ffn_w[layer], sh2, sc2),
                                     w_ffn_gate[layer], w_ffn_up[layer], w_ffn_down[layer])

        if not last:
            _, cg_hg, cq_raw, c_gates = _split_query_side(pc)
            cy_hg = _hgrn_readout(co_fwd + co_bwd, cg_hg, hgrn_norm_w[layer], ctx.dtype)
            cq = _rmsnorm(_heads(cq_raw, ATT_HEADS, HEAD_DIM), q_norm_w[layer])
            cy_at = _context_attention(cq, ck, cv, attn_sinks[layer])
            ctx = ctx + cg1 * _merge(cy_hg, cy_at, c_gates, w_branch_hgrn[layer],
                                     w_branch_attn[layer], w_out[layer])
            ctx = ctx + cg2 * _swiglu(_modulate(ctx, norm_ffn_w[layer], csh2, csc2),
                                      w_ffn_gate[layer], w_ffn_up[layer], w_ffn_down[layer])
        x = x_new
    return x


_first_inputs = first_inputs


def first_inputs(seed=0):
    import zlib

    import numpy as np

    out = dict(_first_inputs(seed))
    spreads = {}
    factors = {}
    for name, (base, spread) in spreads.items():
        noise = np.random.default_rng([zlib.crc32(name.encode()), seed]).standard_normal(out[name].shape)
        drawn = base * np.exp(spread * noise) if base else spread * noise
        out[name] = jnp.asarray(drawn.astype(out[name].dtype))
    for name, factor in factors.items():
        out[name] = (out[name] * factor).astype(out[name].dtype)
    return out


_narrow_inputs = first_inputs


def first_inputs(seed=0):

    out = dict(_narrow_inputs(seed))
    wider = {'ctx': 6.59,
     'b_ada': 3.26,
     'norm_mix_w': 12.0,
     'norm_ffn_w': 10.02,
     'hgrn_lb_logits': 12.0,
     'hgrn_norm_w': 12.0,
     'q_norm_w': 12.0,
     'k_norm_w': 12.0,
     'attn_sinks': 12.0}
    for name, times in wider.items():
        mean = out[name].mean()
        out[name] = (mean + times * (out[name] - mean)).astype(out[name].dtype)
    return out


N_GROUPS = 4
GROUP_W = D_MODEL // N_GROUPS
MIX_W = N_GROUPS * GROUP_W
SSD_HEAD_DIM = 64
SSD_HEADS = GROUP_W // SSD_HEAD_DIM
SSD_BC_GROUPS = 2
SSD_STATE = 128
SSD_CONV = 3
SSD_CHUNK = 128
SSD_XBC = GROUP_W + 2 * SSD_BC_GROUPS * SSD_STATE
SSD_IN = GROUP_W + SSD_XBC + 2 * SSD_HEADS
NA_HEAD_DIM = 64
NA_HEADS = GROUP_W // NA_HEAD_DIM
NA_KH = 8
NA_KW = 16
NA_QB = 16
NA_KSPAN = 32
NA_IN = 3 * GROUP_W
ML_HEAD_DIM = 64
ML_HEADS = GROUP_W // ML_HEAD_DIM
ML_CHUNK = 128
ML_IN = 4 * GROUP_W + 4 * ML_HEADS
HY_CH = GROUP_W
HY_ORDER = 2
HY_CONV = 3
HY_EMB = 33
HY_FFN = 64
HY_SHORT_DECAY_FRAC = 0.3
HY_LONG_DECAY_FRAC = 1.5
HY_DECAY_TARGET = 1e-2
HY_IN = 3 * HY_CH
OFF_NA = SSD_IN
OFF_ML = OFF_NA + NA_IN
OFF_HY = OFF_ML + ML_IN
P_IN = OFF_HY + HY_IN
FFN_HIDDEN = int(math.ceil(8 * D_MODEL / 3 / 256)) * 256
NORM_EPS = 1e-6


F32 = jnp.float32

def rms_norm(x, gain=None):
    xf = x.astype(F32)
    y = xf * lax.rsqrt(jnp.mean(xf * xf, axis=-1, keepdims=True) + NORM_EPS)
    if gain is not None:
        y = y * gain.astype(F32)
    return y.astype(x.dtype)

def depthwise_conv(x, w, b):
    K = w.shape[0]
    y = lax.conv_general_dilated(x, w[:, None, :].astype(x.dtype), window_strides=(1,),
                                 padding=[(K // 2, K // 2)],
                                 dimension_numbers=('NWC', 'WIO', 'NWC'),
                                 feature_group_count=x.shape[-1])
    return y + b.astype(x.dtype)

def ssd_chunk_scan(x, dt, A, Bm, Cm):
    b, L, H, P = x.shape
    N = Bm.shape[-1]
    T = SSD_CHUNK
    nc = L // T
    x = x.reshape(b, nc, T, H, P)
    Bm = Bm.reshape(b, nc, T, H, N)
    Cm = Cm.reshape(b, nc, T, H, N)
    dt = dt.reshape(b, nc, T, H)
    a_cum = jnp.cumsum(jnp.moveaxis(dt * A, -1, 1), axis=-1)
    xdt = x * dt[..., None]
    lower = jnp.tril(jnp.ones((T, T), bool))
    decay = jnp.exp(jnp.where(lower, a_cum[..., :, None] - a_cum[..., None, :], -jnp.inf))
    scores = jnp.einsum('bcthn,bcshn->bhcts', Cm, Bm) * decay
    y_diag = jnp.einsum('bhcts,bcshp->bcthp', scores, xdt)
    decay_to_end = jnp.exp(a_cum[..., -1:] - a_cum)
    chunk_states = jnp.einsum('bcshn,bhcs,bcshp->bchpn', Bm, decay_to_end, xdt)
    chunk_decay = jnp.exp(a_cum[..., -1])

    def step(state, inp):
        s_c, d_c = inp
        return state * d_c[..., None, None] + s_c, state

    _, prev = lax.scan(step, jnp.zeros((b, H, P, N), x.dtype),
                       (jnp.moveaxis(chunk_states, 1, 0), jnp.moveaxis(chunk_decay, 2, 0)))
    prev = jnp.moveaxis(prev, 0, 1)
    y_off = jnp.einsum('bcthn,bchpn,bhct->bcthp', Cm, prev, jnp.exp(a_cum))
    return (y_diag + y_off).reshape(b, L, H, P)

def ssd_mixer(u, conv_w, conv_b, dt_bias, a_log, d_skip, norm_g):
    b, L, _ = u.shape
    z = u[..., :GROUP_W]
    xbc = jax.nn.silu(depthwise_conv(u[..., GROUP_W:GROUP_W + SSD_XBC], conv_w, conv_b)).astype(F32)
    dt_raw = u[..., GROUP_W + SSD_XBC:].astype(F32).reshape(b, L, 2, SSD_HEADS)
    xs = xbc[..., :GROUP_W].reshape(b, L, SSD_HEADS, SSD_HEAD_DIM)
    rep = SSD_HEADS // SSD_BC_GROUPS
    nb = SSD_BC_GROUPS * SSD_STATE
    Bm = jnp.repeat(xbc[..., GROUP_W:GROUP_W + nb].reshape(b, L, SSD_BC_GROUPS, SSD_STATE), rep, axis=2)
    Cm = jnp.repeat(xbc[..., GROUP_W + nb:].reshape(b, L, SSD_BC_GROUPS, SSD_STATE), rep, axis=2)
    dt = jax.nn.softplus(dt_raw + dt_bias.astype(F32))
    A = -jnp.exp(a_log.astype(F32))
    flip = lambda t: jnp.flip(t, axis=1)
    y_fwd = ssd_chunk_scan(xs, dt[:, :, 0], A[0], Bm, Cm)
    y_bwd = flip(ssd_chunk_scan(flip(xs), flip(dt[:, :, 1]), A[1], flip(Bm), flip(Cm)))
    y = y_fwd + y_bwd + d_skip.astype(F32)[:, None] * xs
    y = y.reshape(b, L, GROUP_W) * jax.nn.silu(z.astype(F32))
    return rms_norm(y, norm_g).astype(u.dtype)

def neighborhood_attention(u, rpb):
    b, L, _ = u.shape
    rows = L // GRID_W
    kh = min(NA_KH, rows)
    q, k, v = [t.reshape(b, rows, GRID_W, NA_HEADS, NA_HEAD_DIM).transpose(0, 3, 1, 2, 4)
               for t in jnp.split(u, 3, axis=-1)]
    r = jnp.arange(rows)
    row_idx = jnp.clip(r - kh // 2, 0, rows - kh)[:, None] + jnp.arange(kh)[None, :]
    dr_idx = row_idx - r[:, None] + (NA_KH - 1)
    scale = NA_HEAD_DIM ** -0.5

    def col_block(j0):
        ks0 = jnp.clip(j0 - NA_KW // 2, 0, GRID_W - NA_KSPAN)
        qb = lax.dynamic_slice_in_dim(q, j0, NA_QB, axis=3)
        kb = lax.dynamic_slice_in_dim(k, ks0, NA_KSPAN, axis=3)[:, :, row_idx]
        vb = lax.dynamic_slice_in_dim(v, ks0, NA_KSPAN, axis=3)[:, :, row_idx]
        j = j0 + jnp.arange(NA_QB)
        cs = jnp.clip(j - NA_KW // 2, 0, GRID_W - NA_KW)
        kc = ks0 + jnp.arange(NA_KSPAN)
        valid = (kc[None, :] >= cs[:, None]) & (kc[None, :] < cs[:, None] + NA_KW)
        dc_idx = jnp.clip(kc[None, :] - j[:, None] + (NA_KW - 1), 0, 2 * NA_KW - 2)
        bias = rpb[:, dr_idx[:, None, :, None], dc_idx[None, :, None, :]]
        s = jnp.einsum('bhrqd,bhrkud->bhrqku', qb, kb).astype(F32) * scale + bias.astype(F32)
        s = jnp.where(valid[:, None, :], s, -jnp.inf)
        p = jax.nn.softmax(s.reshape(s.shape[:4] + (kh * NA_KSPAN,)), axis=-1)
        p = p.reshape(s.shape).astype(u.dtype)
        return jnp.einsum('bhrqku,bhrkud->bhrqd', p, vb)

    o = lax.map(col_block, jnp.arange(0, GRID_W, NA_QB))
    return o.transpose(1, 3, 0, 4, 2, 5).reshape(b, L, GROUP_W)

def mlstm_scan(q, k, v, log_i, log_f):
    b, H, L, d = q.shape
    T = ML_CHUNK
    nc = L // T
    to_chunks = lambda t: jnp.moveaxis(t.reshape(t.shape[:2] + (nc, T) + t.shape[3:]), 2, 0)
    lower = jnp.tril(jnp.ones((T, T), bool))

    def step(carry, inp):
        C, n, m = carry
        qc, kc, vc, li, lf = inp
        bcum = jnp.cumsum(lf, axis=-1)
        g_inter = bcum + m[..., None]
        g_intra = jnp.where(lower, bcum[..., :, None] - bcum[..., None, :] + li[..., None, :], -jnp.inf)
        m_t = jnp.maximum(g_inter, jnp.max(g_intra, axis=-1))
        w_inter = jnp.exp(g_inter - m_t)
        s = jnp.einsum('bhtd,bhsd->bhts', qc, kc) * jnp.exp(g_intra - m_t[..., None])
        num = w_inter[..., None] * jnp.einsum('bhtd,bhde->bhte', qc, C) + jnp.einsum('bhts,bhse->bhte', s, vc)
        den = w_inter * jnp.einsum('bhtd,bhd->bht', qc, n) + jnp.sum(s, axis=-1)
        h = num / jnp.maximum(jnp.abs(den), jnp.exp(-m_t))[..., None]
        g_state = bcum[..., -1] + m
        g_src = bcum[..., -1:] - bcum + li
        m_new = jnp.maximum(g_state, jnp.max(g_src, axis=-1))
        w_src = jnp.exp(g_src - m_new[..., None])
        carry_decay = jnp.exp(g_state - m_new)
        C_new = carry_decay[..., None, None] * C + jnp.einsum('bhs,bhsd,bhse->bhde', w_src, kc, vc)
        n_new = carry_decay[..., None] * n + jnp.einsum('bhs,bhsd->bhd', w_src, kc)
        return (C_new, n_new, m_new), h

    init = (jnp.zeros((b, H, d, d), F32), jnp.zeros((b, H, d), F32), jnp.zeros((b, H), F32))
    _, h = lax.scan(step, init, (to_chunks(q), to_chunks(k), to_chunks(v), to_chunks(log_i), to_chunks(log_f)))
    return jnp.moveaxis(h, 0, 2).reshape(b, H, L, d)

def mlstm_mixer(u, i_bias, f_bias, norm_g):
    b, L, _ = u.shape
    heads = lambda t: t.astype(F32).reshape(b, L, ML_HEADS, ML_HEAD_DIM).transpose(0, 2, 1, 3)
    q = heads(u[..., :GROUP_W])
    k = heads(u[..., GROUP_W:2 * GROUP_W]) * (ML_HEAD_DIM ** -0.5)
    v = heads(u[..., 2 * GROUP_W:3 * GROUP_W])
    o = u[..., 3 * GROUP_W:4 * GROUP_W].astype(F32)
    gates = u[..., 4 * GROUP_W:].astype(F32).reshape(b, L, 2, 2, ML_HEADS).transpose(2, 3, 0, 4, 1)
    log_i = gates[0] + i_bias.astype(F32)[:, None, :, None]
    log_f = jax.nn.log_sigmoid(gates[1] + f_bias.astype(F32)[:, None, :, None])
    flip = lambda t: jnp.flip(t, axis=2)
    h_fwd = mlstm_scan(q, k, v, log_i[0], log_f[0])
    h_bwd = flip(mlstm_scan(flip(q), flip(k), flip(v), flip(log_i[1]), flip(log_f[1])))
    h = rms_norm(h_fwd + h_bwd, norm_g.reshape(ML_HEADS, 1, ML_HEAD_DIM))
    h = h.transpose(0, 2, 1, 3).reshape(b, L, GROUP_W)
    return (jax.nn.sigmoid(o) * h).astype(u.dtype)

def hyena_filters(L, w1, b1, w2, b2, w3, freq):
    t = jnp.linspace(0.0, 1.0, L, dtype=F32)[:, None]
    bands = (HY_EMB - 1) // 2
    f = jnp.linspace(1e-4, bands - 1, bands, dtype=F32)
    ang = (2.0 * math.pi) * (jnp.arange(L, dtype=F32) / L)[:, None] * f[None, :]
    feats = jnp.concatenate([t, jnp.cos(ang), -jnp.sin(ang)], axis=-1)
    freq = freq.astype(F32)
    h = jnp.sin(freq[0] * (feats @ w1.astype(F32) + b1.astype(F32)))
    h = jnp.sin(freq[1] * (h @ w2.astype(F32) + b2.astype(F32)))
    h = (h @ w3.astype(F32)).reshape(L, HY_ORDER, 2, HY_CH)
    deltas = jnp.abs(jnp.linspace(math.log(HY_DECAY_TARGET) / HY_LONG_DECAY_FRAC,
                                  math.log(HY_DECAY_TARGET) / HY_SHORT_DECAY_FRAC, HY_CH, dtype=F32))
    h = h * jnp.exp(-t * deltas[None, :])[:, None, None, :]
    return h * lax.rsqrt(jnp.sum(h * h, axis=(0, 2), keepdims=True) + NORM_EPS)

def two_sided_fft_conv(z, h_fwd, h_bwd):
    L = z.shape[1]
    k = jnp.concatenate([h_fwd, jnp.zeros_like(h_fwd[:1]), jnp.flip(h_bwd[1:], axis=0)], axis=0)
    zf = jnp.fft.rfft(z, n=2 * L, axis=1)
    kf = jnp.fft.rfft(k, n=2 * L, axis=0)
    return jnp.fft.irfft(zf * kf[None], n=2 * L, axis=1)[:, :L]

def hyena_mixer(u, conv_w, conv_b, w1, b1, w2, b2, w3, freq, skip, norm_g):
    L = u.shape[1]
    uc = depthwise_conv(u, conv_w, conv_b).astype(F32)
    v, x1, x2 = jnp.split(uc, 3, axis=-1)
    h = hyena_filters(L, w1, b1, w2, b2, w3, freq)
    skip = skip.astype(F32)
    z = v
    for o, gate in enumerate((x1, x2)):
        z = gate * (two_sided_fft_conv(z, h[:, o, 0], h[:, o, 1]) + skip[o] * z)
    return rms_norm(z, norm_g).astype(u.dtype)

def second_inputs(seed: int = 0) -> dict:
    key = jax.random.key(seed)
    ks = iter(jax.random.split(key, 40))
    nrm = lambda shape, s: jax.random.normal(next(ks), shape, F32) * s
    gain = lambda shape: 1.0 + nrm(shape, 0.02)
    Lr = DEPTH
    dt0 = jnp.exp(jax.random.uniform(next(ks), (Lr, 2, SSD_HEADS), F32, math.log(1e-3), math.log(1e-1)))
    return {
        "x": nrm((BATCH, SEQ, D_MODEL), 1.0),
        "c": nrm((BATCH, D_MODEL), 1.0),
        "mod_w": nrm((Lr, D_MODEL, 6 * D_MODEL), D_MODEL ** -0.5),
        "mod_b": nrm((Lr, 6 * D_MODEL), 0.02),
        "w_in": nrm((Lr, D_MODEL, P_IN), D_MODEL ** -0.5),
        "ssd_conv_w": nrm((Lr, SSD_CONV, SSD_XBC), SSD_CONV ** -0.5),
        "ssd_conv_b": nrm((Lr, SSD_XBC), 0.02),
        "ssd_dt_bias": dt0 + jnp.log(-jnp.expm1(-dt0)),
        "ssd_a_log": jnp.log(jax.random.uniform(next(ks), (Lr, 2, SSD_HEADS), F32, 1.0, 16.0)),
        "ssd_d": gain((Lr, SSD_HEADS)),
        "ssd_norm_g": gain((Lr, GROUP_W)),
        "na_rpb": nrm((Lr, NA_HEADS, 2 * NA_KH - 1, 2 * NA_KW - 1), 0.02),
        "na_norm_g": gain((Lr, GROUP_W)),
        "ml_i_bias": nrm((Lr, 2, ML_HEADS), 0.1),
        "ml_f_bias": jnp.linspace(3.0, 6.0, ML_HEADS, dtype=F32)[None, None, :] + nrm((Lr, 2, ML_HEADS), 0.1),
        "ml_norm_g": gain((Lr, GROUP_W)),
        "hy_conv_w": nrm((Lr, HY_CONV, HY_IN), HY_CONV ** -0.5),
        "hy_conv_b": nrm((Lr, HY_IN), 0.02),
        "hy_w1": nrm((Lr, HY_EMB, HY_FFN), HY_EMB ** -0.5),
        "hy_b1": nrm((Lr, HY_FFN), 0.1),
        "hy_w2": nrm((Lr, HY_FFN, HY_FFN), HY_FFN ** -0.5),
        "hy_b2": nrm((Lr, HY_FFN), 0.1),
        "hy_w3": nrm((Lr, HY_FFN, HY_ORDER * 2 * HY_CH), HY_FFN ** -0.5),
        "hy_freq": 1.0 + nrm((Lr, 2, HY_FFN), 0.1),
        "hy_skip": nrm((Lr, HY_ORDER, HY_CH), 0.1),
        "hy_norm_g": gain((Lr, GROUP_W)),
        "w_out": nrm((Lr, MIX_W, D_MODEL), MIX_W ** -0.5),
        "ffn_w_gate": nrm((Lr, D_MODEL, FFN_HIDDEN), D_MODEL ** -0.5),
        "ffn_w_up": nrm((Lr, D_MODEL, FFN_HIDDEN), D_MODEL ** -0.5),
        "ffn_w_down": nrm((Lr, FFN_HIDDEN, D_MODEL), FFN_HIDDEN ** -0.5),
        "final_norm_g": gain((D_MODEL,)),
    }

def second_block(x, c, mod_w, mod_b, w_in, ssd_conv_w, ssd_conv_b, ssd_dt_bias, ssd_a_log, ssd_d,
              ssd_norm_g, na_rpb, na_norm_g, ml_i_bias, ml_f_bias, ml_norm_g, hy_conv_w, hy_conv_b,
              hy_w1, hy_b1, hy_w2, hy_b2, hy_w3, hy_freq, hy_skip, hy_norm_g, w_out,
              ffn_w_gate, ffn_w_up, ffn_w_down, final_norm_g):
    cond = jax.nn.silu(c)
    for l in range(DEPTH):
        mod = cond @ mod_w[l] + mod_b[l]
        sh1, sc1, g1, sh2, sc2, g2 = [m[:, None, :] for m in jnp.split(mod, 6, axis=-1)]
        h = rms_norm(x) * (1 + sc1) + sh1
        u = h @ w_in[l]
        y_ssd = ssd_mixer(u[..., :OFF_NA], ssd_conv_w[l], ssd_conv_b[l], ssd_dt_bias[l],
                          ssd_a_log[l], ssd_d[l], ssd_norm_g[l])
        y_na = rms_norm(neighborhood_attention(u[..., OFF_NA:OFF_ML], na_rpb[l]), na_norm_g[l])
        y_ml = mlstm_mixer(u[..., OFF_ML:OFF_HY], ml_i_bias[l], ml_f_bias[l], ml_norm_g[l])
        y_hy = hyena_mixer(u[..., OFF_HY:], hy_conv_w[l], hy_conv_b[l], hy_w1[l], hy_b1[l],
                           hy_w2[l], hy_b2[l], hy_w3[l], hy_freq[l], hy_skip[l], hy_norm_g[l])
        y = jnp.concatenate([y_ssd, y_na, y_ml, y_hy], axis=-1) @ w_out[l]
        x = x + g1 * y
        h = rms_norm(x) * (1 + sc2) + sh2
        x = x + g2 * ((jax.nn.silu(h @ ffn_w_gate[l]) * (h @ ffn_w_up[l])) @ ffn_w_down[l])
    return rms_norm(x, final_norm_g)


_first_inputs_2 = second_inputs


def second_inputs(seed=0):
    import zlib

    import numpy as np

    out = dict(_first_inputs_2(seed))
    spreads = {}
    factors = {'ssd_conv_b': 8.0,
     'ssd_d': 8.0,
     'ssd_norm_g': 8.0,
     'na_rpb': 8.0,
     'na_norm_g': 8.0,
     'ml_i_bias': 8.0,
     'ml_norm_g': 8.0,
     'hy_conv_b': 5.113,
     'hy_skip': 4.828,
     'hy_norm_g': 7.985,
     'final_norm_g': 2.804}
    for name, (base, spread) in spreads.items():
        noise = np.random.default_rng([zlib.crc32(name.encode()), seed]).standard_normal(out[name].shape)
        drawn = base * np.exp(spread * noise) if base else spread * noise
        out[name] = __import__('jax').numpy.asarray(drawn.astype(out[name].dtype))
    for name, factor in factors.items():
        out[name] = (out[name] * factor).astype(out[name].dtype)
    return out


_narrow_inputs_2 = second_inputs


def second_inputs(seed=0):

    out = dict(_narrow_inputs_2(seed))
    wider = {'ssd_d': 12.0,
     'ssd_norm_g': 5.35,
     'na_norm_g': 5.59,
     'ml_i_bias': 4.31,
     'ml_norm_g': 11.58,
     'hy_norm_g': 4.93,
     'final_norm_g': 3.26}
    for name, times in wider.items():
        mean = out[name].mean()
        out[name] = (mean + times * (out[name] - mean)).astype(out[name].dtype)
    return out


def setup_inputs(seed=0):
    out = dict(first_inputs(seed))
    for name, value in second_inputs(seed + 1).items():
        if name != "x":
            out[name + "_2"] = value
    return out


def reference(
    x, c, ctx, c_ctx, w_ada, b_ada, norm_mix_w, norm_ffn_w, w_in, hgrn_lb_logits, hgrn_norm_w,
    q_norm_w, k_norm_w, attn_sinks, w_branch_hgrn, w_branch_attn, w_out, w_ffn_gate, w_ffn_up,
    w_ffn_down, c_2, mod_w_2, mod_b_2, w_in_2, ssd_conv_w_2, ssd_conv_b_2, ssd_dt_bias_2,
    ssd_a_log_2, ssd_d_2, ssd_norm_g_2, na_rpb_2, na_norm_g_2, ml_i_bias_2, ml_f_bias_2,
    ml_norm_g_2, hy_conv_w_2, hy_conv_b_2, hy_w1_2, hy_b1_2, hy_w2_2, hy_b2_2, hy_w3_2,
    hy_freq_2, hy_skip_2, hy_norm_g_2, w_out_2, ffn_w_gate_2, ffn_w_up_2, ffn_w_down_2,
    final_norm_g_2,
):
    x = first_block(
        x, c, ctx, c_ctx, w_ada, b_ada, norm_mix_w, norm_ffn_w, w_in, hgrn_lb_logits,
        hgrn_norm_w, q_norm_w, k_norm_w, attn_sinks, w_branch_hgrn, w_branch_attn, w_out,
        w_ffn_gate, w_ffn_up, w_ffn_down,
    )
    return second_block(
        x, c_2, mod_w_2, mod_b_2, w_in_2, ssd_conv_w_2, ssd_conv_b_2, ssd_dt_bias_2,
        ssd_a_log_2, ssd_d_2, ssd_norm_g_2, na_rpb_2, na_norm_g_2, ml_i_bias_2, ml_f_bias_2,
        ml_norm_g_2, hy_conv_w_2, hy_conv_b_2, hy_w1_2, hy_b1_2, hy_w2_2, hy_b2_2, hy_w3_2,
        hy_freq_2, hy_skip_2, hy_norm_g_2, w_out_2, ffn_w_gate_2, ffn_w_up_2, ffn_w_down_2,
        final_norm_g_2,
    )


_drawn_inputs = setup_inputs


def setup_inputs(seed=0):
    import zlib

    import numpy as np

    out = dict(_drawn_inputs(seed))
    spreads = {}
    factors = {'ctx': 3.575,
     'hgrn_lb_logits': 3.073,
     'q_norm_w': 8.0,
     'k_norm_w': 8.0,
     'attn_sinks': 5.25}
    for name, (base, spread) in spreads.items():
        noise = np.random.default_rng([zlib.crc32(name.encode()), seed]).standard_normal(out[name].shape)
        drawn = base * np.exp(spread * noise) if base else spread * noise
        out[name] = jnp.asarray(drawn.astype(out[name].dtype))
    for name, factor in factors.items():
        out[name] = (out[name] * factor).astype(out[name].dtype)
    return out
```

```python
import math
from contextlib import ExitStack

import numpy as np

import concourse.bass as bass
from concourse import mybir

F32 = mybir.dt.float32
F32R = mybir.dt.float32r
I32 = mybir.dt.int32
ALU = mybir.AluOpType
ACT = mybir.ActivationFunctionType
AX = mybir.AxisListType

P = 128
D = 1024
KT = D // P
T = 1024
TC = 256
TA = TC + T
HALF = 512
EPS = 1e-6
FF = 2816
FT = FF // P
BIG = 1e30

PP = {}
_n = 0
for _name, _w in (
    ("cond", 3 * KT), ("b_ada", 48), ("mod_b", 48), ("norm_mix", KT), ("norm_ffn", KT), ("final_g", KT),
    ("lb", 16), ("hg_norm", 1), ("q_norm", 1), ("k_norm", 1), ("sink", 8),
    ("cw", 18), ("cb", 6), ("dt_bias", 1), ("a_log", 1), ("ssd_d", 4), ("ssd_g", 256), ("na_g", 2),
    ("ib", 1), ("fb", 1), ("ml_g", 256), ("hcw", 18), ("hcb", 6), ("hb1", 1), ("hb2", 1), ("hfreq", 2),
    ("hskip", 512), ("hy_g", 256),
):
    PP[_name] = (_n, _w)
    _n += _w
NPP = _n

SLOT = 24 * P
M_RING = 2560
M_MAIN = M_RING + 2 * SLOT
M_X = M_MAIN
M_H = M_X + KT * T
M_B1 = M_H + KT * TA
M_YAT = M_B1
M_YHG = M_YAT + 4 * T
M_W1 = M_YHG + 4 * T
M_HID = M_H + KT * T
M_Y2 = M_HID
M_W2 = M_Y2 + KT * T
M_END = 53100
M_PARTS = M_END - 4 * KT * T


def repeat(e, n, body):
    with e.Fori(0, n) as i:
        body(i)


class Chain:

    def __init__(self, e, sem):
        self.e, self.sem, self.n = e, sem, 0

    def __call__(self, ins):
        self.n += 1
        ins.then_inc(self.sem, 1)
        self.e.wait_ge(self.sem, self.n)


class Signal:

    def __init__(self, sem, base):
        self.sem, self.base = sem, base

    def wait(self, e, n):
        e.wait_ge(self.sem, self.base + n)


class Words:

    def __init__(self, tensors):
        self.tensors = tensors

    def __getitem__(self, key):
        rows, words = key
        for a, b, v in self.tensors:
            if a <= words.start and words.stop <= b:
                return v[rows, words.start - a:words.stop - a]
        raise IndexError(words)


class Mem:

    def __init__(self, big, at, end):
        self.big, self.at, self.end = big, at, end

    def __call__(self, *shape, parts=P):
        n = int(np.prod(shape))
        v = self.big[0:parts, self.at:self.at + n]
        self.at += n
        assert self.at <= self.end, (self.at, self.end)
        if len(shape) == 2:
            v = v.rearrange("p (a b) -> p a b", a=shape[0])
        if len(shape) == 3:
            v = v.rearrange("p (a b c) -> p a b c", a=shape[0], b=shape[1])
        return v


def bc(ap, shape):
    return ap.unsqueeze(len(ap.shape)).to_broadcast(shape)


class Program:

    def __init__(self, nc, ctx, dram):
        self.nc, self.ctx, self.d = nc, ctx, dram
        tensor = lambda name, a, b: (a, b, nc.sbuf_tensor(name, [P, b - a], F32))
        own = [tensor("parameters", 0, M_RING), tensor("weight_ring", M_RING, M_X), tensor("x", M_X, M_H)]
        own = [(a, b, ctx.enter_context(v)) for a, b, v in own]
        with nc.sbuf_tensor("work", [P, M_END - M_H], F32) as v:
            self.big = Words(own + [(M_H, M_END, v)])
        with nc.sbuf_tensor("before_split", [P, KT * T + 2 * HALF], F32) as v:
            m = Mem(v, 0, KT * T + 2 * HALF)
            self.whole, self.whole_rs = m(KT, T), m(2, HALF)
            self.whole_hid = self.whole[:, 0:2, :]
        ctx.enter_context(nc.sbuf_tensor("work_below_parts", [P, M_PARTS - M_H], F32))

        def parts(name, a, b):
            m = Mem(ctx.enter_context(nc.sbuf_tensor(name, [P, 2 * a * b], F32R)), 0, 2 * a * b)
            return [m(a, b), m(a, b)]
        self.w_parts = parts("weight_parts", 2, 2048)
        self.hid_parts = parts("hidden_parts", 4, T)
        self.h_parts = parts("input_parts", KT, T)
        self.ps = ctx.enter_context(nc.psum_tensor("banks", [P, 8, HALF], F32))
        self._v = self._a = None
        self.shared = {}
        self.group = 0
        self.fill = 0
        self.stages = []
        self.ends = []
        self.w_ready = [self.sem(f"weights_ready_{s}") for s in range(2)]
        self.ps_full = self.sem("bank_full")
        self.ps_free = self.sem("bank_read")
        self.stage_done = self.sem("stage_done")
        self.loaded = self.sem("parameters_loaded")
        self.vch = self.sem("vector_step")
        self.ach = self.sem("scalar_step")
        m = Mem(self.big, 0, M_RING)
        self.pp = m(NPP)
        self.ident = m(P)
        self.ones = m(P)
        self.silu_c = m(KT, 3)
        self.mod1 = m(48, 2)
        self.mod2 = m(48)
        self.sc_mix = m(KT, 2)
        self.sc_ffn = m(KT)
        self.sc2a = m(KT)
        self.sc2b = m(KT)
        self.eps = m(1)
        self.zero_col = m(1)
        self.perm_left = m
        self.slots = [self.big[:, M_RING + s * SLOT:M_RING + (s + 1) * SLOT] for s in range(2)]
        self.x = Mem(self.big, M_X, M_H)(KT, T)
        self.h2 = Mem(self.big, M_H, M_END)(KT, T)
        self.h1 = Mem(self.big, M_H, M_END)(KT, TA)

    def sem(self, name):
        return self.ctx.enter_context(self.nc.semaphore(name))

    def col(self, name, i=0, n=1, parts=P):
        at = PP[name][0] + i
        return self.pp[0:parts, at:at + n]

    def param(self, name, parts=P):
        at, w = PP[name]
        return self.pp[0:parts, at:at + w]

    def stage(self, **parts):
        self.stages.append(parts)


    def shared_sem(self, name, count):
        if name not in self.shared:
            self.shared[name] = [self.sem(name), 0]
        sem, base = self.shared[name]
        self.shared[name][1] += count
        return Signal(sem, base)

    def scratch(self, *shape):
        n = int(np.prod(shape))
        return Mem(self.big, M_END - n, M_END)(*shape)

    def vchain(self, e):
        if self._v is None:
            self._v = Chain(e, self.vch)
        return self._v

    def achain(self, e):
        if self._a is None:
            self._a = Chain(e, self.ach)
        return self._a

    def take_groups(self, ends):
        g = self.group
        self.ends += ends
        self.group += len(ends)
        return g

    def slot_free(self, e, g):
        if g >= 2:
            e.wait_ge(self.ps_full, self.ends[g - 2])

    def weights(self, e, g):
        e.wait_ge(self.w_ready[g % 2], 16 * (g // 2 + 1))
        return self.slots[g % 2]

    def load(self, e, g, src, *dst_shape):
        self.slot_free(e, g)
        dst = self.slots[g % 2][:, 0:src.shape[-1]]
        e.dma_start(dst, src).then_inc(self.w_ready[g % 2], 16)

    def bank_free(self, e, f):
        if f >= 8:
            e.wait_ge(self.ps_free, f - 7)


def linear_fm(pg, name, w, ktiles, act, n_tiles, spans, evac, engine, per_group=2, first=None):
    ng = n_tiles // per_group
    f0 = pg.fill
    fills = per_group * len(spans)
    g0 = pg.take_groups([f0 + (g + 1) * fills for g in range(ng)])
    pg.fill += ng * fills
    un = 2 if ng % 2 == 0 and (2 * fills) % 8 == 0 and ng > 2 else ng
    loops = ng // un
    width = ktiles * per_group * P

    def run(e, body):
        if loops > 1:
            repeat(e, loops, body)
        else:
            body(0)

    def sync(e):
        pg.slot_free(e, g0)

        def body(i):
            for u in range(un):
                g = g0 + u
                if u or f0 >= fills:
                    e.wait_ge(pg.ps_full, f0 + (u - 1) * fills + i * (un * fills))
                src = w[i * un + u] if loops == 1 else w[bass.ds(i * un + u, 1)].rearrange("a p n -> (a p) n")
                e.dma_start(pg.slots[g % 2][:, 0:width], src).then_inc(pg.w_ready[g % 2], 16)
        run(e, body)

    def tensor(e):
        def body(i):
            for u in range(un):
                g = g0 + u
                e.wait_ge(pg.w_ready[g % 2], 16 * (g // 2 + 1) + i * (8 * un))
                slot = pg.slots[g % 2]
                for t in range(per_group):
                    for s, (a, b) in enumerate(spans):
                        f = f0 + (u * per_group + t) * len(spans) + s
                        if f >= 8:
                            e.wait_ge(pg.ps_free, f - 7 + i * (un * fills))
                        for k in range(ktiles):
                            at = (k * per_group + t) * P
                            mm = e.matmul(pg.ps[:, f % 8, 0:b - a], slot[:, at:at + P], act(k, a, b),
                                          start=(k == 0), stop=(k == ktiles - 1))
                        mm.then_inc(pg.ps_full, 1)
        run(e, body)

    def read(e):
        if first:
            first(e)
        if f0:
            e.wait_ge(pg.ps_free, f0)

        def body(i):
            for u in range(un):
                for t in range(per_group):
                    for s, (a, b) in enumerate(spans):
                        f = f0 + (u * per_group + t) * len(spans) + s
                        e.wait_ge(pg.ps_full, f + 1 + i * (un * fills))
                        tile = (i * un + u) * per_group + t
                        evac(e, tile, s, pg.ps[:, f % 8, 0:b - a], (a, b)).then_inc(pg.ps_free, 1)
        run(e, body)

    pg.stage(name=name, sync=sync, tensor=tensor, **{engine: read})


def linear_tm(pg, name, w, act, tiles, cols, evac, engine):
    ng = w.shape[0]
    f0 = pg.fill
    g0 = pg.take_groups([f0 + (g + 1) * len(tiles) for g in range(ng)])
    pg.fill += ng * len(tiles)

    def sync(e):
        for g in range(ng):
            pg.load(e, g0 + g, w[g])

    def tensor(e):
        for g in range(ng):
            slot = pg.weights(e, g0 + g)
            for t, tile in enumerate(tiles):
                f = f0 + g * len(tiles) + t
                pg.bank_free(e, f)
                for k in range(KT):
                    mm = e.matmul(pg.ps[:, f % 8, 0:cols], act(k, tile), slot[:, k * cols:(k + 1) * cols],
                                  start=(k == 0), stop=(k == KT - 1))
                mm.then_inc(pg.ps_full, 1)

    def read(e):
        if f0:
            e.wait_ge(pg.ps_free, f0)
        for g in range(ng):
            for t, tile in enumerate(tiles):
                f = f0 + g * len(tiles) + t
                e.wait_ge(pg.ps_full, f + 1)
                evac(e, g, tile, pg.ps[:, f % 8, 0:cols]).then_inc(pg.ps_free, 1)

    pg.stage(name=name, sync=sync, tensor=tensor, **{engine: read})


def modulation(pg, name, w, rhs, width, out, bias):
    ng = 24
    f0 = pg.fill
    g0 = pg.take_groups([f0 + g + 1 for g in range(ng)])
    pg.fill += ng

    def sync(e):
        for g in range(ng):
            pg.load(e, g0 + g, w[g])

    def tensor(e):
        if f0 == 0:
            e.wait_ge(pg.cond_ready, 1)
        for g in range(ng):
            slot = pg.weights(e, g0 + g)
            f = f0 + g
            pg.bank_free(e, f)
            for t in range(2):
                for k in range(KT):
                    at = (k * 2 + t) * P
                    mm = e.matmul(pg.ps[:, f % 8, t * width:(t + 1) * width], slot[:, at:at + P], rhs(k),
                                  start=(k == 0), stop=(k == KT - 1))
            mm.then_inc(pg.ps_full, 1)

    def vector(e):
        if f0:
            e.wait_ge(pg.ps_free, f0)
        for g in range(ng):
            f = f0 + g
            e.wait_ge(pg.ps_full, f + 1)
            e.tensor_tensor(out[:, 2 * g:2 * g + 2] if width == 1 else out[:, 2 * g:2 * g + 2, :],
                            pg.ps[:, f % 8, 0:2 * width] if width == 1 else
                            pg.ps[:, f % 8, 0:2 * width].rearrange("p (a b) -> p a b", b=width),
                            bias[:, 2 * g:2 * g + 2] if width == 1 else
                            bc(bias[:, 2 * g:2 * g + 2], [P, 2, width]), ALU.add).then_inc(pg.ps_free, 1)

    pg.stage(name=name, sync=sync, tensor=tensor, vector=vector)


def norm(pg, name, src, dst, spans, scale, shift, aux=None, parts=None):
    n = len(spans)
    sq, ms = pg.shared_sem("norm_squares", KT * n), pg.shared_sem("norm_sums", n)
    rt, md = pg.shared_sem("norm_roots", n), pg.shared_sem("norm_scaled", KT * n)
    rs = pg.scratch(n, HALF)
    if parts is not None:
        rs = pg.whole_rs
        high, low = parts
        high_rd = pg.shared_sem("norm_high", KT * n)

    def scalar(e):
        ch = pg.achain(e)
        if aux is not None:
            aux(e)
        for s, w in enumerate(spans):
            for k in range(KT):
                e.activation(dst(s)[:, k, :], src(s)[:, k, :], ACT.Square).then_inc(sq.sem, 1)
        for s, w in enumerate(spans):
            ms.wait(e, s + 1)
            e.activation(rs[:, s, 0:w], pg.ps[:, s, 0:w], ACT.Sqrt, bias=pg.eps[:, 0:1], scale=1.0 / D).then_inc(rt.sem, 1)
        if shift is not None:
            for s, w in enumerate(spans):
                for k in range(KT):
                    md.wait(e, KT * s + k + 1)
                    if parts is None:
                        e.activation(dst(s)[:, k, :], dst(s)[:, k, :], ACT.Identity, bias=shift(s, k))
                    else:
                        e.activation(high[:, k, s * HALF:(s + 1) * HALF], dst(s)[:, k, :], ACT.Identity,
                                     bias=shift(s, k)).then_inc(high_rd.sem, 1)

    def tensor(e):
        for s, w in enumerate(spans):
            for k in range(KT):
                sq.wait(e, KT * s + k + 1)
                mm = e.matmul(pg.ps[:, s, 0:w], pg.ones[:, :], dst(s)[:, k, :], start=(k == 0), stop=(k == KT - 1))
            mm.then_inc(ms.sem, 1)

    def vector(e):
        ch = pg.vchain(e)
        if aux is not None:
            aux(e)
        for s, w in enumerate(spans):
            rt.wait(e, s + 1)
            ch(e.reciprocal(rs[:, s, 0:w], rs[:, s, 0:w]))
            for k in range(KT):
                e.scalar_tensor_tensor(out=dst(s)[:, k, :], in0=src(s)[:, k, :], scalar=scale(s, k), in1=rs[:, s, 0:w],
                                       op0=ALU.mult, op1=ALU.mult).then_inc(md.sem, 1)
        if parts is not None:
            for s, w in enumerate(spans):
                for k in range(KT):
                    high_rd.wait(e, KT * s + k + 1)
                    half = slice(s * HALF, (s + 1) * HALF)
                    e.scalar_tensor_tensor(out=low[:, k, half], in0=dst(s)[:, k, :], scalar=shift(s, k),
                                           in1=high[:, k, half].bitcast(F32), op0=ALU.add, op1=ALU.subtract)

    pg.stage(name=name, scalar=scalar, tensor=tensor, vector=vector)


def setup(pg):
    pg.cond_ready = pg.sem("cond_ready")
    const = pg.sem("constants_set")
    pg.x_loaded = pg.sem("x_loaded")
    pg.ctx_raw = Mem(pg.big, M_W1, M_END)(KT, TC)

    def pool(e):
        e.dma_start(pg.pp, pg.d["params"]).then_inc(pg.loaded, 16)
        e.dma_start(pg.ident, pg.d["ident"]).then_inc(pg.loaded, 16)
        e.dma_start(pg.ctx_raw, pg.d["ctx_t"]).then_inc(pg.x_loaded, 16)
        e.dma_start(pg.x, pg.d["x_t"]).then_inc(pg.x_loaded, 16)

    def vector(e):
        ch = pg.vchain(e)
        e.memset(pg.ones, 1.0)
        e.memset(pg.zero_col, 0.0)
        ch(e.memset(pg.eps, EPS))
        e.wait_ge(pg.loaded, 32)

    def scalar(e):
        e.wait_ge(pg.loaded, 32)
        e.activation(pg.silu_c, pg.param("cond").rearrange("p (k c) -> p k c", c=3), ACT.Silu).then_inc(pg.cond_ready, 1)

    def tensor(e):
        e.wait_ge(pg.loaded, 32)

    pg.stage(name="setup", gpsimd=pool, vector=vector, scalar=scalar, tensor=tensor)
    modulation(pg, "modulation_1", pg.d["w_ada"], lambda k: pg.silu_c[:, k, 0:2], 2, pg.mod1, pg.param("b_ada"))
    pg.lb = pg.perm_left(8)
    pg.one_minus_lb = pg.perm_left(8)
    e0, mx = pg.perm_left(8), pg.perm_left(8)
    ea = pg.perm_left(8)
    lb_exp = pg.sem("bound_exps")

    terms = pg.sem("bound_terms")

    def scalar2(e):
        e.wait_ge(terms, 1)
        e.activation(e0, e0, ACT.Exp).then_inc(lb_exp, 1)
        e.activation(ea, ea, ACT.Exp).then_inc(lb_exp, 1)

    def vector2(e):
        ch = pg.vchain(e)
        for j in range(2):
            e.scalar_tensor_tensor(out=pg.sc_mix[:, :, j], in0=pg.mod1[:, 8:16, j], scalar=1.0,
                                   in1=pg.param("norm_mix"), op0=ALU.add, op1=ALU.mult)
        e.scalar_tensor_tensor(out=pg.sc_ffn, in0=pg.mod1[:, 32:40, 0], scalar=1.0,
                               in1=pg.param("norm_ffn"), op0=ALU.add, op1=ALU.mult)
        lb = pg.param("lb")
        for d in range(2):
            l0, l1 = lb[:, 8 * d:8 * d + 4], lb[:, 8 * d + 4:8 * d + 8]
            o = slice(4 * d, 4 * d + 4)
            ch(e.tensor_tensor(mx[:, o], l0, l1, ALU.max))
            ch(e.tensor_tensor(e0[:, o], l0, mx[:, o], ALU.subtract))
            ins = e.tensor_tensor(ea[:, o], l1, mx[:, o], ALU.subtract)
            if d == 0:
                ch(ins)
            else:
                ins.then_inc(terms, 1)
        e.wait_ge(lb_exp, 2)
        ch(e.tensor_tensor(mx, e0, ea, ALU.add))
        ch(e.reciprocal(mx, mx))
        ch(e.tensor_tensor(pg.lb, e0, mx, ALU.mult))
        ch(e.tensor_tensor(pg.one_minus_lb, ea, mx, ALU.mult))

    pg.stage(name="bounds", vector=vector2, scalar=scalar2)

    def wait_x(e):
        e.wait_ge(pg.x_loaded, 32)

    h1, x = pg.h1, pg.x
    norm(pg, "norm_mix",
         lambda s: pg.ctx_raw if s == 0 else x[:, :, (s - 1) * HALF:s * HALF],
         lambda s: h1[:, :, 0:TC] if s == 0 else h1[:, :, TC + (s - 1) * HALF:TC + s * HALF],
         [TC, HALF, HALF],
         lambda s, k: pg.sc_mix[:, k, (1 if s == 0 else 0):(2 if s == 0 else 1)],
         lambda s, k: pg.mod1[:, k, (1 if s == 0 else 0):(2 if s == 0 else 1)], aux=wait_x)


LAT = [(TC, TC + HALF), (TC + HALF, TA)]
ALL = [(0, TC)] + LAT


def window_attention(pg):
    m = Mem(pg.big, M_W1, M_END)
    kk, vv, q = m(TA), m(TA // P, P), m(4, T)
    cs, sn = m(T), m(T)
    mask = m(3, 640)
    rot, blk = m(P), m(P)
    stat = m(8, 64)
    mx_ = Mem(pg.big, M_X, M_H)
    S = mx_(4, 640)
    PT = mx_(2, 5, HALF)
    tmp = Mem(pg.big, M_YHG, M_W1)
    sq, rr, t1 = tmp(TA), tmp(TA), tmp(T)
    yat = Mem(pg.big, M_YAT, M_YHG)(4, T)
    pg.yat = yat
    h1 = pg.h1
    consts = pg.sem("attention_tables_loaded")
    k_at = len(pg.stages)

    def q_out(e, tile, s, bank, ab):
        return e.activation(q[:, tile, s * HALF:(s + 1) * HALF], bank, ACT.Copy)
    linear_fm(pg, "attention_q", pg.d["w_q"], KT, lambda k, a, b: h1[:, k, a:b], 4, LAT, q_out, "scalar")

    def k_out(e, tile, s, bank, ab):
        return e.activation(kk[:, ab[0]:ab[1]], bank, ACT.Copy)
    linear_fm(pg, "attention_k", pg.d["w_k"], KT, lambda k, a, b: h1[:, k, a:b], 1, ALL, k_out, "scalar", per_group=1)

    def v_out(e, g, tile, bank):
        return e.tensor_copy(vv[:, tile, :], bank)
    linear_tm(pg, "attention_v", pg.d["w_v"], lambda k, t: h1[:, k, t * P:(t + 1) * P], list(range(TA // P)), P,
              v_out, "vector")

    squares, sums, roots, scaled, turned = (pg.sem(f"qk_{n}") for n in ("squares", "sums", "roots", "scaled", "turned"))
    tiles = [(q[:, j, :], LAT, "q_norm") for j in range(4)] + [(kk, ALL, "k_norm")]

    def spans_of(t):
        return [(a - TC, b - TC) for a, b in LAT] if t < 4 else ALL

    def lat_of(t):
        return tiles[t][0] if t < 4 else kk[:, TC:TA]

    def pool(e):
        e.wait_ge(pg.stage_done, 3 * k_at)
        e.dma_start(cs, pg.d["rope_cos"]).then_inc(consts, 16)
        e.dma_start(sn, pg.d["rope_sin"]).then_inc(consts, 16)
        e.dma_start(mask, pg.d["window_masks"]).then_inc(consts, 16)
        e.dma_start(rot, pg.d["rope_turn"]).then_inc(consts, 16)
        e.dma_start(blk, pg.d["ones_64"]).then_inc(consts, 16)

    def p_scalar(e):
        for t, (v, _, _) in enumerate(tiles):
            n = T if t < 4 else TA
            if t:
                e.wait_ge(sums, t)
            e.activation(sq[:, 0:n], v, ACT.Square).then_inc(squares, 1)
            e.wait_ge(sums, t + 1)
            if t:
                e.wait_ge(scaled, t)
            for s, (a, b) in enumerate(spans_of(t)):
                last = e.activation(rr[:, a:b], pg.ps[:, s, 0:b - a], ACT.Sqrt, bias=pg.eps[:, 0:1], scale=1.0 / 64)
            last.then_inc(roots, 1)

    def p_tensor(e):
        e.wait_ge(consts, 80)
        for t in range(5):
            e.wait_ge(squares, t + 1)
            if t:
                e.wait_ge(roots, t)
            for s, (a, b) in enumerate(spans_of(t)):
                mm = e.matmul(pg.ps[:, s, 0:b - a], blk, sq[:, a:b], start=True, stop=True)
            mm.then_inc(sums, 1)
            e.wait_ge(scaled, t + 1)
            for s in range(2):
                mm = e.matmul(pg.ps[:, 4 + s, :], rot, lat_of(t)[:, s * HALF:(s + 1) * HALF], start=True, stop=True)
            mm.then_inc(turned, 1)

    def p_vector(e):
        ch = pg.vchain(e)
        e.wait_ge(consts, 80)
        ch(e.tensor_scalar(stat[:, 0, 0:1], pg.col("q_norm"), 0.125, None, ALU.mult))
        for t, (v, _, w) in enumerate(tiles):
            n = T if t < 4 else TA
            e.wait_ge(roots, t + 1)
            ch(e.reciprocal(rr[:, 0:n], rr[:, 0:n]))
            e.scalar_tensor_tensor(out=v, in0=v, scalar=stat[:, 0, 0:1] if t < 4 else pg.col("k_norm"),
                                   in1=rr[:, 0:n], op0=ALU.mult, op1=ALU.mult).then_inc(scaled, 1)
            e.wait_ge(turned, t + 1)
            ch(e.tensor_tensor(t1, pg.ps[:, 4:6, :].rearrange("p a b -> p (a b)"), sn, ALU.mult))
            ch(e.tensor_tensor(lat_of(t), lat_of(t), cs, ALU.mult))
            ch(e.tensor_tensor(lat_of(t), lat_of(t), t1, ALU.add))

    pg.stage(name="attention_rotate", gpsimd=pool, scalar=p_scalar, tensor=p_tensor, vector=p_vector)

    NB = T // P
    N = NB * 8
    sc, sm, ex, pr, tr, pt, pv, yo = (pg.sem(f"attention_{n}") for n in (
        "scores", "maxima", "exps", "probs", "turns", "turned", "outputs", "stored"))
    mx, nm, rs, es, dn, ri = (stat[:, i, :] for i in range(1, 7))

    def where(i):
        n, r = divmod(i, 8)
        g, j = divmod(r, 4)
        return n, g, j

    def blocks(n):
        return [max(n - 1, 0), n, min(n + 1, NB - 1)]

    def tensor(e):
        def scores(i):
            n, g, j = where(i)
            rows = slice(64 * g, 64 * g + 64)
            if i >= 2:
                e.wait_ge(sm, i - 1)
            c0 = 2 * (i % 2)
            qq = q[rows, j, n * P:(n + 1) * P]
            e.matmul(pg.ps[:, c0, 0:TC], qq, kk[rows, 0:TC], start=True, stop=True)
            for b, kb in enumerate(blocks(n)):
                at = TC + b * P
                mm = e.matmul(pg.ps[:, c0 + at // HALF, at % HALF:at % HALF + P], qq,
                              kk[rows, TC + kb * P:TC + (kb + 1) * P], start=True, stop=True)
            mm.then_inc(sc, 1)

        def turn(i):
            e.wait_ge(pr, i + 1)
            if i:
                e.wait_ge(pt, i)
            for b in range(5):
                mm = e.transpose(pg.ps[:, 4 + b // 4, (b % 4) * P:(b % 4 + 1) * P], S[:, i % 4, b * P:(b + 1) * P],
                                 pg.ident)
            mm.then_inc(tr, 1)

        def values(u):
            n, g, _ = where(4 * u)
            e.wait_ge(pt, 4 * u + 4)
            if u >= 2:
                e.wait_ge(yo, u - 1)
            for b, kt in enumerate([0, 1] + [2 + kb for kb in blocks(n)]):
                mm = e.matmul(pg.ps[64 * g:64 * g + 64, 6 + u % 2, :], vv[:, kt, 64 * g:64 * g + 64], PT[:, u % 2, b, :],
                              start=(b == 0), stop=(b == 4))
            mm.then_inc(pv, 1)

        for i in range(N + 3):
            if i < N:
                scores(i)
            if 2 <= i < N + 2:
                turn(i - 2)
            if i >= 3 and (i - 3) % 4 == 3:
                values((i - 3) // 4)

    def vector(e):
        ch = pg.vchain(e)
        for i in range(N + 1):
            if i < N:
                n, g, j = where(i)
                h = 4 * g + j
                e.wait_ge(sc, i + 1)
                if i >= 4:
                    e.wait_ge(tr, i - 3)
                kind = 1 if n == 0 else 2 if n == NB - 1 else 0
                ch(e.tensor_tensor_reduce(S[:, i % 4, :], pg.ps[:, 2 * (i % 2):2 * (i % 2) + 2, :]
                                          .rearrange("p a b -> p (a b)")[:, 0:640], mask[:, kind, :], 1.0, -BIG,
                                          ALU.add, ALU.max, mx[:, i:i + 1]))
                e.tensor_scalar(nm[:, i:i + 1], mx[:, i:i + 1], pg.col("sink", h), -1.0, ALU.max,
                                ALU.mult).then_inc(sm, 1)
            if i >= 1:
                r = i - 1
                e.wait_ge(ex, r + 1)
                ch(e.tensor_tensor(dn[:, r:r + 1], rs[:, r:r + 1], es[:, r:r + 1], ALU.add))
                ch(e.reciprocal(ri[:, r:r + 1], dn[:, r:r + 1]))
                e.tensor_scalar(S[:, r % 4, :], S[:, r % 4, :], ri[:, r:r + 1], None, ALU.mult).then_inc(pr, 1)

    def scalar(e):
        for i in range(N + 4):
            if i < N:
                n, g, j = where(i)
                h = 4 * g + j
                e.wait_ge(sm, i + 1)
                e.activation(S[:, i % 4, :], S[:, i % 4, :], ACT.Exp, bias=nm[:, i:i + 1], accum_out=rs[:, i:i + 1])
                e.activation(es[:, i:i + 1], pg.col("sink", h), ACT.Exp, bias=nm[:, i:i + 1]).then_inc(ex, 1)
            if 2 <= i < N + 2:
                r = i - 2
                u, j = divmod(r, 4)
                e.wait_ge(tr, r + 1)
                if u >= 2 and j == 0:
                    e.wait_ge(pv, u - 1)
                e.activation(PT[:, u % 2, :, j * P:(j + 1) * P], pg.ps[:, 4:6, :].rearrange("p a (b c) -> p (a b) c", c=P)
                             [:, 0:5, :], ACT.Copy).then_inc(pt, 1)
            if i >= 4 and (i - 4) % 4 == 3:
                u = (i - 4) // 4
                n, g, _ = where(4 * u)
                e.wait_ge(pv, u + 1)
                e.activation(yat[64 * g:64 * g + 64, :, n * P:(n + 1) * P],
                             pg.ps[64 * g:64 * g + 64, 6 + u % 2, :].rearrange("p (a b) -> p a b", b=P),
                             ACT.Copy).then_inc(yo, 1)

    pg.stage(name="attention", tensor=tensor, vector=vector, scalar=scalar)


def hgrn(pg):
    C = 32
    NC = TA // C
    NT = TA // P
    HEADS = 4
    m = Mem(pg.big, M_W1, M_END)
    V = m(NT, 4 * P)
    B, Cn = m(2, TA), m(2, TA)
    Q, G = m(2, T), m(2, T)
    tri = m(2, P).bitcast(I32)
    reset = m(TA)
    sq = m(T)
    dec = m(2, NC)
    m = Mem(pg.big, M_X, M_H)
    A = m(4, TA)
    S = m(16, P)
    KT_ = m(4, P)
    SM = m(4, P)
    yhg = Mem(pg.big, M_YHG, M_W1)(HEADS, T)
    pg.yhg = yhg
    h1 = pg.h1
    k_at = len(pg.stages)
    tables = pg.sem("hgrn_tables_loaded")

    def v_out(e, g, tile, bank):
        return e.activation(V[:, tile, 256 * g:256 * g + 256], bank, ACT.Copy)
    linear_tm(pg, "hgrn_values", pg.d["w_inp"], lambda k, t: h1[:, k, t * P:(t + 1) * P], list(range(NT)), 256,
              v_out, "scalar")

    f0 = pg.fill
    FH = 10
    g0 = pg.take_groups([f0 + FH * h + n for h in range(HEADS) for n in (6, 10)])
    pg.fill += FH * HEADS
    (f_rd, l_rd, c_rd, n_rd, e_rd, q_rd, t_rd, k_cp, u_rd, s_rd, sc_rd, sm_rd, o_rd, o_cp, r_sq, r_sm, r_rt,
     done) = (pg.sem(f"hgrn_{n}") for n in (
         "gates", "logs", "cums", "inverse_exps", "exps", "operands", "turned", "keys", "updates", "states",
         "scores", "masked", "outputs", "summed", "squares", "square_sums", "roots", "head_done"))
    spans = [[(0, a, b) for a, b in ALL] + [(1, a, b) for a, b in ALL], [(0, a, b) for a, b in LAT] + [(1, a, b) for a, b in LAT]]

    def tile_of(k, d):
        return k if d == 0 else ([1, 0] + list(range(NT - 1, 1, -1)))[k]

    def pool(e):
        e.wait_ge(pg.stage_done, 3 * k_at)
        e.dma_start(tri, pg.d["tri_32"]).then_inc(tables, 16)
        e.dma_start(reset, pg.d["reset_32"]).then_inc(tables, 16)

    def sync(e):
        for g in range(2 * HEADS):
            pg.load(e, g0 + g, pg.d["w_hgrn"][g])

    def tensor(e):
        def project(h):
            if h >= 2:
                e.wait_ge(done, h - 1)
            for part in range(2):
                slot = pg.weights(e, g0 + 2 * h + part)
                for n, (t, a, b) in enumerate(spans[part]):
                    f = f0 + FH * h + 6 * part + n
                    pg.bank_free(e, f)
                    for k in range(KT):
                        mm = e.matmul(pg.ps[:, f % 8, 0:b - a], slot[:, (2 * k + t) * P:(2 * k + t + 1) * P],
                                      h1[:, k, a:b], start=(k == 0), stop=(k == KT - 1))
                    mm.then_inc(pg.ps_full, 1)

        def chunks(h):
            e.wait_ge(pg.ps_free, f0 + FH * min(h + 2, HEADS))
            e.wait_ge(q_rd, 2 * h + 2)
            for s in range(2 * NT + 2):
                if s < 2 * NT:
                    k, d = divmod(s, 2)
                    t = tile_of(k, d)
                    if h or s:
                        e.wait_ge(k_cp, 20 * h + s)
                    e.transpose(pg.ps[:, 4, 0:P], A[:, 2 * (h % 2) + d, t * P:(t + 1) * P], pg.ident).then_inc(t_rd, 1)
                if 1 <= s <= 2 * NT:
                    u = s - 1
                    k, d = divmod(u, 2)
                    t = tile_of(k, d)
                    E = 20 * h + u
                    e.wait_ge(k_cp, E + 1)
                    if E:
                        e.wait_ge(s_rd, E)
                    for c in range(4):
                        r = slice(C * c, C * c + C)
                        mm = e.matmul(pg.ps[:, c, 0:P], KT_[r, E % 4, :], V[r, t, h * P:(h + 1) * P], start=True, stop=True)
                    mm.then_inc(u_rd, 1)
                    if k >= 2:
                        L = 16 * h + u - 4
                        if L:
                            e.wait_ge(sm_rd, L)
                        e.matmul(pg.ps[:, 5, 0:P], Cn[:, d, t * P:(t + 1) * P], B[:, d, t * P:(t + 1) * P],
                                 start=True, stop=True).then_inc(sc_rd, 1)
                if s >= 2:
                    u = s - 2
                    k, d = divmod(u, 2)
                    t = tile_of(k, d)
                    if k >= 2:
                        L = 16 * h + u - 4
                        e.wait_ge(sm_rd, L + 1)
                        e.wait_ge(s_rd, 20 * h + u + 1)
                        if L >= 2:
                            e.wait_ge(o_cp, L - 1)
                        bank = pg.ps[:, 6 + L % 2, 0:P]
                        e.matmul(bank, V[:, t, h * P:(h + 1) * P], SM[:, L % 4, :], start=True, stop=False)
                        for n in range(4):
                            c = n if d == 0 else 3 - n
                            mm = e.matmul(bank[:, C * c:C * c + C], S[:, 8 * d + (4 * k + n) % 8, :],
                                          B[:, d, t * P + C * c:t * P + C * c + C], start=False, stop=(n == 3))
                        mm.then_inc(o_rd, 1)
            e.wait_ge(r_sq, h + 1)
            for s in range(2):
                mm = e.matmul(pg.ps[:, s, :], pg.ones, sq[:, s * HALF:(s + 1) * HALF], start=True, stop=True)
            mm.then_inc(r_sm, 1)

        project(0)
        for h in range(HEADS):
            if h + 1 < HEADS:
                project(h + 1)
            chunks(h)

    def scalar(e):
        if f0:
            e.wait_ge(pg.ps_free, f0)

        def store(h):
            if h >= 2:
                e.wait_ge(done, h - 1)
            for part in range(2):
                for n, (t, a, b) in enumerate(spans[part]):
                    f = f0 + FH * h + 6 * part + n
                    e.wait_ge(pg.ps_full, f + 1)
                    bank = pg.ps[:, f % 8, 0:b - a]
                    if part == 0:
                        ins = e.activation(A[:, 2 * (h % 2) + t, a:b], bank, ACT.Sigmoid)
                    else:
                        ins = e.activation((Q, G)[t][:, h % 2, a - TC:b - TC], bank, ACT.Silu)
                    ins.then_inc(pg.ps_free, 1)

        store(0)
        for h in range(HEADS):
            for d in range(2):
                e.wait_ge(f_rd, 2 * h + d + 1)
                e.activation(B[:, d, :], A[:, 2 * (h % 2) + d, :], ACT.Ln).then_inc(l_rd, 1)
            for d in range(2):
                e.wait_ge(c_rd, 2 * h + d + 1)
                e.activation(Cn[:, d, :], B[:, d, :], ACT.Exp, scale=-1.0).then_inc(n_rd, 1)
                e.activation(B[:, d, :], B[:, d, :], ACT.Exp).then_inc(e_rd, 1)
            if h + 1 < HEADS:
                store(h + 1)
            for s in range(2 * NT):
                E = 20 * h + s
                e.wait_ge(t_rd, E + 1)
                if E >= 4:
                    e.wait_ge(u_rd, E - 3)
                e.activation(KT_[:, E % 4, :], pg.ps[:, 4, 0:P], ACT.Copy).then_inc(k_cp, 1)
            e.wait_ge(o_cp, 16 * (h + 1))
            e.activation(sq, yhg[:, h, :], ACT.Square).then_inc(r_sq, 1)
            e.wait_ge(r_sm, h + 1)
            e.activation(sq, pg.ps[:, 0:2, :].rearrange("p a b -> p (a b)"), ACT.Sqrt, bias=pg.eps[:, 0:1],
                         scale=1.0 / P).then_inc(r_rt, 1)

    def vector(e):
        ch = pg.vchain(e)
        e.wait_ge(tables, 32)
        ch(e.memset(SM, 0.0))
        for h in range(HEADS):
            a = [A[:, 2 * (h % 2) + d, :] for d in range(2)]
            e.wait_ge(pg.ps_free, f0 + FH * h + 6)
            for d in range(2):
                i = 4 * d + h
                e.tensor_scalar(a[d], a[d], pg.one_minus_lb[:, i:i + 1], pg.lb[:, i:i + 1], ALU.mult,
                                ALU.add).then_inc(f_rd, 1)
            for d in range(2):
                e.wait_ge(l_rd, 2 * h + d + 1)
                e.wait_ge(f_rd, 2 * h + d + 1)
                b = B[:, d, :] if d == 0 else B[:, d, ::-1]
                e.tensor_tensor_scan(b, reset, b, 0.0, ALU.mult, ALU.add).then_inc(c_rd, 1)
                ch(e.tensor_scalar(a[d], a[d], -1.0, 1.0, ALU.mult, ALU.add))
            for d in range(2):
                e.wait_ge(n_rd, 2 * h + d + 1)
                ch(e.tensor_tensor(Cn[:, d, :], a[d], Cn[:, d, :], ALU.mult))
                e.wait_ge(e_rd, 2 * h + d + 1)
                end = C - 1 if d == 0 else 0
                ch(e.tensor_copy(dec[:, d, :], B[:, d, :].rearrange("p (n c) -> p n c", c=C)[:, :, end]))
                e.tensor_tensor(a[d].rearrange("p (n c) -> p n c", c=C), Cn[:, d, :].rearrange("p (n c) -> p n c", c=C),
                                bc(dec[:, d, :], [P, NC, C]), ALU.mult)
                e.wait_ge(pg.ps_free, f0 + FH * (h + 1))
                e.scalar_tensor_tensor(out=B[:, d, TC:TA], in0=Q[:, h % 2, :], scalar=float(P) ** -0.5,
                                       in1=B[:, d, TC:TA], op0=ALU.mult, op1=ALU.mult).then_inc(q_rd, 1)
            for d in range(2):
                ch(e.memset(S[:, 8 * d, :], 0.0))
            for s in range(2 * NT + 1):
                if s < 2 * NT:
                    k, d = divmod(s, 2)
                    E = 20 * h + s
                    t = tile_of(k, d)
                    e.wait_ge(u_rd, E + 1)
                    if k >= 4:
                        e.wait_ge(o_rd, 16 * h + 2 * (k - 2) + d - 4 + 1)
                    if E:
                        e.wait_ge(s_rd, E)
                    for n in range(4):
                        c = n if d == 0 else 3 - n
                        q = 4 * k + n
                        ins = e.scalar_tensor_tensor(
                            out=S[:, 8 * d + (q + 1) % 8, :], in0=S[:, 8 * d + q % 8, :],
                            scalar=dec[:, d, 4 * t + c:4 * t + c + 1], in1=pg.ps[:, c, 0:P], op0=ALU.mult, op1=ALU.add)
                        if n < 3:
                            ch(ins)
                        else:
                            ins.then_inc(s_rd, 1)
                    if k >= 2:
                        L = 16 * h + s - 4
                        e.wait_ge(sc_rd, L + 1)
                        if L >= 4:
                            e.wait_ge(o_rd, L - 3)
                        e.copy_predicated(SM[:, L % 4, :], tri[:, d, :], pg.ps[:, 5, 0:P]).then_inc(sm_rd, 1)
                if s >= 5:
                    k, d = divmod(s - 1, 2)
                    L = 16 * h + s - 5
                    t = tile_of(k, d) - 2
                    e.wait_ge(o_rd, L + 1)
                    o = yhg[:, h, t * P:(t + 1) * P]
                    bank = pg.ps[:, 6 + L % 2, 0:P]
                    if k < 6:
                        e.tensor_copy(o, bank).then_inc(o_cp, 1)
                    else:
                        e.wait_ge(o_cp, L)
                        e.tensor_tensor(o, o, bank, ALU.add).then_inc(o_cp, 1)
            e.wait_ge(r_rt, h + 1)
            ch(e.reciprocal(sq, sq))
            ch(e.scalar_tensor_tensor(out=yhg[:, h, :], in0=yhg[:, h, :], scalar=pg.col("hg_norm"), in1=sq,
                                      op0=ALU.mult, op1=ALU.mult))
            e.tensor_tensor(yhg[:, h, :], yhg[:, h, :], G[:, h % 2, :], ALU.mult).then_inc(done, 1)
            e.wait_ge(done, h + 1)

    pg.stage(name="hgrn", gpsimd=pool, sync=sync, tensor=tensor, scalar=scalar, vector=vector)


def merge(pg):
    m = Mem(pg.big, M_W1, M_END)
    mixed = m(KT, T)
    sg = m(4, HALF)
    h1, yat, yhg, x = pg.h1, pg.yat, pg.yhg, pg.x
    k_at = len(pg.stages)
    again = pg.sem("x_loaded_again")
    gates, half = pg.sem("merge_gates"), pg.sem("merge_mixed")
    f0 = pg.fill
    g0 = pg.take_groups([f0 + 8 * (n + 1) for n in range(KT)])
    pg.fill += 8 * KT
    w = pg.d["w_merge"]

    def pool(e):
        e.wait_ge(pg.stage_done, 3 * k_at)
        e.dma_start(x, pg.d["x_t"]).then_inc(again, 16)

    def sync(e):
        pg.slot_free(e, g0)

        def body(i):
            for u in range(2):
                g = g0 + u
                e.wait_ge(pg.ps_full, f0 + 8 * (u - 1) + 16 * i)
                e.dma_start(pg.slots[g % 2], w[bass.ds(2 * i + u, 1)].rearrange("a p n -> (a p) n")).then_inc(
                    pg.w_ready[g % 2], 16)
        repeat(e, KT // 2, body)

    def tensor(e):
        def body(i):
            for u in range(2):
                g = g0 + u
                e.wait_ge(pg.w_ready[g % 2], 16 * (g // 2 + 1) + i * 16)
                slot = pg.slots[g % 2]
                for s in range(2):
                    a = s * HALF
                    for part, (lo, n, act) in enumerate((
                            (16, KT, lambda k: h1[:, k, TC + a:TC + a + HALF]), (8, KT, lambda k: h1[:, k, TC + a:TC + a + HALF]),
                            (0, 4, lambda k: yhg[:, k, a:a + HALF]), (4, 4, lambda k: yat[:, k, a:a + HALF]))):
                        f = f0 + 8 * u + 4 * s + part
                        e.wait_ge(pg.ps_free, f - 7 + i * 16)
                        for k in range(n):
                            mm = e.matmul(pg.ps[:, f % 8, :], slot[:, (lo + k) * P:(lo + k + 1) * P], act(k),
                                          start=(k == 0), stop=(k == n - 1))
                        mm.then_inc(pg.ps_full, 1)
        repeat(e, KT // 2, body)

    def scalar(e):
        def body(i):
            for u in range(2):
                for s in range(2):
                    for part in range(2):
                        f = f0 + 8 * u + 4 * s + part
                        e.wait_ge(pg.ps_full, f + 1 + i * 16)
                        if part == 0:
                            e.wait_ge(half, 2 * u + s + 1 + i * 4)
                        e.activation(sg[:, 2 * (s % 2) + part, :], pg.ps[:, f % 8, :], ACT.Sigmoid).then_inc(gates, 1)
        repeat(e, KT // 2, body)

    def vector(e):
        e.wait_ge(pg.ps_free, f0)
        e.sem_inc(half, 2)

        def body(i):
            for u in range(2):
                for s in range(2):
                    f = f0 + 8 * u + 4 * s
                    st = 2 * u + s
                    out = mixed[:, bass.ds(2 * i + u, 1), s * HALF:(s + 1) * HALF].rearrange("p a b -> p (a b)")
                    e.wait_ge(gates, 2 * st + 2 + i * 8)
                    e.wait_ge(pg.ps_full, f + 4 + i * 16)
                    e.tensor_tensor(sg[:, 2 * s, :], sg[:, 2 * s, :], pg.ps[:, (f + 3) % 8, :], ALU.mult).then_inc(part_a, 1)
                    e.tensor_tensor(sg[:, 2 * s + 1, :], sg[:, 2 * s + 1, :], pg.ps[:, (f + 2) % 8, :], ALU.mult).then_inc(
                        pg.ps_free, 4)
                    e.wait_ge(part_a, st + 1 + i * 4)
                    e.wait_ge(pg.ps_free, f + 4 + i * 16)
                    e.tensor_tensor(out, sg[:, 2 * s, :], sg[:, 2 * s + 1, :], ALU.add).then_inc(half, 1)
        repeat(e, KT // 2, body)

    part_a = pg.sem("merge_products")
    pg.stage(name="merge", gpsimd=pool, sync=sync, tensor=tensor, scalar=scalar, vector=vector)

    def out(e, tile, s, bank, ab):
        xs = x[:, bass.ds(tile, 1), ab[0]:ab[1]].rearrange("p a b -> p (a b)")
        return e.scalar_tensor_tensor(out=xs, in0=bank, scalar=pg.mod1[:, bass.ds(16 + tile, 1), 0], in1=xs,
                                      op0=ALU.mult, op1=ALU.add)
    linear_fm(pg, "merge_out", pg.d["w_out1"], KT, lambda k, a, b: mixed[:, k, a:b], KT, [(0, HALF), (HALF, T)],
              out, "vector", first=lambda e: e.wait_ge(again, 16))


def ffn(pg, name, w_gu, w_down, gate, mod=None):
    steps = [("G", 0), ("G", 1)]
    for n in range(FT // 2 - 1):
        steps += [("G", 2 * n + 2), ("G", 2 * n + 3), ("D", n)]
    steps += [("D", FT // 2 - 1)]
    NS, LOOPS, UN = len(steps), 5, 6
    assert NS == 3 + LOOPS * UN
    F = pg.whole_hid
    (HH, HL), (FH, FL), (SH, SL) = pg.h_parts, pg.hid_parts, pg.w_parts
    mod_slot = pg.big[:, M_RING:M_MAIN].rearrange("p (a n) -> p a n", a=2)[:, :, 2048:SLOT]
    x = pg.x
    plain = lambda v: v.bitcast(F32)
    k_at = len(pg.stages)
    f0 = pg.fill
    NB = 6
    first_fill, f = [], f0
    for kind, _ in steps:
        first_fill.append(f)
        f += 4 if kind == "G" else 16
    fills, per_turn = f - f0, 2 * (4 + 4 + 16)
    first_fill.append(f)
    g0 = pg.take_groups(first_fill[1:NS - 1] + [f, f])
    pg.fill += fills
    high, split = pg.shared_sem("ffn_weights_high", NS), pg.shared_sem("ffn_weights_split", NS)
    silu = pg.shared_sem("ffn_silu", 2 * FT)
    hid_high, hid_split = pg.shared_sem("ffn_hidden_high", 2 * FT), pg.shared_sem("ffn_hidden_split", 2 * FT)
    if mod:
        m_w, m_out, m_bias = mod
        m_ready, m_sum, m_read = pg.sem("modulation_ready"), pg.sem("modulation_sums"), pg.sem("modulation_read")
    half = lambda s: slice(s * HALF, (s + 1) * HALF)

    def over_steps(e, step):
        step(0, 0)
        step(1, 0)

        def body(i):
            for u in range(UN):
                step(2 + u, i)
        repeat(e, LOOPS, body)
        step(NS - 1, 0)

    def mods(n):
        if not mod:
            return [], []
        if n == NS - 1:
            return [(FT, 0)], [(FT + 1, 0)]
        kind, t = steps[n]
        return [(t, 4 if n >= 2 else 0)] if kind == "G" else [], []

    def sync(e):
        def step(n, i):
            g = g0 + n
            if n < 2:
                pg.slot_free(e, g)
            else:
                split.wait(e, n - 1 + i * UN)
            kind, t = steps[n]
            src = w_gu if kind == "G" else w_down
            src = src[t] if n < 2 or n == NS - 1 else src[bass.ds(t + i * (4 if kind == "G" else 2), 1)].rearrange(
                "a p n -> (a p) n")
            e.dma_start(pg.slots[g % 2][:, 0:2048], src).then_inc(pg.w_ready[g % 2], 16)
        over_steps(e, step)

    def pool(e):
        e.wait_ge(pg.stage_done, 3 * k_at)

        def load(t, i, dynamic):
            if t:
                e.wait_ge(m_sum, t + (i * 4 if dynamic else 0))
            src = m_w[bass.ds(t + i * 4, 1)].rearrange("a p (b n) -> (a p) b n", b=2) if dynamic else (
                m_w[t].rearrange("p (b n) -> p b n", b=2))
            e.dma_start(mod_slot, src).then_inc(m_ready, 16)
        load(0, 0, False)
        load(1, 0, False)
        repeat(e, LOOPS, lambda i: [load(t, i, True) for t in range(2, 6)])
        load(FT, 0, False)
        load(FT + 1, 0, False)

    def tensor(e):
        def modulate(groups, i):
            for t, per in groups:
                e.wait_ge(m_ready, 16 * (t + 1) + i * (per * 16))
                if t >= 2:
                    e.wait_ge(m_read, t - 1 + i * per)
                for half_tile in range(2):
                    for k in range(KT):
                        at = (k * 2 + half_tile) * P
                        mm = e.matmul(pg.ps[:, 6 + t % 2, half_tile:half_tile + 1],
                                      mod_slot[:, at // 1024, at % 1024:at % 1024 + P], pg.silu_c[:, k, 2:3],
                                      start=(k == 0), stop=(k == KT - 1))
                mm.then_inc(m_sum, 1)

        def step(n, i):
            modulate(mods(n)[0], i)
            split.wait(e, n + 1 + i * UN)
            kind, t = steps[n]
            wh, wl = SH[:, n % 2, :], SL[:, n % 2, :]
            if kind == "D":
                hid_split.wait(e, 4 * t + 4 + i * 8)
            for q in range(4 if kind == "G" else 16):
                ff = first_fill[n] + q
                if ff - f0 >= NB:
                    e.wait_ge(pg.ps_free, ff - NB + 1 + i * per_turn)
                bank = pg.ps[:, (ff - f0) % NB, :]
                if kind == "G":
                    s, part = divmod(q, 2)
                    terms = [((2 * k + part) * P, HH[:, k, half(s)], HL[:, k, half(s)]) for k in range(KT)]
                else:
                    tile, s = divmod(q, 2)
                    terms = [((8 * k + tile) * P, FH[:, (2 * t + k) % 4, half(s)], FL[:, (2 * t + k) % 4, half(s)])
                             for k in range(2)]
                for k, (at, hi, lo) in enumerate(terms):
                    w_hi, w_lo = wh[:, at:at + P], wl[:, at:at + P]
                    e.matmul(bank, w_hi, hi, start=(k == 0), stop=False)
                    e.matmul(bank, w_hi, lo, start=False, stop=False)
                    mm = e.matmul(bank, w_lo, hi, start=False, stop=(k == len(terms) - 1))
                mm.then_inc(pg.ps_full, 1)
            modulate(mods(n)[1], i)
        over_steps(e, step)

    def scalar(e):
        def take_high(n, i):
            g = g0 + n
            e.wait_ge(pg.w_ready[g % 2], 16 * (g // 2 + 1) + i * (8 * UN))
            if n >= 2:
                e.wait_ge(pg.ps_full, first_fill[n - 1] + i * per_turn)
            e.activation(SH[:, n % 2, :], pg.slots[g % 2][:, 0:2048], ACT.Copy).then_inc(high.sem, 1)

        def step(n, i):
            if n < NS - 1:
                take_high(n + 1, i)
            kind, t = steps[n]
            if kind == "G":
                for s in range(2):
                    ff = first_fill[n] + 2 * s
                    e.wait_ge(pg.ps_full, ff + 1 + i * per_turn)
                    if t >= 2:
                        hid_split.wait(e, 2 * (t - 2) + s + 1 + i * 8)
                    e.activation(F[:, t % 2, half(s)], pg.ps[:, (ff - f0) % NB, :], ACT.Silu).then_inc(silu.sem, 1)
                    e.wait_ge(pg.ps_free, ff + 2 + i * per_turn)
                    e.activation(FH[:, t % 4, half(s)], F[:, t % 2, half(s)], ACT.Copy).then_inc(hid_high.sem, 1)
        take_high(0, 0)
        over_steps(e, step)

    def vector(e):
        def modulated(groups, i):
            for g, per in groups:
                e.wait_ge(m_sum, g + 1 + i * per)
                cols = slice(2 * g, 2 * g + 2) if not per else bass.ds(2 * g + i * (2 * per), 2)
                e.tensor_tensor(m_out[:, cols], pg.ps[:, 6 + g % 2, 0:2], m_bias[:, cols], ALU.add).then_inc(m_read, 1)

        def take_low(n, i):
            g = g0 + n
            high.wait(e, n + 1 + i * UN)
            e.tensor_tensor(SL[:, n % 2, :], pg.slots[g % 2][:, 0:2048], plain(SH[:, n % 2, :]), ALU.subtract).then_inc(split.sem, 1)

        def step(n, i):
            if n < NS - 1:
                take_low(n + 1, i)
            modulated(mods(n)[0], i)
            kind, t = steps[n]
            if kind == "G":
                for s in range(2):
                    ff = first_fill[n] + 2 * s
                    a = F[:, t % 2, half(s)]
                    silu.wait(e, 2 * t + s + 1 + i * 8)
                    e.wait_ge(pg.ps_full, ff + 2 + i * per_turn)
                    e.tensor_tensor(a, a, pg.ps[:, (ff + 1 - f0) % NB, :], ALU.mult).then_inc(pg.ps_free, 2)
                    hid_high.wait(e, 2 * t + s + 1 + i * 8)
                    e.tensor_tensor(FL[:, t % 4, half(s)], a, plain(FH[:, t % 4, half(s)]), ALU.subtract).then_inc(hid_split.sem, 1)
            else:
                e.wait_ge(pg.ps_free, first_fill[n] + i * per_turn)
                for q in range(16):
                    tile, s = divmod(q, 2)
                    ff = first_fill[n] + q
                    e.wait_ge(pg.ps_full, ff + 1 + i * per_turn)
                    e.scalar_tensor_tensor(out=x[:, tile, half(s)], in0=pg.ps[:, (ff - f0) % NB, :], scalar=gate(tile),
                                           in1=x[:, tile, half(s)], op0=ALU.mult, op1=ALU.add).then_inc(pg.ps_free, 1)
            modulated(mods(n)[1], i)
        take_low(0, 0)
        over_steps(e, step)

    pg.stage(name=name, sync=sync, tensor=tensor, scalar=scalar, vector=vector, **({"gpsimd": pool} if mod else {}))


def block_1(pg):
    setup(pg)
    window_attention(pg)
    hgrn(pg)
    merge(pg)
    norm(pg, "norm_ffn_1", lambda s: pg.x[:, :, s * HALF:(s + 1) * HALF], lambda s: pg.whole[:, :, s * HALF:(s + 1) * HALF],
         [HALF, HALF], lambda s, k: pg.sc_ffn[:, k:k + 1], lambda s, k: pg.mod1[:, 24 + k, 0:1], parts=pg.h_parts)
    ffn(pg, "ffn_1", pg.d["w_gu1"], pg.d["w_down1"], lambda t: pg.mod1[:, 40 + t, 0:1],
        (pg.d["mod_w"], pg.mod2, pg.param("mod_b")))


C2 = 128
NCH = T // C2
TWO_SPANS = [(0, HALF), (HALF, T)]
HY_F = 33
TURN_HI = 6.28125
TURN_LO = 2.0 * math.pi - TURN_HI
ROUND = 1.5 * 2.0 ** 23


def linear_rows(pg, name, w, n_out, evac, engine):
    f0 = pg.fill
    g0 = pg.take_groups([f0 + 2 * n_out])
    pg.fill += 2 * n_out

    def sync(e):
        pg.load(e, g0, w[0])

    def tensor(e):
        slot = pg.weights(e, g0)
        for t in range(n_out):
            for s in range(2):
                f = f0 + 2 * t + s
                pg.bank_free(e, f)
                for k in range(KT):
                    at = (k * n_out + t) * 64
                    mm = e.matmul(pg.ps[0:64, f % 8, :], slot[:, at:at + 64], pg.h2[:, k, s * HALF:(s + 1) * HALF],
                                  start=(k == 0), stop=(k == KT - 1))
                mm.then_inc(pg.ps_full, 1)

    def read(e):
        e.wait_ge(pg.ps_free, f0)
        for t in range(n_out):
            for s in range(2):
                f = f0 + 2 * t + s
                e.wait_ge(pg.ps_full, f + 1)
                evac(e, t, s, pg.ps[0:64, f % 8, :]).then_inc(pg.ps_free, 1)

    pg.stage(name=name, sync=sync, tensor=tensor, **{engine: read})


class Softplus:

    def __init__(self, pg, v, temps):
        self.v, self.t = v, temps
        self.asked, self.exps = pg.shared_sem("softplus_abs", 1), pg.shared_sem("softplus_exp", 1)
        self.ones, self.logs = pg.shared_sem("softplus_one_plus", 1), pg.shared_sem("softplus_log", 1)

    def scalar(self, e):
        a1, a2, a3, _ = self.t
        self.asked.wait(e, 1)
        e.activation(a1, a1, ACT.Exp, scale=-1.0).then_inc(self.exps.sem, 1)
        self.ones.wait(e, 1)
        e.activation(a3, a2, ACT.Ln).then_inc(self.logs.sem, 1)

    def vector(self, e, ch):
        v = self.v
        a1, a2, a3, a4 = self.t
        e.scalar_tensor_tensor(out=a1, in0=v, scalar=-1.0, in1=v, op0=ALU.mult, op1=ALU.max).then_inc(self.asked.sem, 1)
        self.exps.wait(e, 1)
        e.tensor_scalar(a2, a1, 1.0, None, ALU.add).then_inc(self.ones.sem, 1)
        self.logs.wait(e, 1)
        ch(e.tensor_scalar(a2, a2, -1.0, None, ALU.add))
        ch(e.tensor_scalar(a4, a2, 0.0, None, ALU.is_equal))
        ch(e.tensor_tensor(a2, a2, a4, ALU.add))
        ch(e.reciprocal(a2, a2))
        ch(e.tensor_tensor(a3, a3, a1, ALU.mult))
        ch(e.tensor_tensor(a3, a3, a2, ALU.mult))
        ch(e.tensor_tensor(a4, a4, a1, ALU.mult))
        ch(e.tensor_tensor(a3, a3, a4, ALU.add))
        ch(e.scalar_tensor_tensor(out=v, in0=v, scalar=0.0, in1=a3, op0=ALU.max, op1=ALU.add))


def row_of(pg, r):
    return pg.ident[0:64, r:r + 1].to_broadcast([64, P])


def both(lo, hi):
    return [(0, slice(0, 32), lo), (1, slice(32, 64), hi)]


def chunk_scan(e, ch, out, data, reset):
    ch(e.tensor_tensor_scan(out[0:32, :], reset[0:32, :], data[0:32, :], 0.0, ALU.mult, ALU.add))
    ch(e.tensor_tensor_scan(out[32:64, ::-1], reset[32:64, :], data[32:64, ::-1], 0.0, ALU.mult, ALU.add))


def dh_cols(v):
    return v.rearrange("p (d r) -> p d r", r=32)[:, :, 0:4]


def convolve(pg, e, ch, u, out, w, b, tile):
    n = 6
    ch(e.tensor_scalar(out[:, tile, :], u[:, tile, 1:T + 1], pg.col(w, n + tile), pg.col(b, tile), ALU.mult, ALU.add))
    ch(e.scalar_tensor_tensor(out=out[:, tile, :], in0=u[:, tile, 0:T], scalar=pg.col(w, tile), in1=out[:, tile, :],
                              op0=ALU.mult, op1=ALU.add))
    return e.scalar_tensor_tensor(out=out[:, tile, :], in0=u[:, tile, 2:T + 2], scalar=pg.col(w, 2 * n + tile),
                                  in1=out[:, tile, :], op0=ALU.mult, op1=ALU.add)


def to_fm(pg, name, y, tile0, gain=None, times=None, small=None):
    out = Mem(pg.big, M_Y2, M_W2)(KT, T)
    sums, roots, ready, turned, copied = (pg.shared_sem(f"to_fm_{n}", c) for n, c in (
        ("sums", 1 if gain else 0), ("roots", 1 if gain else 0), ("ready", NCH if gain else 0), ("turned", NCH),
        ("copied", NCH)))
    if gain:
        ss, rr, scr = small[:, 0:8], small[:, 8:16], small[:, 16:16 + 256]

    def vector(e):
        ch = pg.vchain(e)
        if gain:
            if times is not None:
                ch(e.tensor_tensor(y, y, times, ALU.mult))
            for c in range(NCH):
                ch(e.tensor_tensor_reduce(scr, y[:, c, :], y[:, c, :], 1.0, 0.0, ALU.mult, ALU.add, ss[:, c:c + 1]))
            e.drain().then_inc(sums.sem, 1)
            roots.wait(e, 1)
            ch(e.reciprocal(rr, rr))
            for c in range(NCH):
                e.scalar_tensor_tensor(out=y[:, c, :], in0=y[:, c, :], scalar=rr[:, c:c + 1], in1=pg.param(gain),
                                       op0=ALU.mult, op1=ALU.mult).then_inc(ready.sem, 1)

    def scalar(e):
        if gain:
            sums.wait(e, 1)
            e.activation(rr, ss, ACT.Sqrt, bias=pg.eps[:, 0:1], scale=1.0 / 256).then_inc(roots.sem, 1)
        for c in range(NCH):
            turned.wait(e, c + 1)
            e.activation(out[:, tile0:tile0 + 2, c * P:(c + 1) * P],
                         pg.ps[:, c % 2, 0:256].rearrange("p (a b) -> p a b", b=P), ACT.Copy).then_inc(copied.sem, 1)

    def tensor(e):
        for c in range(NCH):
            if gain:
                ready.wait(e, c + 1)
            if c >= 2:
                copied.wait(e, c - 1)
            for b in range(2):
                mm = e.transpose(pg.ps[:, c % 2, b * P:(b + 1) * P], y[:, c, b * P:(b + 1) * P], pg.ident)
            mm.then_inc(turned.sem, 1)

    pg.stage(name=name, vector=vector, scalar=scalar, tensor=tensor)


def ssd(pg):
    m = Mem(pg.big, M_W2, M_END)
    Z = m(NCH, 256)
    U = m(6, T + 2)
    XC = m(6, T)
    ST = m(2, NCH, 256)
    G = m(2, P)
    tri = m(2, P)
    acT, dtT, nac, ea, wc = (m(NCH, 8) for _ in range(5))
    cd, last = m(8, NCH), m(8, NCH)
    small = m(16)
    mu = Mem(pg.big, M_W2 + NCH * 256, M_END)
    XB = mu(NCH, 512)
    YT = mu(NCH, 256)
    mx_ = Mem(pg.big, M_W2 + NCH * 256 + 6 * (T + 2), M_END)
    Dd, Mm = mx_(8, P), mx_(8, P)
    my = Mem(pg.big, M_Y2 + 2 * T, M_W2)
    DT, A1, A2, A3, A4, reset = (my(T) for _ in range(6))
    rows = slice(0, 64)
    DTr, A1r, A2r, A3r, A4r, rr = (v[rows] for v in (DT, A1, A2, A3, A4, reset))
    xw = A2.rearrange("p (a b) -> p a b", a=4)
    off = A3[:, 0:512]
    off_d = A3[:, 512:768]
    scr = A4
    h = pg.h2
    k_at = len(pg.stages)
    tables = pg.sem("ssd_tables_loaded")

    linear_tm(pg, "ssd_gate", pg.d["w_z"], lambda k, t: h[:, k, t * P:(t + 1) * P], list(range(NCH)), 256,
              lambda e, g, t, bank: e.activation(Z[:, t, :], bank, ACT.Silu), "scalar")
    linear_fm(pg, "ssd_in", pg.d["w_xbc"], KT, lambda k, a, b: h[:, k, a:b], 6, TWO_SPANS,
              lambda e, t, s, bank, ab: e.activation(U[:, t, 1 + ab[0]:1 + ab[1]], bank, ACT.Copy), "scalar")
    linear_rows(pg, "ssd_steps", pg.d["w_dt"], 1,
                lambda e, t, s, bank: e.activation(DTr[:, s * HALF:(s + 1) * HALF], bank, ACT.Identity,
                                                   bias=pg.col("dt_bias", parts=64)), "scalar")

    sp = Softplus(pg, DTr, (A1r, A2r, A3r, A4r))
    conv, a_rd = pg.sem("ssd_convolved"), pg.sem("ssd_decay_rates")

    def pool(e):
        e.wait_ge(pg.stage_done, 3 * k_at)
        e.dma_start(tri, pg.d["tri_add"]).then_inc(tables, 16)
        e.dma_start(reset, pg.d["reset_128"]).then_inc(tables, 16)

    def vector(e):
        ch = pg.vchain(e)
        e.memset(U[:, :, 0:1], 0.0)
        ch(e.memset(U[:, :, T + 1:T + 2], 0.0))
        sp.vector(e, ch)
        e.wait_ge(a_rd, 1)
        ch(e.tensor_scalar(small[0:64, 1:2], small[0:64, 0:1], -1.0, None, ALU.mult))
        ch(e.tensor_scalar(A1r, DTr, small[0:64, 1:2], None, ALU.mult))
        e.wait_ge(tables, 32)
        chunk_scan(e, ch, A1r, A1r, rr)
        for t in range(6):
            convolve(pg, e, ch, U, XC, "cw", "cb", t).then_inc(conv, 1)

    def scalar(e):
        sp.scalar(e)
        e.activation(small[0:64, 0:1], pg.col("a_log", parts=64), ACT.Exp).then_inc(a_rd, 1)
        for t in range(6):
            e.wait_ge(conv, t + 1)
            e.activation(XC[:, t, :], XC[:, t, :], ACT.Silu)

    pg.stage(name="ssd_convolution", gpsimd=pool, vector=vector, scalar=scalar)

    turned, copied, t_cols, c_cols = (pg.shared_sem(f"chunk_{n}", NCH) for n in (
        "turned", "turned_copied", "cols_turned", "cols_copied"))
    l_rd, l_cp, e_rd = pg.sem("ssd_ends"), pg.sem("ssd_ends_copied"), pg.sem("ssd_exps")

    def tensor(e):
        for c in range(NCH):
            if c >= 2:
                copied.wait(e, c - 1)
            for b in range(4):
                mm = e.transpose(pg.ps[:, c % 2, b * P:(b + 1) * P], XC[:, b, c * P:(c + 1) * P], pg.ident)
            mm.then_inc(turned.sem, 1)
            if c >= 2:
                c_cols.wait(e, c - 1)
            e.transpose(pg.ps[:, 2 + c % 2, 0:64], A1r[:, c * P:(c + 1) * P], pg.ident[0:64, 0:64])
            e.transpose(pg.ps[:, 2 + c % 2, 64:128], DTr[:, c * P:(c + 1) * P], pg.ident[0:64, 0:64]).then_inc(t_cols.sem, 1)
        for r in range(8):
            d, hh = divmod(r, 4)
            mm = e.matmul(pg.ps[:, 4, 8 * r:8 * r + 8], row_of(pg, 32 * d + hh),
                          A1r[:, (C2 - 1 if d == 0 else 0)::C2], start=True, stop=True)
        mm.then_inc(l_rd, 1)

    def scalar(e):
        for c in range(NCH):
            turned.wait(e, c + 1)
            e.activation(XB[:, c, :], pg.ps[:, c % 2, :], ACT.Copy).then_inc(copied.sem, 1)
        e.wait_ge(l_cp, 1)
        e.activation(ea, acT, ACT.Exp)
        e.activation(cd, last, ACT.Exp)
        e.activation(wc, wc, ACT.Exp).then_inc(e_rd, 1)

    def vector(e):
        ch = pg.vchain(e)
        for c in range(NCH):
            t_cols.wait(e, c + 1)
            e.tensor_copy(acT[:, c, :].rearrange("p (d r) -> p d r", d=2), dh_cols(pg.ps[:, 2 + c % 2, 0:64]))
            e.tensor_copy(dtT[:, c, :].rearrange("p (d r) -> p d r", d=2), dh_cols(pg.ps[:, 2 + c % 2, 64:128])).then_inc(c_cols.sem, 1)
        e.wait_ge(l_rd, 1)
        c_cols.wait(e, NCH)
        ch(e.tensor_copy(last, pg.ps[:, 4, 0:64].rearrange("p (r c) -> p r c", c=NCH)))
        ch(e.tensor_scalar(nac, acT, -1.0, None, ALU.mult))
        e.tensor_tensor(wc, last.rearrange("p r c -> p c r"), acT, ALU.subtract).then_inc(l_cp, 1)
        e.wait_ge(e_rd, 1)
        ch(e.tensor_tensor(wc, wc, dtT, ALU.mult))

    pg.stage(name="ssd_columns", tensor=tensor, scalar=scalar, vector=vector)

    order = [(s, d, s if d == 0 else NCH - 1 - s) for s in range(NCH - 1) for d in range(2)]
    w_rd, u_rd, s_rd = (pg.shared_sem(f"chunk_{n}", len(order)) for n in ("weighted", "updates", "states"))

    def tensor(e):
        for n, (s, d, c) in enumerate(order):
            w_rd.wait(e, n + 1)
            if n >= 2:
                s_rd.wait(e, n - 1)
            for b in range(2):
                mm = e.matmul(pg.ps[:, n % 2, b * P:(b + 1) * P], XB[:, c, 256 + b * P:256 + (b + 1) * P],
                              xw[:, n % 4, b * P:(b + 1) * P], start=True, stop=True)
            mm.then_inc(u_rd.sem, 1)

    def vector(e):
        ch = pg.vchain(e)
        e.memset(ST[:, 0, 0, :], 0.0)
        ch(e.memset(ST[:, 1, NCH - 1, :], 0.0))
        for n in range(len(order) + 2):
            if n < len(order):
                s, d, c = order[n]
                e.tensor_tensor(xw[:, n % 4, :].rearrange("p (h x) -> p h x", x=64),
                                XB[:, c, 0:256].rearrange("p (h x) -> p h x", x=64),
                                bc(wc[:, c, 4 * d:4 * d + 4], [P, 4, 64]), ALU.mult).then_inc(w_rd.sem, 1)
            if n >= 2:
                s, d, c = order[n - 2]
                nx = c + 1 if d == 0 else c - 1
                ch(e.tensor_tensor(ST[:, d, nx, :].rearrange("p (h x) -> p h x", x=64),
                                   ST[:, d, c, :].rearrange("p (h x) -> p h x", x=64),
                                   bc(cd[:, 4 * d:4 * d + 4, c], [P, 4, 64]), ALU.mult))
                u_rd.wait(e, n - 1)
                e.tensor_tensor(ST[:, d, nx, :], ST[:, d, nx, :], pg.ps[:, n % 2, 0:256], ALU.add).then_inc(s_rd.sem, 1)
                s_rd.wait(e, n - 1)

    pg.stage(name="ssd_states", tensor=tensor, vector=vector)

    p_rd, m_rd, x_rd, s2_rd, y_rd, y_cp = (pg.shared_sem(f"chunk_{n}", NCH) for n in (
        "products", "masked", "decays", "scores", "outputs", "summed"))
    g_cp = pg.sem("ssd_products_copied")

    def tensor(e):
        def pre(c):
            if c:
                e.wait_ge(g_cp, c)
                m_rd.wait(e, c)
            t = slice(c * P, c * P + P)
            for b in range(2):
                e.matmul(pg.ps[:, 0, b * P:(b + 1) * P], XC[:, 2 + b, t], XC[:, 4 + b, t], start=True, stop=True)
            for r in range(8):
                mm = e.matmul(pg.ps[:, 1 + r // 4, (r % 4) * P:(r % 4 + 1) * P], row_of(pg, 32 * (r // 4) + r % 4),
                              A1r[:, t], start=True, stop=True)
            mm.then_inc(p_rd.sem, 1)

        pre(0)
        for c in range(NCH):
            if c + 1 < NCH:
                pre(c + 1)
            s2_rd.wait(e, c + 1)
            if c:
                y_cp.wait(e, c)
            for hh in range(4):
                for d in range(2):
                    e.matmul(pg.ps[:, 3, hh * 64:hh * 64 + 64], Mm[:, 4 * d + hh, :], XB[:, c, hh * 64:hh * 64 + 64],
                             start=(d == 0), stop=(d == 1))
            for d in range(2):
                for b in range(2):
                    mm = e.matmul(pg.ps[:, 4, 256 * d + P * b:256 * d + P * b + P], XC[:, 4 + b, c * P:(c + 1) * P],
                                  ST[:, d, c, b * P:(b + 1) * P], start=True, stop=True)
            mm.then_inc(y_rd.sem, 1)

    def scalar(e):
        for c in range(NCH):
            p_rd.wait(e, c + 1)
            if c:
                s2_rd.wait(e, c)
            e.activation(G, pg.ps[:, 0, 0:256].rearrange("p (a b) -> p a b", b=P), ACT.Copy).then_inc(g_cp, 1)
            m_rd.wait(e, c + 1)
            for r in range(8):
                ins = e.activation(Dd[:, r, :], Dd[:, r, :], ACT.Exp, bias=nac[:, c, r:r + 1])
            ins.then_inc(x_rd.sem, 1)

    def vector(e):
        ch = pg.vchain(e)

        def masked(c):
            p_rd.wait(e, c + 1)
            for d in range(2):
                ins = e.tensor_tensor(Dd[:, 4 * d:4 * d + 4, :], pg.ps[:, 1 + d, :].rearrange("p (a b) -> p a b", b=P),
                                      tri[:, d:d + 1, :].to_broadcast([P, 4, P]), ALU.add)
            ins.then_inc(m_rd.sem, 1)

        masked(0)
        for c in range(NCH):
            x_rd.wait(e, c + 1)
            e.wait_ge(g_cp, c + 1)
            if c:
                y_rd.wait(e, c)
            for r in range(8):
                ins = e.scalar_tensor_tensor(out=Mm[:, r, :], in0=G[:, (r % 4) // 2, :], scalar=dtT[:, c, r:r + 1],
                                             in1=Dd[:, r, :], op0=ALU.mult, op1=ALU.mult)
            ins.then_inc(s2_rd.sem, 1)
            s2_rd.wait(e, c + 1)
            if c + 1 < NCH:
                masked(c + 1)
            ch(e.tensor_tensor(off_d.rearrange("p (h x) -> p h x", x=64), XB[:, c, 0:256].rearrange("p (h x) -> p h x", x=64),
                               bc(pg.param("ssd_d"), [P, 4, 64]), ALU.mult))
            y_rd.wait(e, c + 1)
            ch(e.tensor_tensor(off.rearrange("p (h x) -> p h x", x=64), pg.ps[:, 4, :].rearrange("p (h x) -> p h x", x=64),
                               bc(ea[:, c, :], [P, 8, 64]), ALU.mult))
            ch(e.tensor_tensor(YT[:, c, :], off_d, pg.ps[:, 3, 0:256], ALU.add))
            ch(e.tensor_tensor(YT[:, c, :], YT[:, c, :], off[:, 0:256], ALU.add))
            e.tensor_tensor(YT[:, c, :], YT[:, c, :], off[:, 256:512], ALU.add).then_inc(y_cp.sem, 1)
        y_cp.wait(e, NCH)

    pg.stage(name="ssd_outputs", tensor=tensor, scalar=scalar, vector=vector)
    to_fm(pg, "ssd_out", YT, 0, "ssd_g", Z, scr)


def neighbourhood(pg):
    m = Mem(pg.big, M_W2, M_END)
    kf = m(2, T)
    v, vs = m(NCH, 256), m(NCH - 1, 256)
    QD = m(2, 16, P)
    table, tmask = m(2, 15 * 64), m(2, 15 * 64)
    S = m(4, HALF)
    PT = m(2, 4, P)
    stat = m(4, 32)
    y = Mem(pg.big, M_Y2, M_W2)(KT, T)
    sq, rr = y[:, 4:6, :], y[:, 6, :]
    h = pg.h2
    k_at = len(pg.stages)
    tables, moved = pg.sem("na_tables_loaded"), pg.sem("na_values_moved")

    def pool(e):
        e.wait_ge(pg.stage_done, 3 * k_at)
        e.dma_start(table, pg.d["na_bias"]).then_inc(tables, 16)
        e.dma_start(tmask, pg.d["na_mask"]).then_inc(tables, 16)

    def vector(e):
        ch = pg.vchain(e)
        e.memset(QD, 0.0)
        e.wait_ge(tables, 32)
        ch(e.tensor_tensor(table, table, tmask, ALU.add))

    pg.stage(name="na_tables", gpsimd=pool, vector=vector)

    def q_out(e, t, s, bank, ab):
        for hh in range(2):
            r = slice(64 * hh, 64 * hh + 64)
            ins = e.activation(QD[r, t, 8 * s:8 * s + 8, 64 * hh:64 * hh + 64],
                               bank[r, :].rearrange("p (a b) -> p a b", b=64), ACT.Copy, scale=0.125)
        return ins
    linear_fm(pg, "na_q", pg.d["w_nq"], KT, lambda k, a, b: h[:, k, a:b], 2, TWO_SPANS, q_out, "scalar")
    linear_fm(pg, "na_k", pg.d["w_nk"], KT, lambda k, a, b: h[:, k, a:b], 2, TWO_SPANS,
              lambda e, t, s, bank, ab: e.activation(kf[:, t, ab[0]:ab[1]], bank, ACT.Copy), "scalar")
    linear_tm(pg, "na_v", pg.d["w_nv"], lambda k, t: h[:, k, t * P:(t + 1) * P], list(range(NCH)), 256,
              lambda e, g, t, bank: e.activation(v[:, t, :], bank, ACT.Copy), "scalar")
    k_mv = len(pg.stages)

    def pool(e):
        e.wait_ge(pg.stage_done, 3 * k_mv)
        e.dma_start(vs[0:64], v[64:128, 0:NCH - 1, :]).then_inc(moved, 16)
        e.dma_start(vs[64:128], v[0:64, 1:NCH, :]).then_inc(moved, 16)

    N = 32
    sc, sm, ex, pr, tr, pt, pv, yo = (pg.sem(f"na_{n}") for n in (
        "scores", "maxima", "exps", "probs", "turns", "turned", "outputs", "stored"))
    mx, nm, rs, ri = (stat[:, i, :] for i in range(4))

    def where(i):
        r, pair = divmod(i, 2)
        return r, pair, min(max(r - 4, 0), 8)

    def tensor(e):
        e.wait_ge(moved, 32)

        def scores(i):
            r, pair, base = where(i)
            if i >= 2:
                e.wait_ge(sm, i - 1)
            e.matmul(pg.ps[:, i % 2, :], QD[:, pair, r, :], kf[:, pair, base * 64:base * 64 + HALF],
                     start=True, stop=True).then_inc(sc, 1)

        def turn(i):
            e.wait_ge(pr, i + 1)
            if i >= 2:
                e.wait_ge(pt, i - 1)
            for b in range(4):
                mm = e.transpose(pg.ps[:, 2 + i % 2, b * P:(b + 1) * P], S[:, i % 4, b * P:(b + 1) * P], pg.ident)
            mm.then_inc(tr, 1)

        def values(i):
            r, pair, base = where(i)
            e.wait_ge(pt, i + 1)
            if i >= 2:
                e.wait_ge(yo, i - 1)
            for b in range(4):
                vv = v[:, base // 2 + b, :] if base % 2 == 0 else vs[:, base // 2 + b, :]
                mm = e.matmul(pg.ps[:, 4 + i % 2, 0:P], vv[:, pair * P:(pair + 1) * P], PT[:, i % 2, b, :],
                              start=(b == 0), stop=(b == 3))
            mm.then_inc(pv, 1)

        for i in range(N + 3):
            if i < N:
                scores(i)
            if 2 <= i < N + 2:
                turn(i - 2)
            if i >= 3:
                values(i - 3)

    def vector(e):
        ch = pg.vchain(e)
        for i in range(N + 1):
            if i < N:
                r, pair, base = where(i)
                e.wait_ge(sc, i + 1)
                if i >= 4:
                    e.wait_ge(tr, i - 3)
                dr = base - r + 7
                ch(e.tensor_tensor_reduce(S[:, i % 4, :], pg.ps[:, i % 2, :], table[:, pair, dr * 64:dr * 64 + HALF],
                                          1.0, -BIG, ALU.add, ALU.max, mx[:, i:i + 1]))
                e.tensor_scalar(nm[:, i:i + 1], mx[:, i:i + 1], -1.0, None, ALU.mult).then_inc(sm, 1)
            if i >= 1:
                q = i - 1
                e.wait_ge(ex, q + 1)
                ch(e.reciprocal(ri[:, q:q + 1], rs[:, q:q + 1]))
                e.tensor_scalar(S[:, q % 4, :], S[:, q % 4, :], ri[:, q:q + 1], None, ALU.mult).then_inc(pr, 1)

    def scalar(e):
        for i in range(N + 4):
            if i < N:
                e.wait_ge(sm, i + 1)
                e.activation(S[:, i % 4, :], S[:, i % 4, :], ACT.Exp, bias=nm[:, i:i + 1],
                             accum_out=rs[:, i:i + 1]).then_inc(ex, 1)
            if 2 <= i < N + 2:
                q = i - 2
                e.wait_ge(tr, q + 1)
                if q >= 2:
                    e.wait_ge(pv, q - 1)
                e.activation(PT[:, q % 2, :, :], pg.ps[:, 2 + q % 2, :].rearrange("p (a b) -> p a b", b=P),
                             ACT.Copy).then_inc(pt, 1)
            if i >= 4:
                q = i - 4
                r, pair, _ = where(q)
                e.wait_ge(pv, q + 1)
                for hh in range(2):
                    rw = slice(64 * hh, 64 * hh + 64)
                    ins = e.activation(y[rw, 2 + pair, r * 64:r * 64 + 64], pg.ps[rw, 4 + q % 2, 64 * hh:64 * hh + 64],
                                       ACT.Copy)
                ins.then_inc(yo, 1)

    pg.stage(name="na_attention", gpsimd=pool, tensor=tensor, vector=vector, scalar=scalar)

    squares, sums, roots = pg.sem("na_squares"), pg.sem("na_sums"), pg.sem("na_roots")

    def scalar(e):
        e.activation(sq, y[:, 2:4, :], ACT.Square).then_inc(squares, 1)
        e.wait_ge(sums, 1)
        e.activation(rr, pg.ps[:, 0:2, :].rearrange("p a b -> p (a b)"), ACT.Sqrt, bias=pg.eps[:, 0:1],
                     scale=1.0 / 256).then_inc(roots, 1)

    def tensor(e):
        e.wait_ge(squares, 1)
        for s in range(2):
            for t in range(2):
                mm = e.matmul(pg.ps[:, s, :], pg.ones, sq[:, t, s * HALF:(s + 1) * HALF], start=(t == 0), stop=(t == 1))
        mm.then_inc(sums, 1)

    def vector(e):
        ch = pg.vchain(e)
        e.wait_ge(roots, 1)
        ch(e.reciprocal(rr, rr))
        for t in range(2):
            ch(e.scalar_tensor_tensor(out=y[:, 2 + t, :], in0=y[:, 2 + t, :], scalar=pg.col("na_g", t), in1=rr,
                                      op0=ALU.mult, op1=ALU.mult))

    pg.stage(name="na_norm", tensor=tensor, vector=vector, scalar=scalar)


def mlstm(pg):
    m = Mem(pg.big, M_W2, M_END)
    qf, kf = m(2, T), m(2, T)
    KTm = m(NCH, 256)
    V1 = m(NCH, 4, 65)
    OG = m(NCH, 256)
    at = m.at
    YT = m(NCH, 256)
    ST = m(2, NCH, 2 * 65)
    Dd = m(8, P)
    cols = m(NCH, 4, 8)
    kw = m(4, 256)
    I2 = m(4, 65)
    H2 = m(256)
    cdb = m(4, NCH)
    tri = m(2, P)
    den = m(8)
    mp, rl, cdr = m(NCH), m(NCH), m(NCH)
    ssum, srt = m(32), m(32)
    reset = m(T)
    early = Mem(pg.big, at, M_END)
    A = [early(T)[0:64] for _ in range(4)]
    my = Mem(pg.big, M_Y2 + 4 * T, M_W2)
    LI, NB, R, WS = (my(T)[0:64] for _ in range(4))
    WI = Dd.rearrange("p a b -> p (a b)")[0:64]
    y_all = Mem(pg.big, M_Y2, M_W2)(KT, T)
    rr = reset[0:64]
    h = pg.h2
    k_at = len(pg.stages)
    tables = pg.sem("ml_tables_loaded")
    FM = lambda k, a, b: h[:, k, a:b]
    TM = lambda k, t: h[:, k, t * P:(t + 1) * P]

    linear_fm(pg, "ml_q", pg.d["w_mq"], KT, FM, 2, TWO_SPANS,
              lambda e, t, s, bank, ab: e.activation(qf[:, t, ab[0]:ab[1]], bank, ACT.Copy), "scalar")
    linear_fm(pg, "ml_k", pg.d["w_mk"], KT, FM, 2, TWO_SPANS,
              lambda e, t, s, bank, ab: e.activation(kf[:, t, ab[0]:ab[1]], bank, ACT.Copy, scale=0.125), "scalar")
    linear_tm(pg, "ml_v", pg.d["w_mv"], TM, list(range(NCH)), 256,
              lambda e, g, t, bank: e.activation(V1[:, t, :, 0:64], bank.rearrange("p (a b) -> p a b", b=64), ACT.Copy), "scalar")
    linear_tm(pg, "ml_o", pg.d["w_mo"], TM, list(range(NCH)), 256,
              lambda e, g, t, bank: e.activation(OG[:, t, :], bank, ACT.Sigmoid), "scalar")

    def g_out(e, t, s, bank):
        a = slice(s * HALF, (s + 1) * HALF)
        if t == 0:
            return e.tensor_scalar(LI[:, a], bank, pg.col("ib", parts=64), None, ALU.add)
        return e.tensor_scalar(NB[:, a], bank, pg.col("fb", parts=64), -1.0, ALU.add, ALU.mult)
    linear_rows(pg, "ml_gates", pg.d["w_mg"], 2, g_out, "vector")

    sp = Softplus(pg, NB, A)
    diff = pg.sem("ml_differences")

    def pool(e):
        e.wait_ge(pg.stage_done, 3 * k_at)
        e.dma_start(tri, pg.d["tri_add"]).then_inc(tables, 16)
        e.dma_start(reset, pg.d["reset_128"]).then_inc(tables, 16)

    def vector(e):
        ch = pg.vchain(e)
        ch(e.memset(V1[:, :, :, 64:65], 1.0))
        sp.vector(e, ch)
        e.wait_ge(tables, 32)
        chunk_scan(e, ch, A[0], NB, rr)
        ch(e.tensor_copy(NB, A[0]))
        ch(e.tensor_tensor(LI, LI, NB, ALU.add))
        ch(e.memset(mp, 0.0))
        for s in range(NCH):
            for d in range(2):
                c = s if d == 0 else NCH - 1 - s
                rw = slice(32 * d, 32 * d + 32)
                t = slice(c * C2, (c + 1) * C2)
                src, dst = LI[rw, t], R[rw, t]
                end = C2 - 1
                if d == 1:
                    src, dst, end = src[:, ::-1], dst[:, ::-1], 0
                ch(e.tensor_tensor_scan(dst, src, src, mp[rw, c:c + 1], ALU.max, ALU.max))
                e_at = c * C2 + end
                ch(e.tensor_copy(rl[rw, c:c + 1], R[rw, e_at:e_at + 1]))
                if s + 1 < NCH:
                    nx = c + 1 if d == 0 else c - 1
                    ch(e.tensor_tensor(mp[rw, nx:nx + 1], rl[rw, c:c + 1], NB[rw, e_at:e_at + 1], ALU.subtract))
        v3 = lambda v: v.rearrange("p (c t) -> p c t", t=C2)
        n64 = slice(0, 64)
        ch(e.tensor_tensor(v3(WI), bc(mp[n64], [64, NCH, C2]), v3(R), ALU.subtract))
        ch(e.tensor_tensor(NB, NB, R, ALU.subtract))
        ch(e.tensor_tensor(v3(WS), v3(LI), bc(rl[n64], [64, NCH, C2]), ALU.subtract))
        ch(e.tensor_scalar(R, R, -1.0, None, ALU.mult))
        e.tensor_tensor(cdr[n64], mp[n64], rl[n64], ALU.subtract).then_inc(diff, 1)

    def scalar(e):
        sp.scalar(e)
        e.wait_ge(diff, 1)
        for v in (WI, NB, WS, cdr[0:64]):
            e.activation(v, v, ACT.Exp)

    pg.stage(name="ml_rows", gpsimd=pool, vector=vector, scalar=scalar)

    turned, copied, t_cols, c_cols = (pg.shared_sem(f"chunk_{n}", NCH) for n in (
        "turned", "turned_copied", "cols_turned", "cols_copied"))
    c_rd = pg.sem("ml_carries")

    def tensor(e):
        for c in range(NCH):
            t = slice(c * P, (c + 1) * P)
            if c >= 2:
                copied.wait(e, c - 1)
            for b in range(2):
                mm = e.transpose(pg.ps[:, c % 2, b * P:(b + 1) * P], kf[:, b, t], pg.ident)
            mm.then_inc(turned.sem, 1)
            if c >= 2:
                c_cols.wait(e, c - 1)
            for n, v in enumerate((LI, WI, NB, WS)):
                mm = e.transpose(pg.ps[:, 2 + c % 2, 64 * n:64 * n + 64], v[:, t], pg.ident[0:64, 0:64])
            mm.then_inc(t_cols.sem, 1)
        for n in range(4):
            d, pair = divmod(n, 2)
            r = 32 * d + 2 * pair
            for j in range(2):
                mm = e.matmul(pg.ps[64 * j:64 * j + 64, 4, 8 * n:8 * n + 8],
                              pg.ident[0:64, r + j:r + j + 1].to_broadcast([64, 64]), cdr[0:64], start=True, stop=True)
        mm.then_inc(c_rd, 1)

    def scalar(e):
        for c in range(NCH):
            turned.wait(e, c + 1)
            e.activation(KTm[:, c, :], pg.ps[:, c % 2, 0:256], ACT.Copy).then_inc(copied.sem, 1)

    def vector(e):
        for c in range(NCH):
            t_cols.wait(e, c + 1)
            e.tensor_copy(cols[:, c, :, :].rearrange("p n (d r) -> p (n d) r", r=4),
                          pg.ps[:, 2 + c % 2, 0:256].rearrange("p (n r) -> p n r", r=32)[:, :, 0:4]).then_inc(c_cols.sem, 1)
        e.wait_ge(c_rd, 1)
        e.tensor_copy(cdb, pg.ps[:, 4, 0:32].rearrange("p (n c) -> p n c", c=NCH))

    pg.stage(name="ml_columns", tensor=tensor, scalar=scalar, vector=vector)

    order = [(s, d, s if d == 0 else NCH - 1 - s) for s in range(NCH - 1) for d in range(2)]
    w_rd, u_rd, s_rd = (pg.shared_sem(f"chunk_{n}", len(order)) for n in ("weighted", "updates", "states"))

    def tensor(e):
        for n, (s, d, c) in enumerate(order):
            w_rd.wait(e, n + 1)
            if n >= 2:
                s_rd.wait(e, n - 1)
            for hh in range(4):
                mm = e.matmul(pg.ps[64 * (hh % 2):64 * (hh % 2) + 64, n % 2, 65 * (hh // 2):65 * (hh // 2) + 65],
                              kw[:, n % 4, 64 * hh:64 * hh + 64], V1[:, c, hh, :], start=True, stop=True)
            mm.then_inc(u_rd.sem, 1)

    def vector(e):
        ch = pg.vchain(e)
        e.memset(ST[:, 0, 0, :], 0.0)
        ch(e.memset(ST[:, 1, NCH - 1, :], 0.0))
        for n in range(len(order) + 2):
            if n < len(order):
                s, d, c = order[n]
                e.tensor_tensor(kw[:, n % 4, :].rearrange("p (h x) -> p h x", x=64),
                                KTm[:, c, :].rearrange("p (h x) -> p h x", x=64),
                                bc(cols[:, c, 3, 4 * d:4 * d + 4], [P, 4, 64]), ALU.mult).then_inc(w_rd.sem, 1)
            if n >= 2:
                s, d, c = order[n - 2]
                nx = c + 1 if d == 0 else c - 1
                u_rd.wait(e, n - 1)
                for pair in range(2):
                    a = slice(65 * pair, 65 * pair + 65)
                    ins = e.scalar_tensor_tensor(out=ST[:, d, nx, a], in0=ST[:, d, c, a],
                                                 scalar=cdb[:, 2 * d + pair, c:c + 1], in1=pg.ps[:, n % 2, a],
                                                 op0=ALU.mult, op1=ALU.add)
                ins.then_inc(s_rd.sem, 1)
                s_rd.wait(e, n - 1)

    pg.stage(name="ml_states", tensor=tensor, vector=vector)

    p_rd, m_rd, x2_rd, sc_rd, y_rd, y_cp = (pg.shared_sem(f"chunk_{n}", NCH) for n in (
        "products", "masked", "decays", "scores", "outputs", "summed"))

    def tensor(e):
        def pre(c):
            if c:
                sc_rd.wait(e, c)
            t = slice(c * P, c * P + P)
            for hh in range(4):
                r = slice(64 * (hh % 2), 64 * (hh % 2) + 64)
                e.matmul(pg.ps[:, hh % 2, (hh // 2) * P:(hh // 2 + 1) * P], kf[r, hh // 2, t], qf[r, hh // 2, t], start=True, stop=True)
            for r in range(8):
                mm = e.matmul(pg.ps[:, 2 + r // 4, (r % 4) * P:(r % 4 + 1) * P], row_of(pg, 32 * (r // 4) + r % 4),
                              R[:, t], start=True, stop=True)
            mm.then_inc(p_rd.sem, 1)

        pre(0)
        for c in range(NCH):
            sc_rd.wait(e, c + 1)
            if c:
                y_cp.wait(e, c)
            for d in range(2):
                for hh in range(4):
                    r = slice(64 * (hh % 2), 64 * (hh % 2) + 64)
                    a, at = slice(65 * hh, 65 * hh + 65), 65 * (2 * d + hh // 2)
                    e.matmul(pg.ps[:, 4 + d, a], Dd[:, 4 * d + hh, :], V1[:, c, hh, :], start=True, stop=True)
                    mm = e.matmul(pg.ps[:, 6 + hh % 2, at:at + 65], qf[r, hh // 2, c * P:(c + 1) * P],
                                  ST[r, d, c, 65 * (hh // 2):65 * (hh // 2) + 65], start=True, stop=True)
            mm.then_inc(y_rd.sem, 1)
            if c + 1 < NCH:
                pre(c + 1)

    def scalar(e):
        for c in range(NCH):
            m_rd.wait(e, c + 1)
            for r in range(8):
                ins = e.activation(Dd[:, r, :], Dd[:, r, :], ACT.Exp, bias=cols[:, c, 0, r:r + 1])
            ins.then_inc(x2_rd.sem, 1)

    def vector(e):
        ch = pg.vchain(e)
        for c in range(NCH):
            p_rd.wait(e, c + 1)
            for d in range(2):
                ins = e.tensor_tensor(Dd[:, 4 * d:4 * d + 4, :], pg.ps[:, 2 + d, :].rearrange("p (a b) -> p a b", b=P),
                                      tri[:, d:d + 1, :].to_broadcast([P, 4, P]), ALU.add)
            ins.then_inc(m_rd.sem, 1)
            x2_rd.wait(e, c + 1)
            for d in range(2):
                pairs = Dd[:, 4 * d:4 * d + 4, :].rearrange("p (i j) t -> p i j t", j=2)
                ins = e.tensor_tensor(pairs, pairs,
                                      pg.ps[:, 0:2, 0:2 * P].rearrange("p j (i t) -> p i j t", t=P), ALU.mult)
            ins.then_inc(sc_rd.sem, 1)
            y_rd.wait(e, c + 1)
            for d in range(2):
                four = slice(4 * d, 4 * d + 4)
                ch(e.tensor_tensor(I2.rearrange("p (i j) x -> p i j x", j=2),
                                   pg.ps[:, 6:8, 130 * d:130 * d + 130].rearrange("p j (i x) -> p i j x", x=65),
                                   bc(cols[:, c, 1, four].rearrange("p (i j) -> p i j", j=2), [P, 2, 2, 65]), ALU.mult))
                ch(e.tensor_tensor(I2, I2, pg.ps[:, 4 + d, 0:260].rearrange("p (a b) -> p a b", b=65), ALU.add))
                ch(e.scalar_tensor_tensor(out=den[:, four], in0=I2[:, :, 64], scalar=-1.0, in1=I2[:, :, 64],
                                          op0=ALU.mult, op1=ALU.max))
                ch(e.tensor_tensor(den[:, four], den[:, four], cols[:, c, 2, four], ALU.max))
                ch(e.reciprocal(den[:, four], den[:, four]))
                dst = YT[:, c, :] if d == 0 else H2
                ch(e.tensor_tensor(dst.rearrange("p (h x) -> p h x", x=64), I2[:, :, 0:64],
                                   bc(den[:, four], [P, 4, 64]), ALU.mult))
            e.tensor_tensor(YT[:, c, :], YT[:, c, :], H2, ALU.add).then_inc(y_cp.sem, 1)
        y_cp.wait(e, NCH)

    pg.stage(name="ml_outputs", tensor=tensor, scalar=scalar, vector=vector)

    sums, roots = pg.sem("ml_norm_sums"), pg.sem("ml_norm_roots")
    SQ = KTm

    def vector(e):
        ch = pg.vchain(e)
        heads = lambda v: v.rearrange("p c (h x) -> p (c h) x", x=64)
        ch(e.tensor_tensor(SQ, YT, YT, ALU.mult))
        e.tensor_reduce(ssum, heads(SQ), AX.X, ALU.add).then_inc(sums, 1)
        e.wait_ge(roots, 1)
        ch(e.reciprocal(srt, srt))
        ch(e.tensor_tensor(heads(YT), heads(YT), bc(srt, [P, 32, 64]), ALU.mult))
        ch(e.tensor_tensor(YT, YT, pg.param("ml_g").unsqueeze(1).to_broadcast([P, NCH, 256]), ALU.mult))
        ch(e.tensor_tensor(YT, YT, OG, ALU.mult))

    def scalar(e):
        e.wait_ge(sums, 1)
        e.activation(srt, ssum, ACT.Sqrt, bias=pg.eps[:, 0:1], scale=1.0 / 64).then_inc(roots, 1)

    pg.stage(name="ml_norm", vector=vector, scalar=scalar)
    to_fm(pg, "ml_out", YT, 4)


def hyena(pg):
    NF = KT
    m = Mem(pg.big, M_W2, M_END)
    U = Mem(pg.big, M_W2, M_END)(6, T + 2)
    FA, FB = m(NF, 512), m(NF, 512)
    Zt = m(3, NCH, 256)
    at = m.at
    SUM = m(NCH, 512)
    two = Mem(pg.big, at, M_END)
    YC, YS = two(NF, 256), two(NF, 256)
    alt = m(P + 1)
    fN = m(512)
    zN = m(256)
    stp = m(256)
    small = Mem(pg.big, at, M_END)(16 + 256)
    XC = Mem(pg.big, M_H, M_HID)(6, T)
    HT = Mem(pg.big, M_H, M_HID)(NCH, 1024)
    early = Mem(pg.big, M_W2, M_END)
    feats, e1, e2, e3 = (early(T) for _ in range(4))
    w1, w2, w3 = early(64), early(64), early(1024)
    win = SUM.rearrange("p a b -> p (a b)")[:, 0:2048].rearrange("p (a b) -> p a b", b=256)
    scr = SUM.rearrange("p a b -> p (a b)")[:, 2048:4096].rearrange("p (a b) -> p a b", a=2)
    k_at = len(pg.stages)
    h = pg.h2
    tables = pg.sem("hy_tables_loaded")

    linear_fm(pg, "hy_in", pg.d["w_hy"], KT, lambda k, a, b: h[:, k, a:b], 6, TWO_SPANS,
              lambda e, t, s, bank, ab: e.activation(U[:, t, 1 + ab[0]:1 + ab[1]], bank, ACT.Copy), "scalar")
    conv = pg.sem("hy_convolved")
    turned, copied = pg.sem("hy_turned"), pg.sem("hy_turned_copied")

    def vector(e):
        ch = pg.vchain(e)
        e.memset(U[:, :, 0:1], 0.0)
        ch(e.memset(U[:, :, T + 1:T + 2], 0.0))
        for t in range(6):
            convolve(pg, e, ch, U, XC, "hcw", "hcb", t).then_inc(conv, 1)

    def tensor(e):
        n = 0
        for t in range(6):
            e.wait_ge(conv, t + 1)
            for half in range(2):
                if n >= 2:
                    e.wait_ge(copied, n - 1)
                for c in range(4):
                    a = (4 * half + c) * P
                    mm = e.transpose(pg.ps[:, n % 2, c * P:(c + 1) * P], XC[:, t, a:a + P], pg.ident)
                mm.then_inc(turned, 1)
                n += 1

    def scalar(e):
        for n in range(12):
            t, half = divmod(n, 2)
            e.wait_ge(turned, n + 1)
            e.activation(Zt[:, t // 2, 4 * half:4 * half + 4, (t % 2) * P:(t % 2 + 1) * P],
                         pg.ps[:, n % 2, :].rearrange("p (a b) -> p a b", b=P), ACT.Copy).then_inc(copied, 1)

    pg.stage(name="hy_convolution", tensor=tensor, vector=vector, scalar=scalar)
    k_f = len(pg.stages)

    def pool(e):
        e.wait_ge(pg.stage_done, 3 * k_f)
        for dst, src in ((feats[0:HY_F], "hy_feats"), (w1[0:HY_F], "hy_w1"), (w2[0:64], "hy_w2"), (w3[0:64], "hy_w3"),
                         (win, "hy_window"), (alt, "alternate")):
            e.dma_start(dst, pg.d[src]).then_inc(tables, 16)

    a_rd, r_rd, s_rd, f_rd, f_cp = (pg.sem(f"hy_{n}") for n in ("layer", "angle", "sine", "filter", "filter_windowed"))
    r64 = slice(0, 64)

    def tensor(e):
        e.wait_ge(tables, 96)
        for layer in range(2):
            if layer:
                e.wait_ge(s_rd, 1)
            for s in range(2):
                mm = e.matmul(pg.ps[0:64, s, :], w1[0:HY_F] if layer == 0 else w2[r64],
                              (feats[0:HY_F] if layer == 0 else e1[r64])[:, s * HALF:(s + 1) * HALF], start=True, stop=True)
            mm.then_inc(a_rd, 1)
        e.wait_ge(s_rd, 2)
        for c in range(NCH):
            if c >= 2:
                e.wait_ge(f_cp, c - 1)
            for s in range(2):
                mm = e.matmul(pg.ps[:, 2 + 2 * (c % 2) + s, :], e1[r64, c * P:(c + 1) * P], w3[r64, s * HALF:(s + 1) * HALF],
                              start=True, stop=True)
            mm.then_inc(f_rd, 1)

    def scalar(e):
        for layer in range(2):
            e.wait_ge(r_rd, layer + 1)
            e.activation(e1[r64], e2[r64], ACT.Sin).then_inc(s_rd, 1)

    def vector(e):
        ch = pg.vchain(e)
        for layer in range(2):
            e.wait_ge(a_rd, layer + 1)
            x, k = e2[r64], e3[r64]
            ch(e.tensor_scalar(x, pg.ps[r64, 0:2, :].rearrange("p a b -> p (a b)"), pg.col("hb1" if layer == 0 else "hb2", parts=64),
                               pg.col("hfreq", layer, parts=64), ALU.add, ALU.mult))
            ch(e.tensor_scalar(k, x, 1.0 / (2.0 * math.pi), ROUND, ALU.mult, ALU.add))
            ch(e.tensor_scalar(k, k, -ROUND, None, ALU.add))
            ch(e.scalar_tensor_tensor(out=x, in0=k, scalar=-TURN_HI, in1=x, op0=ALU.mult, op1=ALU.add))
            ch(e.scalar_tensor_tensor(out=x, in0=k, scalar=-TURN_LO, in1=x, op0=ALU.mult, op1=ALU.add))
            e.tensor_scalar(x, x, 3.1415925, -3.1415925, ALU.min, ALU.max).then_inc(r_rd, 1)
        for c in range(NCH):
            e.wait_ge(f_rd, c + 1)
            for s in range(2):
                ins = e.tensor_tensor(HT[:, c, s * HALF:(s + 1) * HALF].rearrange("p (d x) -> p d x", d=2),
                                      pg.ps[:, 2 + 2 * (c % 2) + s, :].rearrange("p (d x) -> p d x", d=2),
                                      win[:, c:c + 1, :].to_broadcast([P, 2, 256]), ALU.mult)
            ins.then_inc(f_cp, 1)

    pg.stage(name="hy_network", gpsimd=pool, tensor=tensor, vector=vector, scalar=scalar)

    sq_rd, ss_rd, rt_rd = pg.sem("hy_squares"), pg.sem("hy_square_sums"), pg.sem("hy_roots")

    def tensor(e):
        for c in range(NCH):
            e.wait_ge(sq_rd, c + 1)
            for o in range(2):
                for d in range(2):
                    mm = e.matmul(pg.ps[:, o, 0:256], pg.ones, scr[:, c % 2, 512 * o + 256 * d:512 * o + 256 * d + 256],
                                  start=(c == 0 and d == 0), stop=(c == NCH - 1 and d == 1))
            mm.then_inc(ss_rd, 1)

    rn = e2[:, 0:512].rearrange("p (o x) -> p o x", o=2)

    def scalar(e):
        for c in range(NCH):
            if c >= 2:
                e.wait_ge(ss_rd, c - 1)
            e.activation(scr[:, c % 2, :], HT[:, c, :], ACT.Square).then_inc(sq_rd, 1)
        e.wait_ge(ss_rd, NCH)
        e.activation(rn, pg.ps[:, 0:2, 0:256], ACT.Sqrt, bias=pg.eps[:, 0:1]).then_inc(rt_rd, 1)

    def vector(e):
        ch = pg.vchain(e)
        e.wait_ge(rt_rd, 1)
        ch(e.reciprocal(rn, rn))
        for c in range(NCH):
            for d in range(2):
                v = HT[:, c, :].rearrange("p (o d x) -> p o d x", o=2, d=2)[:, :, d, :]
                ch(e.tensor_tensor(v, v, rn, ALU.mult))
        ch(e.memset(HT[0:1, 0, :].rearrange("p (o d x) -> p o d x", o=2, d=2)[:, :, 1, :], 0.0))
        for c in range(NCH):
            v = HT[:, c, :].rearrange("p (o d x) -> p o d x", o=2, d=2)
            s = SUM[:, c, :].rearrange("p (o x) -> p o x", o=2)
            ch(e.tensor_tensor(s, v[:, :, 0, :], v[:, :, 1, :], ALU.add))
            ch(e.tensor_tensor(v[:, :, 0, :], v[:, :, 0, :], v[:, :, 1, :], ALU.subtract))

    pg.stage(name="hy_filters", tensor=tensor, vector=vector, scalar=scalar)

    def groups(fills, n=NF):
        g = pg.take_groups([pg.fill + fills * (i + 1) for i in range(n)])
        f = pg.fill
        pg.fill += fills * n
        return g, f

    def sync_of(g0):
        def sync(e):
            for n in range(NF):
                pg.load(e, g0 + n, pg.d["dft"][n])
        return sync

    gF, fF = groups(2)
    nyq = pg.sem("hy_last_frequency")

    def tensor(e):
        for n in range(NF):
            slot = pg.weights(e, gF + n)
            for t in range(2):
                f = fF + 2 * n + t
                pg.bank_free(e, f)
                for k in range(NCH):
                    rhs = SUM[:, k, :] if t == 0 else HT[:, k, :].rearrange("p (o d x) -> p o d x", o=2, d=2)[:, :, 0, :]
                    mm = e.matmul(pg.ps[:, f % 8, :], slot[:, (2 * k + t) * P:(2 * k + t + 1) * P], rhs,
                                  start=(k == 0), stop=(k == NCH - 1))
                mm.then_inc(pg.ps_full, 1)
        e.wait_ge(pg.ps_free, fF + 2 * NF)
        for k in range(NCH):
            mm = e.matmul(pg.ps[0:1, 0, :], alt[:, 0:1], SUM[:, k, :], start=(k == 0), stop=(k == NCH - 1))
        mm.then_inc(nyq, 1)

    def vector(e):
        ch = pg.vchain(e)
        e.wait_ge(pg.ps_free, fF)
        for n in range(NF):
            for t in range(2):
                f = fF + 2 * n + t
                e.wait_ge(pg.ps_full, f + 1)
                e.tensor_scalar((FA, FB)[t][:, n, :], pg.ps[:, f % 8, :], 2.0 / (2 * T), None, ALU.mult).then_inc(pg.ps_free, 1)
        e.wait_ge(nyq, 1)
        e.wait_ge(pg.ps_free, fF + 2 * NF)
        ch(e.tensor_scalar(fN[0:1, :], pg.ps[0:1, 0, :], 1.0 / (2 * T), None, ALU.mult))
        ch(e.tensor_scalar(FA[0:1, 0, :], FA[0:1, 0, :], 0.5, None, ALU.mult))

    pg.stage(name="hy_filter_dft", sync=sync_of(gF), tensor=tensor, vector=vector)

    for o in range(2):
        z, gate = Zt[:, 0, :, :], Zt[:, 1 + o, :, :]
        fa, fb = FA[:, :, 256 * o:256 * o + 256], FB[:, :, 256 * o:256 * o + 256]
        g1, f1 = groups(2)
        nq = pg.shared_sem("hy_last_of_z", 1)

        def tensor(e, g1=g1, f1=f1, z=z, nq=nq):
            for n in range(NF):
                slot = pg.weights(e, g1 + n)
                for t in range(2):
                    f = f1 + 2 * n + t
                    pg.bank_free(e, f)
                    for k in range(NCH):
                        mm = e.matmul(pg.ps[:, f % 8, 0:256], slot[:, (2 * k + t) * P:(2 * k + t + 1) * P], z[:, k, :],
                                      start=(k == 0), stop=(k == NCH - 1))
                    mm.then_inc(pg.ps_full, 1)
            e.wait_ge(pg.ps_free, f1 + 2 * NF)
            for k in range(NCH):
                mm = e.matmul(pg.ps[0:1, 0, 0:256], alt[:, 0:1], z[:, k, :], start=(k == 0), stop=(k == NCH - 1))
            mm.then_inc(nq.sem, 1)

        def vector(e, f1=f1, fa=fa, fb=fb, nq=nq, o=o):
            ch = pg.vchain(e)
            e.wait_ge(pg.ps_free, f1)
            for n in range(NF):
                f = f1 + 2 * n
                e.wait_ge(pg.ps_full, f + 2)
                pc, qs = pg.ps[:, f % 8, 0:256], pg.ps[:, (f + 1) % 8, 0:256]
                ch(e.tensor_tensor(YC[:, n, :], fa[:, n, :], pc, ALU.mult))
                ch(e.tensor_tensor(stp, fb[:, n, :], qs, ALU.mult))
                ch(e.tensor_tensor(YC[:, n, :], YC[:, n, :], stp, ALU.subtract))
                ch(e.tensor_tensor(YS[:, n, :], fb[:, n, :], pc, ALU.mult))
                e.tensor_tensor(stp, fa[:, n, :], qs, ALU.mult).then_inc(pg.ps_free, 2)
                e.wait_ge(pg.ps_free, f + 2)
                ch(e.tensor_tensor(YS[:, n, :], YS[:, n, :], stp, ALU.add))
            nq.wait(e, 1)
            ch(e.tensor_tensor(zN[0:1, :], fN[0:1, 256 * o:256 * o + 256], pg.ps[0:1, 0, 0:256], ALU.mult))

        pg.stage(name=f"hy_dft_{o}", sync=sync_of(g1), tensor=tensor, vector=vector)

        g2, f2 = groups(1)

        def tensor(e, g2=g2, f2=f2):
            for n in range(NCH):
                slot = pg.weights(e, g2 + n)
                f = f2 + n
                pg.bank_free(e, f)
                bank = pg.ps[:, f % 8, 0:256]
                for k in range(NF):
                    for t in range(2):
                        e.matmul(bank, slot[:, (2 * k + t) * P:(2 * k + t + 1) * P], (YC, YS)[t][:, k, :],
                                 start=(k == 0 and t == 0), stop=False)
                e.matmul(bank, alt[0:1, 1:P + 1], zN[0:1, :], start=False, stop=True).then_inc(pg.ps_full, 1)

        def vector(e, f2=f2, z=z, gate=gate, o=o):
            ch = pg.vchain(e)
            e.wait_ge(pg.ps_free, f2)
            for n in range(NCH):
                f = f2 + n
                ch(e.tensor_tensor(z[:, n, :], z[:, n, :], pg.param("hskip")[:, 256 * o:256 * o + 256], ALU.mult))
                e.wait_ge(pg.ps_full, f + 1)
                e.tensor_tensor(z[:, n, :], z[:, n, :], pg.ps[:, f % 8, 0:256], ALU.add).then_inc(pg.ps_free, 1)
                e.wait_ge(pg.ps_free, f + 1)
                ch(e.tensor_tensor(z[:, n, :], z[:, n, :], gate[:, n, :], ALU.mult))

        pg.stage(name=f"hy_inverse_{o}", sync=sync_of(g2), tensor=tensor, vector=vector)

    to_fm(pg, "hy_out", Zt[:, 0, :, :], 6, "hy_g", None, small)


def block_2(pg):
    x, h = pg.x, pg.h2

    def vector(e):
        ch = pg.vchain(e)
        ch(e.tensor_scalar(pg.sc2a, pg.mod2[:, 8:16], 1.0, None, ALU.add))
        ch(e.tensor_scalar(pg.sc2b, pg.mod2[:, 32:40], 1.0, None, ALU.add))
    pg.stage(name="scales_2", vector=vector)
    half = lambda v: (lambda s: v[:, :, s * HALF:(s + 1) * HALF])
    norm(pg, "norm_mix_2", half(x), half(h), [HALF, HALF], lambda s, k: pg.sc2a[:, k:k + 1], lambda s, k: pg.mod2[:, k:k + 1])
    ssd(pg)
    neighbourhood(pg)
    mlstm(pg)
    hyena(pg)
    y = Mem(pg.big, M_Y2, M_W2)(KT, T)

    def out(e, tile, s, bank, ab):
        xs = x[:, bass.ds(tile, 1), ab[0]:ab[1]].rearrange("p a b -> p (a b)")
        return e.scalar_tensor_tensor(out=xs, in0=bank, scalar=pg.mod2[:, bass.ds(16 + tile, 1)], in1=xs,
                                      op0=ALU.mult, op1=ALU.add)
    linear_fm(pg, "merge_2", pg.d["w_out2"], KT, lambda k, a, b: y[:, k, a:b], KT, TWO_SPANS, out, "vector")
    norm(pg, "norm_ffn_2", half(x), half(pg.whole), [HALF, HALF], lambda s, k: pg.sc2b[:, k:k + 1], lambda s, k: pg.mod2[:, 24 + k:25 + k],
         parts=pg.h_parts)
    ffn(pg, "ffn_2", pg.d["w_gu2"], pg.d["w_down2"], lambda t: pg.mod2[:, 40 + t:41 + t])
    norm(pg, "norm_final", half(x), half(h), [HALF, HALF], lambda s, k: pg.col("final_g", k), None)
    pg.result = h


def block_2_layout(l0, o, gu):
    f = np.float32
    w = l0["w_in_2"]
    o["mod_w"] = fm_groups(l0["mod_w_2"], 2)
    o["w_z"] = tm_groups(w[:, 0:256], 256)
    o["w_xbc"] = fm_groups(w[:, 256:1024], 2)

    def rows(cols):
        k, n = cols.shape[:2]
        v = np.zeros((k, n, 2, 32), f)
        v[:, :, :, 0:4] = cols
        return v.reshape(KT, P, n * 64).transpose(1, 0, 2).reshape(1, P, -1)
    o["w_dt"] = rows(w[:, 1024:1032].reshape(D, 1, 2, 4))
    na = w[:, 1032:1800]
    o["w_nq"], o["w_nk"] = fm_groups(na[:, 0:256], 2), fm_groups(na[:, 256:512], 2)
    o["w_nv"] = tm_groups(na[:, 512:768], 256)
    ml = w[:, 1800:2840]
    o["w_mq"], o["w_mk"] = fm_groups(ml[:, 0:256], 2), fm_groups(ml[:, 256:512], 2)
    o["w_mv"], o["w_mo"] = tm_groups(ml[:, 512:768], 256), tm_groups(ml[:, 768:1024], 256)
    o["w_mg"] = rows(ml[:, 1024:1040].reshape(D, 2, 2, 4))
    o["w_hy"] = fm_groups(w[:, 2840:3608], 2)
    o["w_out2"] = fm_groups(l0["w_out_2"], 2)
    o["w_gu2"] = gu(l0["ffn_w_gate_2"], l0["ffn_w_up_2"])
    o["w_down2"] = down_groups(l0["ffn_w_down_2"])
    o["hy_w1"], o["hy_w2"], o["hy_w3"] = l0["hy_w1_2"], l0["hy_w2_2"], l0["hy_w3_2"]

    rpb = l0["na_rpb_2"]
    q, k = np.arange(64)[:, None], np.arange(64)[None]
    first = np.clip(q - 8, 0, 48)
    valid = (k >= first) & (k < first + 16)
    dist = np.where(valid, k - q + 15, 0)
    bias = np.where(valid[None, None], rpb[:, :, dist], f(0.0))
    o["na_bias"] = bias.transpose(0, 2, 1, 3).reshape(2, P, 15 * 64).transpose(1, 0, 2)
    mask = np.where(valid, 0, -BIG).astype(f)
    mask = np.broadcast_to(mask[None, :, None], (2, 64, 15, 64)).reshape(P, 1, 960)
    o["na_mask"] = np.broadcast_to(mask, (P, 2, 960))

    s, t = np.arange(P)[:, None], np.arange(P)[None]
    o["tri_add"] = np.stack([np.where(s <= t, 0, -BIG), np.where(s >= t, 0, -BIG)], 1).astype(f)
    o["reset_128"] = np.broadcast_to((np.arange(T) % C2 != 0).astype(f), (P, T))

    bands = (HY_F - 1) // 2
    tt = np.linspace(0.0, 1.0, T, dtype=f)
    ff = np.linspace(1e-4, bands - 1, bands, dtype=f)
    ang = (f(2.0 * math.pi) * (np.arange(T, dtype=f) / f(T))[:, None] * ff[None]).astype(f)
    o["hy_feats"] = np.concatenate([tt[:, None], np.cos(ang), -np.sin(ang)], 1).astype(f).T
    deltas = np.abs(np.linspace(math.log(1e-2) / 1.5, math.log(1e-2) / 0.3, 256, dtype=f))
    o["hy_window"] = np.exp(-tt[:, None] * deltas[None]).astype(f).reshape(NCH, P, 256).transpose(1, 0, 2)
    n = np.arange(T)
    turns = (n[:, None] * n[None]) % (2 * T) * (np.pi / T)
    o["dft"] = fm_groups(np.stack([np.cos(turns).reshape(T, KT, P), np.sin(turns).reshape(T, KT, P)], 2)
                         .reshape(T, 2 * T).astype(f), 2)
    alt = np.zeros((P, P + 1), f)
    alt[:, 0] = (-1.0) ** np.arange(P)
    alt[0, 1:] = (-1.0) ** np.arange(P)
    o["alternate"] = alt


def build_program(nc, dram, out, stop=None):
    with ExitStack() as ctx:
        pg = Program(nc, ctx, dram)
        block_1(pg)
        if stop != 1:
            block_2(pg)
        stages = pg.stages if stop is None or stop < 10 else pg.stages[:stop - 10]
        result = pg.x if stop == 1 else pg.result
        stored = pg.sem("output_stored")
        block = ctx.enter_context(nc.Block())

        def compute(e, engine):
            for n, st in enumerate(stages):
                if engine in st:
                    st[engine](e)
                e.drain().then_inc(pg.stage_done, 1)
                e.wait_ge(pg.stage_done, 3 * (n + 1))

        @block.sync
        def _(e):
            for st in stages:
                if "sync" in st:
                    st["sync"](e)
            e.wait_ge(pg.stage_done, 3 * len(stages))
            e.dma_start(out, result).then_inc(stored, 16)
            e.wait_ge(stored, 16)

        @block.gpsimd
        def _(e):
            for st in stages:
                if "gpsimd" in st:
                    st["gpsimd"](e)

        @block.tensor
        def _(e):
            compute(e, "tensor")

        @block.scalar
        def _(e):
            compute(e, "scalar")

        @block.vector
        def _(e):
            compute(e, "vector")
        return pg


def fm_groups(w, per):
    k, n = w.shape
    return w.reshape(k // P, P, n // (per * P), per, P).transpose(2, 1, 0, 3, 4).reshape(n // (per * P), P, -1)


def down_groups(w):
    return w.reshape(FT // 2, 2, P, D).transpose(0, 2, 1, 3).reshape(FT // 2, P, 2 * D)


def tm_groups(w, cols):
    k, n = w.shape
    return w.reshape(k // P, P, n // cols, cols).transpose(2, 1, 0, 3).reshape(n // cols, P, -1)


def column(v):
    return v.reshape(-1, P).T


def rows_of(v, n=4):
    c = np.zeros((P, 1), v.dtype)
    c[0:n, 0] = v[0]
    c[32:32 + n, 0] = v[1]
    return c


def constants():
    f = np.float32
    c = {"ident": np.eye(P, dtype=f), "ones_64": np.kron(np.eye(2), np.ones((64, 64))).astype(f)}
    pos = np.arange(T)
    inv = (f(10000.0) ** (-np.arange(0, 32, 2, dtype=f) / f(32))).astype(f)
    d = np.arange(P) % 64
    at = np.where((d < 32)[:, None], (pos // 64)[None], (pos % 64)[None]).astype(f)
    ang = at * inv[d % 16][:, None]
    c["rope_cos"], c["rope_sin"] = np.cos(ang).astype(f), np.sin(ang).astype(f)
    turn = np.zeros((P, P), f)
    for m in range(P):
        turn[m + 16 if m % 32 < 16 else m - 16, m] = -1.0 if m % 32 < 16 else 1.0
    c["rope_turn"] = turn
    qi, kj = np.arange(P)[:, None], np.arange(P)[None]
    masks = np.zeros((P, 3, 640), f)
    masks[:, :, 256:384] = np.where(kj >= qi, 0, -BIG)[:, None]
    masks[:, :, 512:640] = np.where(kj <= qi, 0, -BIG)[:, None]
    masks[:, 1, 256:384] = -BIG
    masks[:, 2, 512:640] = -BIG
    c["window_masks"] = masks
    same = qi // 32 == kj // 32
    c["tri_32"] = np.stack([same & (qi <= kj), same & (qi >= kj)], 1).astype(np.int32)
    c["reset_32"] = np.broadcast_to((np.arange(TA) % 32 != 0).astype(f), (P, TA)).copy()
    return c


def lay_out(i):
    g = {k: np.asarray(v) for k, v in i.items()}
    l0 = {k: v[0] for k, v in g.items() if k not in ("hgrn_lb_logits", "c_ctx", "final_norm_g_2")}
    o = constants()
    w = l0["w_in"]
    o["x_t"] = l0["x"].T.reshape(KT, P, T).transpose(1, 0, 2)
    o["ctx_t"] = l0["ctx"].T.reshape(KT, P, TC).transpose(1, 0, 2)
    o["w_ada"] = fm_groups(l0["w_ada"], 2)
    heads = [h * 64 + n for j in range(4) for h in (j, 4 + j) for n in range(64)]
    o["w_q"] = fm_groups(w[:, 2816:3328][:, heads], 2)
    o["w_k"] = fm_groups(w[:, 1536:1664], 1)
    o["w_v"] = tm_groups(w[:, 1664:1792], P)
    o["w_inp"] = tm_groups(w[:, 1024:1536], 256)
    hg = []
    for h in range(4):
        c = slice(h * P, h * P + P)
        hg.append(fm_groups(np.concatenate([w[:, 0:512][:, c], w[:, 512:1024][:, c]], 1), 2)[0])
        hg.append(fm_groups(np.concatenate([w[:, 1792:2304][:, c], w[:, 2304:2816][:, c]], 1), 2)[0])
    o["w_hgrn"] = np.stack(hg)
    gates = w[:, 3328:5376]
    o["w_merge"] = np.concatenate([fm_groups(l0["w_branch_hgrn"], 1), fm_groups(l0["w_branch_attn"][heads], 1),
                                   fm_groups(gates[:, 0:D], 1), fm_groups(gates[:, D:], 1)], 2)
    o["w_out1"] = fm_groups(l0["w_out"], 2)

    def gu(a, b):
        k, n = a.shape
        return fm_groups(np.stack([a.reshape(k, n // P, P), b.reshape(k, n // P, P)], 2).reshape(k, 2 * n), 2)
    o["w_gu1"] = gu(l0["w_ffn_gate"], l0["w_ffn_up"])
    o["w_down1"] = down_groups(l0["w_ffn_down"])
    block_2_layout(l0, o, gu)

    pp = np.zeros((P, NPP), np.float32)

    def put(name, v):
        at, n = PP[name]
        pp[:, at:at + n] = v

    def wide(v):
        return np.broadcast_to(v.reshape(1, -1), (P, v.size))
    put("cond", np.stack([column(l0["c"]), column(g["c_ctx"]), column(l0["c_2"])], 2).reshape(P, -1))
    put("b_ada", column(l0["b_ada"]))
    put("mod_b", column(l0["mod_b_2"]))
    put("norm_mix", column(l0["norm_mix_w"]))
    put("norm_ffn", column(l0["norm_ffn_w"]))
    put("final_g", column(g["final_norm_g_2"]))
    put("lb", column(g["hgrn_lb_logits"]))
    put("hg_norm", column(l0["hgrn_norm_w"]))
    put("q_norm", column(np.concatenate([l0["q_norm_w"]] * 2)))
    put("k_norm", column(np.concatenate([l0["k_norm_w"]] * 2)))
    put("sink", wide(l0["attn_sinks"]))
    put("cw", column(l0["ssd_conv_w_2"]))
    put("cb", column(l0["ssd_conv_b_2"]))
    put("dt_bias", rows_of(l0["ssd_dt_bias_2"]))
    put("a_log", rows_of(l0["ssd_a_log_2"]))
    put("ssd_d", wide(l0["ssd_d_2"]))
    put("ssd_g", wide(l0["ssd_norm_g_2"]))
    put("na_g", column(l0["na_norm_g_2"]))
    put("ib", rows_of(l0["ml_i_bias_2"]))
    put("fb", rows_of(l0["ml_f_bias_2"]))
    put("ml_g", wide(l0["ml_norm_g_2"]))
    put("hcw", column(l0["hy_conv_w_2"]))
    put("hcb", column(l0["hy_conv_b_2"]))
    pad = np.zeros(64, np.float32)
    put("hb1", column(np.concatenate([l0["hy_b1_2"], pad])))
    put("hb2", column(np.concatenate([l0["hy_b2_2"], pad])))
    put("hfreq", column(np.stack([np.concatenate([l0["hy_freq_2"][n], pad]) for n in range(2)])))
    put("hskip", wide(l0["hy_skip_2"]))
    put("hy_g", wide(l0["hy_norm_g_2"]))
    o["params"] = pp
    return {k: np.ascontiguousarray(v) for k, v in o.items()}


def kernel(**inputs):
    import concourse.bacc as _bacc
    from concourse.bass_utils import run_bass_kernel_spmd as _run

    nc = _bacc.Bacc("TRN2", target_bir_lowering=False, num_devices=1)
    arrays = lay_out(inputs)
    dram = {n: nc.dram_tensor(f"in_{n}", list(a.shape), mybir.dt.from_np(a.dtype), kind="ExternalInput").ap()
            for n, a in arrays.items()}
    out = nc.dram_tensor("out_x", [P, KT, T], F32, kind="ExternalOutput").ap()
    build_program(nc, dram, out)
    r = _run(nc, [{f"in_{n}": a for n, a in arrays.items()}], core_ids=[0])
    got = r.results[0]["out_x"]
    return got.transpose(1, 0, 2).reshape(1, D, T).transpose(0, 2, 1)
```

```python
import math
from contextlib import ExitStack

import numpy as np

import concourse.bass as bass
from concourse import mybir

F32 = mybir.dt.float32
F32R = mybir.dt.float32r
I32 = mybir.dt.int32
ALU = mybir.AluOpType
ACT = mybir.ActivationFunctionType
AX = mybir.AxisListType

P = 128
D = 1024
KT = D // P
T = 1024
TC = 256
TA = TC + T
HALF = 512
EPS = 1e-6
FF = 2816
FT = FF // P
BIG = 1e30

PP = {}
_n = 0
for _name, _w in (
    ("cond", 3 * KT), ("b_ada", 48), ("mod_b", 48), ("norm_mix", KT), ("norm_ffn", KT), ("final_g", KT),
    ("lb", 16), ("hg_norm", 1), ("q_norm", 1), ("k_norm", 1), ("sink", 8),
    ("cw", 18), ("cb", 6), ("dt_bias", 1), ("a_log", 1), ("ssd_d", 4), ("ssd_g", 256), ("na_g", 2),
    ("ib", 1), ("fb", 1), ("ml_g", 256), ("hcw", 18), ("hcb", 6), ("hb1", 1), ("hb2", 1), ("hfreq", 2),
    ("hskip", 512), ("hy_g", 256),
):
    PP[_name] = (_n, _w)
    _n += _w
NPP = _n

SLOT = 24 * P
M_RING = 2560
M_MAIN = M_RING + 2 * SLOT
M_X = M_MAIN
M_H = M_X + KT * T
M_B1 = M_H + KT * TA
M_YAT = M_B1
M_YHG = M_YAT + 4 * T
M_W1 = M_YHG + 4 * T
M_HID = M_H + KT * T
M_Y2 = M_HID
M_W2 = M_Y2 + KT * T
M_END = 53100
M_PARTS = M_END - 4 * KT * T


def repeat(e, n, body):
    with e.Fori(0, n) as i:
        body(i)


class Chain:

    def __init__(self, e, sem):
        self.e, self.sem, self.n = e, sem, 0

    def __call__(self, ins):
        self.n += 1
        ins.then_inc(self.sem, 1)
        self.e.wait_ge(self.sem, self.n)


class Signal:

    def __init__(self, sem, base):
        self.sem, self.base = sem, base

    def wait(self, e, n):
        e.wait_ge(self.sem, self.base + n)


class Words:

    def __init__(self, tensors):
        self.tensors = tensors

    def __getitem__(self, key):
        rows, words = key
        for a, b, v in self.tensors:
            if a <= words.start and words.stop <= b:
                return v[rows, words.start - a:words.stop - a]
        raise IndexError(words)


class Mem:

    def __init__(self, big, at, end):
        self.big, self.at, self.end = big, at, end

    def __call__(self, *shape, parts=P):
        n = int(np.prod(shape))
        v = self.big[0:parts, self.at:self.at + n]
        self.at += n
        assert self.at <= self.end, (self.at, self.end)
        if len(shape) == 2:
            v = v.rearrange("p (a b) -> p a b", a=shape[0])
        if len(shape) == 3:
            v = v.rearrange("p (a b c) -> p a b c", a=shape[0], b=shape[1])
        return v


def in_turn(*parts):
    def run(e):
        for part in parts:
            part(e)
    return run


def bc(ap, shape):
    return ap.unsqueeze(len(ap.shape)).to_broadcast(shape)


class Program:

    def __init__(self, nc, ctx, dram):
        self.nc, self.ctx, self.d = nc, ctx, dram
        tensor = lambda name, a, b: (a, b, nc.sbuf_tensor(name, [P, b - a], F32))
        own = [tensor("parameters", 0, M_RING), tensor("weight_ring", M_RING, M_X), tensor("x", M_X, M_H)]
        own = [(a, b, ctx.enter_context(v)) for a, b, v in own]
        with nc.sbuf_tensor("work", [P, M_END - M_H], F32) as v:
            self.big = Words(own + [(M_H, M_END, v)])
        with nc.sbuf_tensor("before_split", [P, KT * T + 2 * HALF], F32) as v:
            m = Mem(v, 0, KT * T + 2 * HALF)
            self.whole, self.whole_rs = m(KT, T), m(2, HALF)
            self.whole_hid = self.whole[:, 0:2, :]
        ctx.enter_context(nc.sbuf_tensor("work_below_parts", [P, M_PARTS - M_H], F32))

        def parts(name, a, b):
            m = Mem(ctx.enter_context(nc.sbuf_tensor(name, [P, 2 * a * b], F32R)), 0, 2 * a * b)
            return [m(a, b), m(a, b)]
        self.w_parts = parts("weight_parts", 2, 2048)
        self.hid_parts = parts("hidden_parts", 4, T)
        self.h_parts = parts("input_parts", KT, T)
        self.ps = ctx.enter_context(nc.psum_tensor("banks", [P, 8, HALF], F32))
        self._v = self._a = None
        self.shared = {}
        self.group = 0
        self.fill = 0
        self.stages = []
        self.ends = []
        self.w_ready = [self.sem(f"weights_ready_{s}") for s in range(2)]
        self.ps_full = self.sem("bank_full")
        self.ps_free = self.sem("bank_read")
        self.stage_done = self.sem("stage_done")
        self.loaded = self.sem("parameters_loaded")
        self.vch = self.sem("vector_step")
        self.ach = self.sem("scalar_step")
        m = Mem(self.big, 0, M_RING)
        self.pp = m(NPP)
        self.ident = m(P)
        self.ones = m(P)
        self.silu_c = m(KT, 3)
        self.mod1 = m(48, 2)
        self.mod2 = m(48)
        self.sc_mix = m(KT, 2)
        self.sc_ffn = m(KT)
        self.sc2a = m(KT)
        self.sc2b = m(KT)
        self.eps = m(1)
        self.perm_left = m
        self.slots = [self.big[:, M_RING + s * SLOT:M_RING + (s + 1) * SLOT] for s in range(2)]
        self.spare = self.big[:, M_RING:M_X].rearrange("p (a n) -> p a n", a=2)[:, :, 2048:SLOT]
        self.x = Mem(self.big, M_X, M_H)(KT, T)
        self.h2 = Mem(self.big, M_H, M_END)(KT, T)
        self.h1 = Mem(self.big, M_H, M_END)(KT, TA)

    def sem(self, name):
        return self.ctx.enter_context(self.nc.semaphore(name))

    def col(self, name, i=0, n=1, parts=P):
        at = PP[name][0] + i
        return self.pp[0:parts, at:at + n]

    def param(self, name, parts=P):
        at, w = PP[name]
        return self.pp[0:parts, at:at + w]

    def stage(self, **parts):
        self.stages.append(parts)

    def shared_sem(self, name, count):
        if name not in self.shared:
            self.shared[name] = [self.sem(name), 0]
        sem, base = self.shared[name]
        self.shared[name][1] += count
        return Signal(sem, base)

    def together(self, name, n, scalar=None, scalar_after=None, **parts):
        last = self.stages[-n:]
        del self.stages[-n:]
        stage = {"name": name}
        for engine in ("sync", "tensor", "gpsimd", "vector", "scalar"):
            todo = [s[engine] for s in last if engine in s]
            if engine == "scalar":
                todo = [v for v in [scalar] + todo + [scalar_after] if v]
            elif engine in parts:
                todo.append(parts[engine])
            if todo:
                stage[engine] = in_turn(*todo)
        self.stages.append(stage)

    def scratch(self, *shape):
        n = int(np.prod(shape))
        return Mem(self.big, M_END - n, M_END)(*shape)

    def vchain(self, e):
        if self._v is None:
            self._v = Chain(e, self.vch)
        return self._v

    def achain(self, e):
        if self._a is None:
            self._a = Chain(e, self.ach)
        return self._a

    def take_groups(self, ends):
        g = self.group
        self.ends += ends
        self.group += len(ends)
        return g

    def slot_free(self, e, g):
        if g >= 2:
            e.wait_ge(self.ps_full, self.ends[g - 2])

    def weights(self, e, g):
        e.wait_ge(self.w_ready[g % 2], 16 * (g // 2 + 1))
        return self.slots[g % 2]

    def load(self, e, g, src, *dst_shape):
        self.slot_free(e, g)
        dst = self.slots[g % 2][:, 0:src.shape[-1]]
        e.dma_start(dst, src).then_inc(self.w_ready[g % 2], 16)

    def bank_free(self, e, f):
        if f >= 8:
            e.wait_ge(self.ps_free, f - 7)


def linear_fm(pg, name, w, ktiles, act, n_tiles, spans, evac, engine, per_group=2, first=None):
    ng = n_tiles // per_group
    f0 = pg.fill
    fills = per_group * len(spans)
    g0 = pg.take_groups([f0 + (g + 1) * fills for g in range(ng)])
    pg.fill += ng * fills
    un = 2 if ng % 2 == 0 and (2 * fills) % 8 == 0 and ng > 2 else ng
    loops = ng // un
    width = ktiles * per_group * P

    assert loops == 1 or f0 > fills

    def run(e, body):
        if loops > 1:
            repeat(e, loops, body)
        else:
            body(0)

    def sync(e):
        pg.slot_free(e, g0)

        def body(i):
            for u in range(un):
                g = g0 + u
                if u or f0 > fills:
                    e.wait_ge(pg.ps_full, f0 + (u - 1) * fills + i * (un * fills))
                src = w[i * un + u] if loops == 1 else w[bass.ds(i * un + u, 1)].rearrange("a p n -> (a p) n")
                e.dma_start(pg.slots[g % 2][:, 0:width], src).then_inc(pg.w_ready[g % 2], 16)
        run(e, body)

    def tensor(e):
        def body(i):
            for u in range(un):
                g = g0 + u
                e.wait_ge(pg.w_ready[g % 2], 16 * (g // 2 + 1) + i * (8 * un))
                slot = pg.slots[g % 2]
                for t in range(per_group):
                    for s, (a, b) in enumerate(spans):
                        f = f0 + (u * per_group + t) * len(spans) + s
                        if f >= 8:
                            e.wait_ge(pg.ps_free, f - 7 + i * (un * fills))
                        for k in range(ktiles):
                            at = (k * per_group + t) * P
                            mm = e.matmul(pg.ps[:, f % 8, 0:b - a], slot[:, at:at + P], act(k, a, b),
                                          start=(k == 0), stop=(k == ktiles - 1))
                        mm.then_inc(pg.ps_full, 1)
        run(e, body)

    def read(e):
        if first:
            first(e)
        if f0:
            e.wait_ge(pg.ps_free, f0)

        def body(i):
            for u in range(un):
                for t in range(per_group):
                    for s, (a, b) in enumerate(spans):
                        f = f0 + (u * per_group + t) * len(spans) + s
                        e.wait_ge(pg.ps_full, f + 1 + i * (un * fills))
                        tile = (i * un + u) * per_group + t
                        evac(e, tile, s, pg.ps[:, f % 8, 0:b - a], (a, b)).then_inc(pg.ps_free, 1)
        run(e, body)

    pg.stage(name=name, sync=sync, tensor=tensor, **{engine: read})


def linear_tm(pg, name, w, act, tiles, cols, evac, engine):
    ng = w.shape[0]
    f0 = pg.fill
    g0 = pg.take_groups([f0 + (g + 1) * len(tiles) for g in range(ng)])
    pg.fill += ng * len(tiles)

    def sync(e):
        for g in range(ng):
            pg.load(e, g0 + g, w[g])

    def tensor(e):
        for g in range(ng):
            slot = pg.weights(e, g0 + g)
            for t, tile in enumerate(tiles):
                f = f0 + g * len(tiles) + t
                pg.bank_free(e, f)
                for k in range(KT):
                    mm = e.matmul(pg.ps[:, f % 8, 0:cols], act(k, tile), slot[:, k * cols:(k + 1) * cols],
                                  start=(k == 0), stop=(k == KT - 1))
                mm.then_inc(pg.ps_full, 1)

    def read(e):
        if f0:
            e.wait_ge(pg.ps_free, f0)
        for g in range(ng):
            for t, tile in enumerate(tiles):
                f = f0 + g * len(tiles) + t
                e.wait_ge(pg.ps_full, f + 1)
                evac(e, g, tile, pg.ps[:, f % 8, 0:cols]).then_inc(pg.ps_free, 1)

    pg.stage(name=name, sync=sync, tensor=tensor, **{engine: read})


MOD_GROUPS = 24
MOD_FIRST = 8


def linear_split(pg, name, w, evac, act=None, first=None):
    (HH, HL), (SH, SL) = pg.h_parts, pg.w_parts
    NG, fills = 4, 4
    f0 = pg.fill
    g0 = pg.take_groups([f0 + fills * (g + 1) for g in range(NG)])
    pg.fill += NG * fills
    high, split = pg.shared_sem("ffn_weights_high", NG), pg.shared_sem("ffn_weights_split", NG)
    act_high, act_split = pg.shared_sem("norm_high", KT if act is not None else 0), pg.shared_sem("act_split", KT if act is not None else 0)
    half = lambda s: slice(s * HALF, (s + 1) * HALF)

    def sync(e):
        for g in range(NG):
            if g < 2:
                pg.slot_free(e, g0 + g)
            else:
                split.wait(e, g - 1)
            e.dma_start(pg.slots[(g0 + g) % 2][:, 0:2048], w[g]).then_inc(pg.w_ready[(g0 + g) % 2], 16)

    def tensor(e):
        for g in range(NG):
            if g == 0 and act is not None:
                act_split.wait(e, KT)
            split.wait(e, g + 1)
            for q in range(fills):
                t, s = divmod(q, 2)
                f = f0 + fills * g + q
                pg.bank_free(e, f)
                bank = pg.ps[:, f % 8, :]
                for k in range(KT):
                    at = (2 * k + t) * P
                    w_hi, w_lo = SH[:, g % 2, at:at + P], SL[:, g % 2, at:at + P]
                    e.matmul(bank, w_hi, HH[:, k, half(s)], start=(k == 0), stop=False)
                    e.matmul(bank, w_hi, HL[:, k, half(s)], start=False, stop=False)
                    mm = e.matmul(bank, w_lo, HH[:, k, half(s)], start=False, stop=(k == KT - 1))
                mm.then_inc(pg.ps_full, 1)

    def scalar(e):
        def weights(g):
            pg.weights(e, g0 + g)
            if g >= 2:
                e.wait_ge(pg.ps_full, f0 + fills * (g - 1))
            e.activation(SH[:, g % 2, :], pg.slots[(g0 + g) % 2][:, 0:2048], ACT.Copy).then_inc(high.sem, 1)

        def tiles(a, b):
            for k in range(a, b):
                e.activation(HH[:, k, :], act[:, k, :], ACT.Copy).then_inc(act_high.sem, 1)
        if act is not None:
            tiles(0, 4)
            act_split.wait(e, 4)
        weights(0)
        if act is not None:
            tiles(4, KT)
        for g in range(1, NG):
            weights(g)

    def vector(e):
        def weights(g):
            high.wait(e, g + 1)
            e.tensor_tensor(SL[:, g % 2, :], pg.slots[(g0 + g) % 2][:, 0:2048], SH[:, g % 2, :].bitcast(F32),
                            ALU.subtract).then_inc(split.sem, 1)

        def tiles(a, b):
            for k in range(a, b):
                act_high.wait(e, k + 1)
                e.tensor_tensor(HL[:, k, :], act[:, k, :], HH[:, k, :].bitcast(F32), ALU.subtract).then_inc(act_split.sem, 1)
        if act is not None:
            tiles(0, 4)
        weights(0)
        if act is not None:
            tiles(4, KT)
        weights(1)
        if first:
            first(e)
        e.wait_ge(pg.ps_free, f0)
        for g in range(NG):
            for q in range(fills):
                t, s = divmod(q, 2)
                f = f0 + fills * g + q
                e.wait_ge(pg.ps_full, f + 1)
                evac(e, 2 * g + t, s, pg.ps[:, f % 8, :], (s * HALF, (s + 1) * HALF)).then_inc(pg.ps_free, 1)
            if g + 2 < NG:
                weights(g + 2)

    pg.stage(name=name, sync=sync, tensor=tensor, scalar=scalar, vector=vector)


def modulation_first(pg):
    ng = MOD_FIRST // 2
    f0 = pg.fill
    pg.fill += ng
    m = Mem(pg.big, M_H, M_W1)
    slots, rows = m(ng, 2 * KT * P), m(2 * ng, D)
    cond = Mem(pg.big, M_END - 4 * D, M_END)(2, D)
    products = Mem(pg.big, M_END - 2 * D, M_END)(2, D)
    loaded = [pg.sem(f"modulation_loaded_{n}") for n in range(ng)]
    cond_loaded, cond_silu, used = pg.sem("conditions_loaded"), pg.sem("conditions_silu"), pg.sem("first_scales")

    def sync(e):
        e.dma_start(cond[:, 0, :], pg.d["cond_rows"][0]).then_inc(cond_loaded, 16)
        e.dma_start(cond[:, 1, :], pg.d["cond_rows"][2]).then_inc(cond_loaded, 16)
        for g in range(ng):
            e.dma_start(slots[:, g, :], pg.d["w_ada"][g]).then_inc(loaded[g], 16)
            e.dma_start(rows[:, 2 * g:2 * g + 2, :], pg.d["w_ada_rest"][g].rearrange("p (b n) -> p b n", b=2)).then_inc(loaded[g], 16)

    def tensor(e):
        e.wait_ge(pg.cond_ready, 1)
        for g in range(ng):
            e.wait_ge(loaded[g], 32)
            for t in range(2):
                for k in range(KT):
                    at = (k * 2 + t) * P
                    mm = e.matmul(pg.ps[:, f0 + g, 2 * t:2 * t + 2], slots[:, g, at:at + P], pg.silu_c[:, k, 0:2],
                                  start=(k == 0), stop=(k == KT - 1))
            mm.then_inc(pg.ps_full, 1)

    def scalar(e):
        e.wait_ge(cond_loaded, 32)
        e.activation(cond, cond, ACT.Silu).then_inc(cond_silu, 1)

    def vector(e):
        bias = pg.param("b_ada")
        e.wait_ge(cond_silu, 1)
        n = 0
        for g in range(ng):
            e.wait_ge(loaded[g], 32)
            for t in range(2):
                for c in range(2):
                    if n >= 2:
                        e.wait_ge(used, n - 1)
                    tile = 2 * ng + 2 * g + t
                    e.tensor_tensor_reduce(products[:, n % 2, :], rows[:, 2 * g + t, :], cond[:, c, :], 1.0, 0.0,
                                           ALU.mult, ALU.add, pg.mod1[:, tile, c:c + 1]).then_inc(used, 1)
                    n += 1
        e.wait_ge(used, n)
        scales = slice(2 * ng, 4 * ng)
        e.tensor_tensor(pg.mod1[:, scales, :], pg.mod1[:, scales, :], bc(bias[:, scales], [P, 2 * ng, 2]), ALU.add)
        for g in range(ng):
            e.wait_ge(pg.ps_full, f0 + g + 1)
            e.tensor_tensor(pg.mod1[:, 2 * g:2 * g + 2, :], pg.ps[:, f0 + g, 0:4].rearrange("p (a b) -> p a b", b=2),
                            bc(bias[:, 2 * g:2 * g + 2], [P, 2, 2]), ALU.add).then_inc(pg.ps_free, 1)

    pg.stage(name="modulation_1", sync=sync, tensor=tensor, scalar=scalar, vector=vector)


def norm(pg, name, src, dst, spans, scale, shift, aux=None, parts=None):
    n = len(spans)
    sq, ms = pg.shared_sem("norm_squares", KT * n), pg.shared_sem("norm_sums", n)
    rt, md = pg.shared_sem("norm_roots", n), pg.shared_sem("norm_scaled", KT * n)
    rs = pg.scratch(n, HALF)
    if parts is not None:
        rs = pg.whole_rs
        high, low = parts
        high_rd = pg.shared_sem("norm_high", KT * n)

    def scalar(e):
        ch = pg.achain(e)
        if aux is not None:
            aux(e)
        for s, w in enumerate(spans):
            for k in range(KT):
                e.activation(dst(s)[:, k, :], src(s)[:, k, :], ACT.Square).then_inc(sq.sem, 1)
        for s, w in enumerate(spans):
            ms.wait(e, s + 1)
            ch(e.activation(rs[:, s, 0:w], pg.ps[:, s, 0:w], ACT.Ln, bias=pg.eps[:, 0:1], scale=1.0 / D))
            e.activation(rs[:, s, 0:w], rs[:, s, 0:w], ACT.Exp, scale=-0.5).then_inc(rt.sem, 1)
        if shift is not None:
            for s, w in enumerate(spans):
                for k in range(KT):
                    md.wait(e, KT * s + k + 1)
                    if parts is None:
                        e.activation(dst(s)[:, k, :], dst(s)[:, k, :], ACT.Identity, bias=shift(s, k))
                    else:
                        e.activation(high[:, k, s * HALF:(s + 1) * HALF], dst(s)[:, k, :], ACT.Identity,
                                     bias=shift(s, k)).then_inc(high_rd.sem, 1)

    def tensor(e):
        for s, w in enumerate(spans):
            for k in range(KT):
                sq.wait(e, KT * s + k + 1)
                mm = e.matmul(pg.ps[:, s, 0:w], pg.ones[:, :], dst(s)[:, k, :], start=(k == 0), stop=(k == KT - 1))
            mm.then_inc(ms.sem, 1)

    def vector(e):
        ch = pg.vchain(e)
        if aux is not None:
            aux(e)
        for s, w in enumerate(spans):
            rt.wait(e, s + 1)
            for k in range(KT):
                e.scalar_tensor_tensor(out=dst(s)[:, k, :], in0=src(s)[:, k, :], scalar=scale(s, k), in1=rs[:, s, 0:w],
                                       op0=ALU.mult, op1=ALU.mult).then_inc(md.sem, 1)
        if parts is not None:
            for s, w in enumerate(spans):
                for k in range(KT):
                    high_rd.wait(e, KT * s + k + 1)
                    half = slice(s * HALF, (s + 1) * HALF)
                    e.scalar_tensor_tensor(out=low[:, k, half], in0=dst(s)[:, k, :], scalar=shift(s, k),
                                           in1=high[:, k, half].bitcast(F32), op0=ALU.add, op1=ALU.subtract)

    pg.stage(name=name, scalar=scalar, tensor=tensor, vector=vector)


def setup(pg):
    pg.cond_ready = pg.sem("cond_ready")
    const = pg.sem("constants_set")
    pg.x_loaded = pg.sem("x_loaded")
    pg.ctx_raw = Mem(pg.big, M_W1, M_END)(KT, TC)

    def pool(e):
        e.dma_start(pg.pp, pg.d["params"]).then_inc(pg.loaded, 16)
        e.dma_start(pg.ident, pg.d["ident"]).then_inc(pg.loaded, 16)
        e.dma_start(pg.ctx_raw, pg.d["ctx_t"]).then_inc(pg.x_loaded, 16)
        e.dma_start(pg.x, pg.d["x_t"]).then_inc(pg.x_loaded, 16)

    def vector(e):
        ch = pg.vchain(e)
        e.memset(pg.ones, 1.0)
        ch(e.memset(pg.eps, EPS))
        e.wait_ge(pg.loaded, 32)

    def scalar(e):
        e.wait_ge(pg.loaded, 32)
        e.activation(pg.silu_c, pg.param("cond").rearrange("p (k c) -> p k c", c=3), ACT.Silu).then_inc(pg.cond_ready, 1)

    def tensor(e):
        e.wait_ge(pg.loaded, 32)

    pg.stage(name="setup", gpsimd=pool, vector=vector, scalar=scalar, tensor=tensor)
    modulation_first(pg)
    pg.lb = pg.perm_left(8)
    pg.one_minus_lb = pg.perm_left(8)
    e0, mx = pg.perm_left(8), pg.perm_left(8)
    ea = pg.perm_left(8)
    lb_exp = pg.sem("bound_exps")

    terms = pg.sem("bound_terms")

    def scalar2(e):
        e.wait_ge(terms, 1)
        e.activation(e0, e0, ACT.Exp).then_inc(lb_exp, 1)
        e.activation(ea, ea, ACT.Exp).then_inc(lb_exp, 1)

    def vector2(e):
        ch = pg.vchain(e)
        for j in range(2):
            e.scalar_tensor_tensor(out=pg.sc_mix[:, :, j], in0=pg.mod1[:, 8:16, j], scalar=1.0,
                                   in1=pg.param("norm_mix"), op0=ALU.add, op1=ALU.mult)
        lb = pg.param("lb")
        for d in range(2):
            l0, l1 = lb[:, 8 * d:8 * d + 4], lb[:, 8 * d + 4:8 * d + 8]
            o = slice(4 * d, 4 * d + 4)
            ch(e.tensor_tensor(mx[:, o], l0, l1, ALU.max))
            ch(e.tensor_tensor(e0[:, o], l0, mx[:, o], ALU.subtract))
            ins = e.tensor_tensor(ea[:, o], l1, mx[:, o], ALU.subtract)
            if d == 0:
                ch(ins)
            else:
                ins.then_inc(terms, 1)
        e.wait_ge(lb_exp, 2)
        ch(e.tensor_tensor(mx, e0, ea, ALU.add))
        ch(e.reciprocal(mx, mx))
        ch(e.tensor_tensor(pg.lb, e0, mx, ALU.mult))
        ch(e.tensor_tensor(pg.one_minus_lb, ea, mx, ALU.mult))

    pg.stage(name="bounds", vector=vector2, scalar=scalar2)

    def wait_x(e):
        e.wait_ge(pg.x_loaded, 32)

    h1, x = pg.h1, pg.x
    norm(pg, "norm_mix",
         lambda s: pg.ctx_raw if s == 0 else x[:, :, (s - 1) * HALF:s * HALF],
         lambda s: h1[:, :, 0:TC] if s == 0 else h1[:, :, TC + (s - 1) * HALF:TC + s * HALF],
         [TC, HALF, HALF],
         lambda s, k: pg.sc_mix[:, k, (1 if s == 0 else 0):(2 if s == 0 else 1)],
         lambda s, k: pg.mod1[:, k, (1 if s == 0 else 0):(2 if s == 0 else 1)], aux=wait_x)


LAT = [(TC, TC + HALF), (TC + HALF, TA)]
ALL = [(0, TC)] + LAT


def modulation_rest(pg, part):
    n_part = (MOD_GROUPS - MOD_FIRST) // 2
    slots = (pg.spare, Mem(pg.big, 46720, 49664)(2, D))
    row = Mem(pg.big, 51200, M_END)(D)
    products = Mem(pg.big, M_X, M_H)(D)
    ready = [pg.shared_sem(f"modulation_ready_{n}", 16 * n_part // 2) for n in range(2)]
    used = pg.shared_sem("modulation_used", 2 * n_part)
    if part == 0:
        row_loaded, row_ready = pg.shared_sem("condition_loaded", 16), pg.shared_sem("condition_silu", 1)
    k_at = len(pg.stages) - 1

    def pool(e):
        e.wait_ge(pg.stage_done, 3 * k_at)
        if part == 0:
            e.dma_start(row, pg.d["cond_rows"][0]).then_inc(row_loaded.sem, 16)
        for n in range(n_part):
            if n >= 2:
                used.wait(e, 2 * (n - 1))
            e.dma_start(slots[n % 2], pg.d["w_ada_rest"][MOD_FIRST // 2 + n_part * part + n].rearrange("p (b n) -> p b n", b=2)).then_inc(
                ready[n % 2].sem, 16)

    def scalar(e):
        row_loaded.wait(e, 16)
        e.activation(row, row, ACT.Silu).then_inc(row_ready.sem, 1)

    def vector(e):
        if part == 0:
            row_ready.wait(e, 1)
        for n in range(n_part):
            ready[n % 2].wait(e, 16 * (n // 2 + 1))
            for t in range(2):
                tile = 2 * (MOD_FIRST + n_part * part + n) + t
                if n or t:
                    used.wait(e, 2 * n + t)
                e.tensor_tensor_reduce(products, slots[n % 2][:, t, :], row, 1.0, 0.0, ALU.mult, ALU.add,
                                       pg.mod1[:, tile, 0:1]).then_inc(used.sem, 1)

    return pool, scalar, vector


def window_attention(pg):
    m = Mem(pg.big, M_W1, M_END)
    kk, vv, q = m(TA), m(TA // P, P), m(4, T)
    cs, sn = m(T), m(T)
    mask = m(3, 640)
    rot, blk = m(P), m(P)
    stat = m(8, 64)
    mx_ = Mem(pg.big, M_X, M_H)
    S = mx_(4, 640)
    PT = mx_(2, 5, HALF)
    tmp = Mem(pg.big, M_YHG, M_W1)
    sq, rr, t1 = tmp(TA), tmp(TA), tmp(T)
    yat = Mem(pg.big, M_YAT, M_YHG)(4, T)
    pg.yat = yat
    h1 = pg.h1
    consts = pg.sem("attention_tables_loaded")
    k_at = len(pg.stages)

    def q_out(e, tile, s, bank, ab):
        return e.activation(q[:, tile, s * HALF:(s + 1) * HALF], bank, ACT.Copy)
    linear_fm(pg, "attention_q", pg.d["w_q"], KT, lambda k, a, b: h1[:, k, a:b], 4, LAT, q_out, "scalar")
    beside = modulation_rest(pg, 0)
    pg.stages[-1].update(gpsimd=beside[0], vector=beside[2], scalar=in_turn(beside[1], pg.stages[-1]["scalar"]))

    def k_out(e, tile, s, bank, ab):
        return e.activation(kk[:, ab[0]:ab[1]], bank, ACT.Copy)
    linear_fm(pg, "attention_k", pg.d["w_k"], KT, lambda k, a, b: h1[:, k, a:b], 1, ALL, k_out, "scalar", per_group=1)

    def v_out(e, g, tile, bank):
        return e.tensor_copy(vv[:, tile, :], bank)
    linear_tm(pg, "attention_v", pg.d["w_v"], lambda k, t: h1[:, k, t * P:(t + 1) * P], list(range(TA // P)), P,
              v_out, "vector")

    squares, sums, roots, scaled, turned = (pg.sem(f"qk_{n}") for n in ("squares", "sums", "roots", "scaled", "turned"))
    tiles = [(q[:, j, :], LAT, "q_norm") for j in range(4)] + [(kk, ALL, "k_norm")]

    def spans_of(t):
        return [(a - TC, b - TC) for a, b in LAT] if t < 4 else ALL

    def lat_of(t):
        return tiles[t][0] if t < 4 else kk[:, TC:TA]

    def pool(e):
        e.wait_ge(pg.stage_done, 3 * k_at)
        e.dma_start(cs, pg.d["rope_cos"]).then_inc(consts, 16)
        e.dma_start(sn, pg.d["rope_sin"]).then_inc(consts, 16)
        e.dma_start(mask, pg.d["window_masks"]).then_inc(consts, 16)
        e.dma_start(rot, pg.d["rope_turn"]).then_inc(consts, 16)
        e.dma_start(blk, pg.d["ones_64"]).then_inc(consts, 16)

    def p_scalar(e):
        for t, (v, _, _) in enumerate(tiles):
            n = T if t < 4 else TA
            if t:
                e.wait_ge(sums, t)
            e.activation(sq[:, 0:n], v, ACT.Square).then_inc(squares, 1)
            e.wait_ge(sums, t + 1)
            if t:
                e.wait_ge(scaled, t)
            for s, (a, b) in enumerate(spans_of(t)):
                last = e.activation(rr[:, a:b], pg.ps[:, s, 0:b - a], ACT.Ln, bias=pg.eps[:, 0:1], scale=1.0 / 64)
            pg.achain(e)(last)
            e.activation(rr[:, 0:n], rr[:, 0:n], ACT.Exp, scale=-0.5).then_inc(roots, 1)

    def p_tensor(e):
        e.wait_ge(consts, 80)
        for t in range(5):
            e.wait_ge(squares, t + 1)
            if t:
                e.wait_ge(roots, t)
            for s, (a, b) in enumerate(spans_of(t)):
                mm = e.matmul(pg.ps[:, s, 0:b - a], blk, sq[:, a:b], start=True, stop=True)
            mm.then_inc(sums, 1)
            e.wait_ge(scaled, t + 1)
            for s in range(2):
                mm = e.matmul(pg.ps[:, 4 + s, :], rot, lat_of(t)[:, s * HALF:(s + 1) * HALF], start=True, stop=True)
            mm.then_inc(turned, 1)

    def p_vector(e):
        ch = pg.vchain(e)
        e.wait_ge(consts, 80)
        ch(e.tensor_scalar(stat[:, 0, 0:1], pg.col("q_norm"), 0.125, None, ALU.mult))
        for t, (v, _, w) in enumerate(tiles):
            n = T if t < 4 else TA
            e.wait_ge(roots, t + 1)
            e.scalar_tensor_tensor(out=v, in0=v, scalar=stat[:, 0, 0:1] if t < 4 else pg.col("k_norm"),
                                   in1=rr[:, 0:n], op0=ALU.mult, op1=ALU.mult).then_inc(scaled, 1)
            e.wait_ge(turned, t + 1)
            ch(e.tensor_tensor(t1, pg.ps[:, 4:6, :].rearrange("p a b -> p (a b)"), sn, ALU.mult))
            ch(e.tensor_tensor(lat_of(t), lat_of(t), cs, ALU.mult))
            ch(e.tensor_tensor(lat_of(t), lat_of(t), t1, ALU.add))

    pg.stage(name="attention_rotate", gpsimd=pool, scalar=p_scalar, tensor=p_tensor, vector=p_vector)

    NB = T // P
    N = NB * 8
    sc, sm, ex, pr, tr, pt, pv, yo = (pg.sem(f"attention_{n}") for n in (
        "scores", "maxima", "exps", "probs", "turns", "turned", "outputs", "stored"))
    mx, nm, rs, es, dn, ri = (stat[:, i, :] for i in range(1, 7))

    def where(i):
        n, r = divmod(i, 8)
        g, j = divmod(r, 4)
        return n, g, j

    def blocks(n):
        return [max(n - 1, 0), n, min(n + 1, NB - 1)]

    def tensor(e):
        def scores(i):
            n, g, j = where(i)
            rows = slice(64 * g, 64 * g + 64)
            if i >= 2:
                e.wait_ge(sm, i - 1)
            c0 = 2 * (i % 2)
            qq = q[rows, j, n * P:(n + 1) * P]
            e.matmul(pg.ps[:, c0, 0:TC], qq, kk[rows, 0:TC], start=True, stop=True)
            for b, kb in enumerate(blocks(n)):
                at = TC + b * P
                mm = e.matmul(pg.ps[:, c0 + at // HALF, at % HALF:at % HALF + P], qq,
                              kk[rows, TC + kb * P:TC + (kb + 1) * P], start=True, stop=True)
            mm.then_inc(sc, 1)

        def turn(i):
            e.wait_ge(pr, i + 1)
            if i:
                e.wait_ge(pt, i)
            for b in range(5):
                mm = e.transpose(pg.ps[:, 4 + b // 4, (b % 4) * P:(b % 4 + 1) * P], S[:, i % 4, b * P:(b + 1) * P],
                                 pg.ident)
            mm.then_inc(tr, 1)

        def values(u):
            n, g, _ = where(4 * u)
            e.wait_ge(pt, 4 * u + 4)
            if u >= 2:
                e.wait_ge(yo, u - 1)
            for b, kt in enumerate([0, 1] + [2 + kb for kb in blocks(n)]):
                mm = e.matmul(pg.ps[64 * g:64 * g + 64, 6 + u % 2, :], vv[:, kt, 64 * g:64 * g + 64], PT[:, u % 2, b, :],
                              start=(b == 0), stop=(b == 4))
            mm.then_inc(pv, 1)

        for i in range(N + 3):
            if i < N:
                scores(i)
            if 2 <= i < N + 2:
                turn(i - 2)
            if i >= 3 and (i - 3) % 4 == 3:
                values((i - 3) // 4)

    def vector(e):
        ch = pg.vchain(e)
        for i in range(N + 1):
            if i < N:
                n, g, j = where(i)
                h = 4 * g + j
                e.wait_ge(sc, i + 1)
                if i >= 4:
                    e.wait_ge(tr, i - 3)
                kind = 1 if n == 0 else 2 if n == NB - 1 else 0
                ch(e.tensor_tensor_reduce(S[:, i % 4, :], pg.ps[:, 2 * (i % 2):2 * (i % 2) + 2, :]
                                          .rearrange("p a b -> p (a b)")[:, 0:640], mask[:, kind, :], 1.0, -BIG,
                                          ALU.add, ALU.max, mx[:, i:i + 1]))
                e.tensor_scalar(nm[:, i:i + 1], mx[:, i:i + 1], pg.col("sink", h), -1.0, ALU.max,
                                ALU.mult).then_inc(sm, 1)
            if i >= 1:
                r = i - 1
                e.wait_ge(ex, r + 1)
                ch(e.tensor_tensor(dn[:, r:r + 1], rs[:, r:r + 1], es[:, r:r + 1], ALU.add))
                ch(e.reciprocal(ri[:, r:r + 1], dn[:, r:r + 1]))
                e.tensor_scalar(S[:, r % 4, :], S[:, r % 4, :], ri[:, r:r + 1], None, ALU.mult).then_inc(pr, 1)

    def scalar(e):
        for i in range(N + 4):
            if i < N:
                n, g, j = where(i)
                h = 4 * g + j
                e.wait_ge(sm, i + 1)
                e.activation(S[:, i % 4, :], S[:, i % 4, :], ACT.Exp, bias=nm[:, i:i + 1], accum_out=rs[:, i:i + 1])
                e.activation(es[:, i:i + 1], pg.col("sink", h), ACT.Exp, bias=nm[:, i:i + 1]).then_inc(ex, 1)
            if 2 <= i < N + 2:
                r = i - 2
                u, j = divmod(r, 4)
                e.wait_ge(tr, r + 1)
                if u >= 2 and j == 0:
                    e.wait_ge(pv, u - 1)
                e.activation(PT[:, u % 2, :, j * P:(j + 1) * P], pg.ps[:, 4:6, :].rearrange("p a (b c) -> p (a b) c", c=P)
                             [:, 0:5, :], ACT.Copy).then_inc(pt, 1)
            if i >= 4 and (i - 4) % 4 == 3:
                u = (i - 4) // 4
                n, g, _ = where(4 * u)
                e.wait_ge(pv, u + 1)
                e.activation(yat[64 * g:64 * g + 64, :, n * P:(n + 1) * P],
                             pg.ps[64 * g:64 * g + 64, 6 + u % 2, :].rearrange("p (a b) -> p a b", b=P),
                             ACT.Copy).then_inc(yo, 1)

    pg.stage(name="attention", tensor=tensor, vector=vector, scalar=scalar)


def hgrn(pg):
    C = 32
    NC = TA // C
    NT = TA // P
    HEADS = 4
    m = Mem(pg.big, M_W1, M_END)
    V = m(NT, 4 * P)
    B, Cn = m(2, TA), m(2, TA)
    Q, G = m(2, T), m(2, T)
    tri = m(2, P).bitcast(I32)
    reset = m(TA)
    sq = m(T)
    dec = m(2, NC)
    m = Mem(pg.big, M_X, M_H)
    A = m(4, TA)
    S = m(16, P)
    KT_ = m(4, P)
    SM = m(4, P)
    yhg = Mem(pg.big, M_YHG, M_W1)(HEADS, T)
    pg.yhg = yhg
    h1 = pg.h1
    k_at = len(pg.stages)
    tables = pg.sem("hgrn_tables_loaded")

    def v_out(e, g, tile, bank):
        return e.activation(V[:, tile, 256 * g:256 * g + 256], bank, ACT.Copy)
    linear_tm(pg, "hgrn_values", pg.d["w_inp"], lambda k, t: h1[:, k, t * P:(t + 1) * P], list(range(NT)), 256,
              v_out, "scalar")
    beside = modulation_rest(pg, 1)
    pg.stages[-1].update(gpsimd=beside[0], vector=beside[2])

    f0 = pg.fill
    spans = [[(0, a, b) for a, b in ALL] + [(1, a, b) for a, b in ALL], [(0, a, b) for a, b in LAT] + [(1, a, b) for a, b in LAT]]
    gates, others = [(0, v) for v in spans[0]], [(1, v) for v in spans[1]]
    fills = gates + others
    FH, FG = len(fills), len(gates)
    g0 = pg.take_groups([f0 + FH * h + n for h in range(HEADS) for n in (FG, FH)])
    pg.fill += FH * HEADS
    (f_rd, l_rd, c_rd, n_rd, e_rd, q_rd, t_rd, k_cp, u_rd, s_rd, sc_rd, sm_rd, o_rd, o_cp, r_sq, r_sm, r_rt,
     done) = (pg.sem(f"hgrn_{n}") for n in (
         "gates", "logs", "cums", "inverse_exps", "exps", "operands", "turned", "keys", "updates", "states",
         "scores", "masked", "outputs", "summed", "squares", "square_sums", "roots", "head_done"))

    AHEAD = FH + 4

    def bank_of(h, n):
        if FH * h + n < AHEAD:
            return (f0 + FH * h + n) % 8
        return 7 if n < FG else 2 + n - FG

    def beside(h):
        todo = range(AHEAD - FH if h == 0 else 0, FG)
        return {3 * i + 2: n for i, n in enumerate(todo)}

    def tile_of(k, d):
        return k if d == 0 else ([1, 0] + list(range(NT - 1, 1, -1)))[k]

    def pool(e):
        e.wait_ge(pg.stage_done, 3 * k_at)
        e.dma_start(tri, pg.d["tri_32"]).then_inc(tables, 16)
        e.dma_start(reset, pg.d["reset_32"]).then_inc(tables, 16)

    def sync(e):
        for g in range(2 * HEADS):
            pg.load(e, g0 + g, pg.d["w_hgrn"][g])

    def tensor(e):
        def project(h, which):
            for n in which:
                part, (t, a, b) = fills[n]
                f = f0 + FH * h + n
                if f < f0 + AHEAD:
                    pg.bank_free(e, f)
                elif n < FG:
                    e.wait_ge(pg.ps_free, f)
                elif n == FG:
                    e.wait_ge(s_rd, 20 * h)
                    e.wait_ge(sm_rd, 16 * h)
                slot = pg.weights(e, g0 + 2 * h + part)
                for k in range(KT):
                    mm = e.matmul(pg.ps[:, bank_of(h, n), 0:b - a], slot[:, (2 * k + t) * P:(2 * k + t + 1) * P],
                                  h1[:, k, a:b], start=(k == 0), stop=(k == KT - 1))
                mm.then_inc(pg.ps_full, 1)

        def chunks(h):
            e.wait_ge(pg.ps_free, f0 + max(FH * (h + 1), AHEAD))
            e.wait_ge(q_rd, 2 * h + 2)
            for s in range(2 * NT + 2):
                if s < 2 * NT:
                    k, d = divmod(s, 2)
                    t = tile_of(k, d)
                    if h or s:
                        e.wait_ge(k_cp, 20 * h + s)
                    e.transpose(pg.ps[:, 4, 0:P], A[:, 2 * (h % 2) + d, t * P:(t + 1) * P], pg.ident).then_inc(t_rd, 1)
                if 1 <= s <= 2 * NT:
                    u = s - 1
                    k, d = divmod(u, 2)
                    t = tile_of(k, d)
                    E = 20 * h + u
                    e.wait_ge(k_cp, E + 1)
                    if E:
                        e.wait_ge(s_rd, E)
                    for c in range(4):
                        r = slice(C * c, C * c + C)
                        mm = e.matmul(pg.ps[:, c, 0:P], KT_[r, E % 4, :], V[r, t, h * P:(h + 1) * P], start=True, stop=True)
                    mm.then_inc(u_rd, 1)
                    if k >= 2:
                        L = 16 * h + u - 4
                        if L:
                            e.wait_ge(sm_rd, L)
                        e.matmul(pg.ps[:, 5, 0:P], Cn[:, d, t * P:(t + 1) * P], B[:, d, t * P:(t + 1) * P],
                                 start=True, stop=True).then_inc(sc_rd, 1)
                if s >= 2:
                    u = s - 2
                    k, d = divmod(u, 2)
                    t = tile_of(k, d)
                    if k >= 2:
                        L = 16 * h + u - 4
                        e.wait_ge(sm_rd, L + 1)
                        e.wait_ge(s_rd, 20 * h + u + 1)
                        if L:
                            e.wait_ge(o_cp, L)
                        bank = pg.ps[:, 6, 0:P]
                        e.matmul(bank, V[:, t, h * P:(h + 1) * P], SM[:, L % 4, :], start=True, stop=False)
                        for n in range(4):
                            c = n if d == 0 else 3 - n
                            mm = e.matmul(bank[:, C * c:C * c + C], S[:, 8 * d + (4 * k + n) % 8, :],
                                          B[:, d, t * P + C * c:t * P + C * c + C], start=False, stop=(n == 3))
                        mm.then_inc(o_rd, 1)
                if h + 1 < HEADS and s in beside(h):
                    project(h + 1, [beside(h)[s]])
            if h + 1 < HEADS:
                project(h + 1, [FG])
            e.wait_ge(r_sq, h + 1)
            for s in range(2):
                mm = e.matmul(pg.ps[:, s, :], pg.ones, sq[:, s * HALF:(s + 1) * HALF], start=True, stop=True)
            mm.then_inc(r_sm, 1)
            if h + 1 < HEADS:
                project(h + 1, range(FG + 1, FH))

        project(0, range(FH))
        project(1, range(AHEAD - FH))
        for h in range(HEADS):
            chunks(h)

    def scalar(e):
        if f0:
            e.wait_ge(pg.ps_free, f0)

        def store(h, which):
            for n in which:
                part, (t, a, b) = fills[n]
                if h >= 2 and n == 0:
                    e.wait_ge(done, h - 1)
                e.wait_ge(pg.ps_full, f0 + FH * h + n + 1)
                bank = pg.ps[:, bank_of(h, n), 0:b - a]
                if part == 0:
                    ins = e.activation(A[:, 2 * (h % 2) + t, a:b], bank, ACT.Sigmoid)
                else:
                    ins = e.activation((Q, G)[t][:, h % 2, a - TC:b - TC], bank, ACT.Silu)
                ins.then_inc(pg.ps_free, 1)

        store(0, range(FH))
        for h in range(HEADS):
            if h:
                store(h, [FG + 1])
            for d in range(2):
                e.wait_ge(f_rd, 2 * h + d + 1)
                e.activation(B[:, d, :], A[:, 2 * (h % 2) + d, :], ACT.Ln).then_inc(l_rd, 1)
            for d in range(2):
                e.wait_ge(c_rd, 2 * h + d + 1)
                e.activation(Cn[:, d, :], B[:, d, :], ACT.Exp, scale=-1.0).then_inc(n_rd, 1)
                e.activation(B[:, d, :], B[:, d, :], ACT.Exp).then_inc(e_rd, 1)
            if h:
                store(h, range(FG + 2, FH))
            else:
                store(1, range(AHEAD - FH))
            for s in range(2 * NT):
                E = 20 * h + s
                e.wait_ge(t_rd, E + 1)
                if E >= 4:
                    e.wait_ge(u_rd, E - 3)
                e.activation(KT_[:, E % 4, :], pg.ps[:, 4, 0:P], ACT.Copy).then_inc(k_cp, 1)
                if h + 1 < HEADS and s - 1 in beside(h):
                    store(h + 1, [beside(h)[s - 1]])
            e.wait_ge(o_cp, 16 * (h + 1))
            e.activation(sq, yhg[:, h, :], ACT.Square).then_inc(r_sq, 1)
            if h + 1 < HEADS:
                store(h + 1, [FG])
            e.wait_ge(r_sm, h + 1)
            pg.achain(e)(e.activation(sq, pg.ps[:, 0:2, :].rearrange("p a b -> p (a b)"), ACT.Ln, bias=pg.eps[:, 0:1],
                                      scale=1.0 / P))
            e.activation(sq, sq, ACT.Exp, scale=-0.5).then_inc(r_rt, 1)

    def vector(e):
        ch = pg.vchain(e)
        e.wait_ge(tables, 32)
        ch(e.memset(SM, 0.0))
        for h in range(HEADS):
            a = [A[:, 2 * (h % 2) + d, :] for d in range(2)]
            e.wait_ge(pg.ps_free, f0 + FH * h + FG)
            for d in range(2):
                i = 4 * d + h
                e.tensor_scalar(a[d], a[d], pg.one_minus_lb[:, i:i + 1], pg.lb[:, i:i + 1], ALU.mult,
                                ALU.add).then_inc(f_rd, 1)
            for d in range(2):
                e.wait_ge(l_rd, 2 * h + d + 1)
                e.wait_ge(f_rd, 2 * h + d + 1)
                b = B[:, d, :] if d == 0 else B[:, d, ::-1]
                e.tensor_tensor_scan(b, reset, b, 0.0, ALU.mult, ALU.add).then_inc(c_rd, 1)
                ch(e.tensor_scalar(a[d], a[d], -1.0, 1.0, ALU.mult, ALU.add))
            for d in range(2):
                e.wait_ge(n_rd, 2 * h + d + 1)
                ch(e.tensor_tensor(Cn[:, d, :], a[d], Cn[:, d, :], ALU.mult))
                e.wait_ge(e_rd, 2 * h + d + 1)
                end = C - 1 if d == 0 else 0
                ch(e.tensor_copy(dec[:, d, :], B[:, d, :].rearrange("p (n c) -> p n c", c=C)[:, :, end]))
                e.tensor_tensor(a[d].rearrange("p (n c) -> p n c", c=C), Cn[:, d, :].rearrange("p (n c) -> p n c", c=C),
                                bc(dec[:, d, :], [P, NC, C]), ALU.mult)
                e.wait_ge(pg.ps_free, f0 + FH * h + FG + 2)
                e.scalar_tensor_tensor(out=B[:, d, TC:TA], in0=Q[:, h % 2, :], scalar=float(P) ** -0.5,
                                       in1=B[:, d, TC:TA], op0=ALU.mult, op1=ALU.mult).then_inc(q_rd, 1)
            for d in range(2):
                ch(e.memset(S[:, 8 * d, :], 0.0))
            for s in range(2 * NT + 1):
                if s < 2 * NT:
                    k, d = divmod(s, 2)
                    E = 20 * h + s
                    t = tile_of(k, d)
                    e.wait_ge(u_rd, E + 1)
                    if k >= 4:
                        e.wait_ge(o_rd, 16 * h + 2 * (k - 2) + d - 4 + 1)
                    if E:
                        e.wait_ge(s_rd, E)
                    for n in range(4):
                        c = n if d == 0 else 3 - n
                        q = 4 * k + n
                        ins = e.scalar_tensor_tensor(
                            out=S[:, 8 * d + (q + 1) % 8, :], in0=S[:, 8 * d + q % 8, :],
                            scalar=dec[:, d, 4 * t + c:4 * t + c + 1], in1=pg.ps[:, c, 0:P], op0=ALU.mult, op1=ALU.add)
                        if n < 3:
                            ch(ins)
                        else:
                            ins.then_inc(s_rd, 1)
                    if k >= 2:
                        L = 16 * h + s - 4
                        e.wait_ge(sc_rd, L + 1)
                        if L >= 4:
                            e.wait_ge(o_rd, L - 3)
                        e.copy_predicated(SM[:, L % 4, :], tri[:, d, :], pg.ps[:, 5, 0:P]).then_inc(sm_rd, 1)
                if s >= 5:
                    k, d = divmod(s - 1, 2)
                    L = 16 * h + s - 5
                    t = tile_of(k, d) - 2
                    e.wait_ge(o_rd, L + 1)
                    o = yhg[:, h, t * P:(t + 1) * P]
                    bank = pg.ps[:, 6, 0:P]
                    if k < 6:
                        e.tensor_copy(o, bank).then_inc(o_cp, 1)
                    else:
                        e.wait_ge(o_cp, L)
                        e.tensor_tensor(o, o, bank, ALU.add).then_inc(o_cp, 1)
            e.wait_ge(r_rt, h + 1)
            ch(e.scalar_tensor_tensor(out=yhg[:, h, :], in0=yhg[:, h, :], scalar=pg.col("hg_norm"), in1=sq,
                                      op0=ALU.mult, op1=ALU.mult))
            e.tensor_tensor(yhg[:, h, :], yhg[:, h, :], G[:, h % 2, :], ALU.mult).then_inc(done, 1)
            e.wait_ge(done, h + 1)

    pg.stage(name="hgrn", gpsimd=pool, sync=sync, tensor=tensor, scalar=scalar, vector=vector)


def merge(pg):
    sg = Mem(pg.big, M_X, M_H)(4, HALF)
    mixed_high, mixed_low = pg.h_parts
    h1, yat, yhg, x = pg.h1, pg.yat, pg.yhg, pg.x
    again = pg.sem("x_loaded_again")
    gates, half = pg.sem("merge_gates"), pg.sem("merge_mixed")
    summed, high = pg.sem("merge_summed"), pg.sem("merge_high")
    f0 = pg.fill
    g0 = pg.take_groups([f0 + 8 * (n + 1) for n in range(KT)])
    pg.fill += 8 * KT
    w = pg.d["w_merge"]

    def tile_of(v, i, u, s):
        return v[:, bass.ds(2 * i + u, 1), s * HALF:(s + 1) * HALF].rearrange("p a b -> p (a b)")

    def sync(e):
        pg.slot_free(e, g0)

        def body(i):
            for u in range(2):
                g = g0 + u
                e.wait_ge(pg.ps_full, f0 + 8 * (u - 1) + 16 * i)
                e.dma_start(pg.slots[g % 2], w[bass.ds(2 * i + u, 1)].rearrange("a p n -> (a p) n")).then_inc(
                    pg.w_ready[g % 2], 16)
        repeat(e, KT // 2, body)

    def tensor(e):
        def body(i):
            for u in range(2):
                g = g0 + u
                e.wait_ge(pg.w_ready[g % 2], 16 * (g // 2 + 1) + i * 16)
                slot = pg.slots[g % 2]
                for s in range(2):
                    a = s * HALF
                    for part, (lo, n, act) in enumerate((
                            (16, KT, lambda k: h1[:, k, TC + a:TC + a + HALF]), (8, KT, lambda k: h1[:, k, TC + a:TC + a + HALF]),
                            (0, 4, lambda k: yhg[:, k, a:a + HALF]), (4, 4, lambda k: yat[:, k, a:a + HALF]))):
                        f = f0 + 8 * u + 4 * s + part
                        e.wait_ge(pg.ps_free, f - 7 + i * 16)
                        for k in range(n):
                            mm = e.matmul(pg.ps[:, f % 8, :], slot[:, (lo + k) * P:(lo + k + 1) * P], act(k),
                                          start=(k == 0), stop=(k == n - 1))
                        mm.then_inc(pg.ps_full, 1)
        repeat(e, KT // 2, body)

    def scalar(e):
        def body(i):
            for u in range(2):
                for s in range(2):
                    for part in range(2):
                        f = f0 + 8 * u + 4 * s + part
                        e.wait_ge(pg.ps_full, f + 1 + i * 16)
                        if part == 0:
                            e.wait_ge(half, 2 * u + s + 1 + i * 4)
                        e.activation(sg[:, 2 * (s % 2) + part, :], pg.ps[:, f % 8, :], ACT.Sigmoid).then_inc(gates, 1)
                    e.wait_ge(summed, 2 * u + s + 1 + i * 4)
                    e.activation(tile_of(mixed_high, i, u, s), sg[:, 2 * s, :], ACT.Copy).then_inc(high, 1)
        repeat(e, KT // 2, body)

    def vector(e):
        e.wait_ge(pg.ps_free, f0)
        e.sem_inc(half, 2)
        rest = slice(2 * MOD_FIRST, 2 * MOD_GROUPS)
        pg.vchain(e)(e.tensor_tensor(pg.mod1[:, rest, 0], pg.mod1[:, rest, 0], pg.param("b_ada")[:, rest], ALU.add))
        e.scalar_tensor_tensor(out=pg.sc_ffn, in0=pg.mod1[:, 32:40, 0], scalar=1.0,
                               in1=pg.param("norm_ffn"), op0=ALU.add, op1=ALU.mult)

        def body(i):
            for u in range(2):
                for s in range(2):
                    f = f0 + 8 * u + 4 * s
                    st = 2 * u + s
                    e.wait_ge(gates, 2 * st + 2 + i * 8)
                    e.wait_ge(pg.ps_full, f + 4 + i * 16)
                    e.tensor_tensor(sg[:, 2 * s, :], sg[:, 2 * s, :], pg.ps[:, (f + 3) % 8, :], ALU.mult).then_inc(part_a, 1)
                    e.tensor_tensor(sg[:, 2 * s + 1, :], sg[:, 2 * s + 1, :], pg.ps[:, (f + 2) % 8, :], ALU.mult).then_inc(
                        pg.ps_free, 4)
                    e.wait_ge(part_a, st + 1 + i * 4)
                    e.wait_ge(pg.ps_free, f + 4 + i * 16)
                    e.tensor_tensor(sg[:, 2 * s, :], sg[:, 2 * s, :], sg[:, 2 * s + 1, :], ALU.add).then_inc(summed, 1)
                    e.wait_ge(high, st + 1 + i * 4)
                    e.tensor_tensor(tile_of(mixed_low, i, u, s), sg[:, 2 * s, :], tile_of(mixed_high, i, u, s).bitcast(F32),
                                    ALU.subtract).then_inc(half, 1)
        repeat(e, KT // 2, body)

    part_a = pg.sem("merge_products")
    pg.stage(name="merge", sync=sync, tensor=tensor, scalar=scalar, vector=vector)

    def out(e, tile, s, bank, ab):
        xs = x[:, tile, ab[0]:ab[1]]
        return e.scalar_tensor_tensor(out=xs, in0=bank, scalar=pg.mod1[:, 16 + tile, 0:1], in1=xs,
                                      op0=ALU.mult, op1=ALU.add)
    k_at = len(pg.stages)

    def pool(e):
        e.wait_ge(pg.stage_done, 3 * k_at)
        e.dma_start(x, pg.d["x_t"]).then_inc(again, 16)

    linear_split(pg, "merge_out", pg.d["w_out1"], out, first=lambda e: e.wait_ge(again, 16))
    pg.stages[-1]["gpsimd"] = pool


def ffn(pg, name, w_gu, w_down, gate, mod=None):
    steps = [("G", 0), ("G", 1)]
    for n in range(FT // 2 - 1):
        steps += [("G", 2 * n + 2), ("G", 2 * n + 3), ("D", n)]
    steps += [("D", FT // 2 - 1)]
    NS, LOOPS, UN = len(steps), 5, 6
    assert NS == 3 + LOOPS * UN
    F = pg.whole_hid
    (HH, HL), (FH, FL), (SH, SL) = pg.h_parts, pg.hid_parts, pg.w_parts
    mod_slot = pg.spare
    x = pg.x
    plain = lambda v: v.bitcast(F32)
    k_at = len(pg.stages)
    f0 = pg.fill
    NB = 6
    first_fill, f = [], f0
    for kind, _ in steps:
        first_fill.append(f)
        f += 4 if kind == "G" else 16
    fills, per_turn = f - f0, 2 * (4 + 4 + 16)
    first_fill.append(f)
    g0 = pg.take_groups(first_fill[1:NS - 1] + [f, f])
    pg.fill += fills
    high, split = pg.shared_sem("ffn_weights_high", NS), pg.shared_sem("ffn_weights_split", NS)
    silu = pg.shared_sem("ffn_silu", 2 * FT)
    hid_high, hid_split = pg.shared_sem("ffn_hidden_high", 2 * FT), pg.shared_sem("ffn_hidden_split", 2 * FT)
    if mod:
        m_w, m_row, m_out, m_bias = mod
        sums = pg.perm_left(4)
        row, row_loaded, row_ready = pg.whole[:, 2, :], pg.shared_sem("condition_loaded", 16), pg.shared_sem("condition_silu", 1)
        m_ready, m_used = pg.shared_sem("modulation_ready_0", 16 * MOD_GROUPS), pg.shared_sem("modulation_used", 2 * MOD_GROUPS)
    half = lambda s: slice(s * HALF, (s + 1) * HALF)

    def over_steps(e, step):
        step(0, 0)
        step(1, 0)

        def body(i):
            for u in range(UN):
                step(2 + u, i)
        repeat(e, LOOPS, body)
        step(NS - 1, 0)

    def mods(n):
        if not mod:
            return [], []
        if n == NS - 1:
            return [(FT, 0)], [(FT + 1, 0)]
        kind, t = steps[n]
        return [(t, 4 if n >= 2 else 0)] if kind == "G" else [], []

    def sync(e):
        def step(n, i):
            g = g0 + n
            if n < 2:
                pg.slot_free(e, g)
            else:
                split.wait(e, n - 1 + i * UN)
            kind, t = steps[n]
            src = w_gu if kind == "G" else w_down
            src = src[t] if n < 2 or n == NS - 1 else src[bass.ds(t + i * (4 if kind == "G" else 2), 1)].rearrange(
                "a p n -> (a p) n")
            e.dma_start(pg.slots[g % 2][:, 0:2048], src).then_inc(pg.w_ready[g % 2], 16)
        over_steps(e, step)

    def pool(e):
        e.wait_ge(pg.stage_done, 3 * k_at)
        e.dma_start(row, m_row).then_inc(row_loaded.sem, 16)

        def load(t, i, dynamic):
            if t:
                m_used.wait(e, 2 * t + (i * 8 if dynamic else 0))
            src = m_w[bass.ds(t + i * 4, 1)].rearrange("a p (b n) -> (a p) b n", b=2) if dynamic else (
                m_w[t].rearrange("p (b n) -> p b n", b=2))
            e.dma_start(mod_slot, src).then_inc(m_ready.sem, 16)
        load(0, 0, False)
        load(1, 0, False)
        repeat(e, LOOPS, lambda i: [load(t, i, True) for t in range(2, 6)])
        load(FT, 0, False)
        load(FT + 1, 0, False)

    def tensor(e):
        def step(n, i):
            split.wait(e, n + 1 + i * UN)
            kind, t = steps[n]
            wh, wl = SH[:, n % 2, :], SL[:, n % 2, :]
            if kind == "D":
                hid_split.wait(e, 4 * t + 4 + i * 8)
            for q in range(4 if kind == "G" else 16):
                ff = first_fill[n] + q
                if ff - f0 >= NB:
                    e.wait_ge(pg.ps_free, ff - NB + 1 + i * per_turn)
                bank = pg.ps[:, (ff - f0) % NB, :]
                if kind == "G":
                    s, part = divmod(q, 2)
                    terms = [((2 * k + part) * P, HH[:, k, half(s)], HL[:, k, half(s)]) for k in range(KT)]
                else:
                    tile, s = divmod(q, 2)
                    terms = [((8 * k + tile) * P, FH[:, (2 * t + k) % 4, half(s)], FL[:, (2 * t + k) % 4, half(s)])
                             for k in range(2)]
                for k, (at, hi, lo) in enumerate(terms):
                    w_hi, w_lo = wh[:, at:at + P], wl[:, at:at + P]
                    e.matmul(bank, w_hi, hi, start=(k == 0), stop=False)
                    e.matmul(bank, w_hi, lo, start=False, stop=False)
                    mm = e.matmul(bank, w_lo, hi, start=False, stop=(k == len(terms) - 1))
                mm.then_inc(pg.ps_full, 1)
        over_steps(e, step)

    def scalar(e):
        def take_high(n, i):
            g = g0 + n
            e.wait_ge(pg.w_ready[g % 2], 16 * (g // 2 + 1) + i * (8 * UN))
            if n >= 2:
                e.wait_ge(pg.ps_full, first_fill[n - 1] + i * per_turn)
            e.activation(SH[:, n % 2, :], pg.slots[g % 2][:, 0:2048], ACT.Copy).then_inc(high.sem, 1)

        def step(n, i):
            if n < NS - 1:
                take_high(n + 1, i)
            kind, t = steps[n]
            if kind == "G":
                for s in range(2):
                    ff = first_fill[n] + 2 * s
                    e.wait_ge(pg.ps_full, ff + 1 + i * per_turn)
                    if t >= 2:
                        hid_split.wait(e, 2 * (t - 2) + s + 1 + i * 8)
                    e.activation(F[:, t % 2, half(s)], pg.ps[:, (ff - f0) % NB, :], ACT.Silu).then_inc(silu.sem, 1)
                    e.wait_ge(pg.ps_free, ff + 2 + i * per_turn)
                    e.activation(FH[:, t % 4, half(s)], F[:, t % 2, half(s)], ACT.Copy).then_inc(hid_high.sem, 1)
        take_high(0, 0)
        if mod:
            row_loaded.wait(e, 16)
            e.activation(row, row, ACT.Silu).then_inc(row_ready.sem, 1)
        over_steps(e, step)

    def vector(e):
        def modulate(groups, i):
            for g, per in groups:
                m_ready.wait(e, 16 * (g + 1) + i * (16 * per))
                for t in range(2):
                    if g or t:
                        m_used.wait(e, 2 * g + t + i * (2 * per))
                    at = 2 * (g % 2) + t
                    e.tensor_tensor_reduce(pg.ps[:, 6:8, :].rearrange("p a b -> p (a b)"), mod_slot[:, t, :], row,
                                           1.0, 0.0, ALU.mult, ALU.add, sums[:, at:at + 1]).then_inc(m_used.sem, 1)
                m_used.wait(e, 2 * g + 2 + i * (2 * per))
                cols = slice(2 * g, 2 * g + 2) if not per else bass.ds(2 * g + i * (2 * per), 2)
                at = 2 * (g % 2)
                e.tensor_tensor(m_out[:, cols], sums[:, at:at + 2], m_bias[:, cols], ALU.add)

        def take_low(n, i):
            g = g0 + n
            high.wait(e, n + 1 + i * UN)
            e.tensor_tensor(SL[:, n % 2, :], pg.slots[g % 2][:, 0:2048], plain(SH[:, n % 2, :]), ALU.subtract).then_inc(split.sem, 1)

        def step(n, i):
            if n < NS - 1:
                take_low(n + 1, i)
            modulate(mods(n)[0], i)
            kind, t = steps[n]
            if kind == "G":
                for s in range(2):
                    ff = first_fill[n] + 2 * s
                    a = F[:, t % 2, half(s)]
                    silu.wait(e, 2 * t + s + 1 + i * 8)
                    e.wait_ge(pg.ps_full, ff + 2 + i * per_turn)
                    e.tensor_tensor(a, a, pg.ps[:, (ff + 1 - f0) % NB, :], ALU.mult).then_inc(pg.ps_free, 2)
                    hid_high.wait(e, 2 * t + s + 1 + i * 8)
                    e.tensor_tensor(FL[:, t % 4, half(s)], a, plain(FH[:, t % 4, half(s)]), ALU.subtract).then_inc(hid_split.sem, 1)
            else:
                e.wait_ge(pg.ps_free, first_fill[n] + i * per_turn)
                for q in range(16):
                    tile, s = divmod(q, 2)
                    ff = first_fill[n] + q
                    e.wait_ge(pg.ps_full, ff + 1 + i * per_turn)
                    e.scalar_tensor_tensor(out=x[:, tile, half(s)], in0=pg.ps[:, (ff - f0) % NB, :], scalar=gate(tile),
                                           in1=x[:, tile, half(s)], op0=ALU.mult, op1=ALU.add).then_inc(pg.ps_free, 1)
            modulate(mods(n)[1], i)
        take_low(0, 0)
        if mod:
            row_ready.wait(e, 1)
        over_steps(e, step)

    pg.stage(name=name, sync=sync, tensor=tensor, scalar=scalar, vector=vector, **({"gpsimd": pool} if mod else {}))


def block_1(pg):
    setup(pg)
    window_attention(pg)
    hgrn(pg)
    merge(pg)
    norm(pg, "norm_ffn_1", lambda s: pg.x[:, :, s * HALF:(s + 1) * HALF], lambda s: pg.whole[:, :, s * HALF:(s + 1) * HALF],
         [HALF, HALF], lambda s, k: pg.sc_ffn[:, k:k + 1], lambda s, k: pg.mod1[:, 24 + k, 0:1], parts=pg.h_parts)
    ffn(pg, "ffn_1", pg.d["w_gu1"], pg.d["w_down1"], lambda t: pg.mod1[:, 40 + t, 0:1],
        (pg.d["mod_w"], pg.d["cond_rows"][1], pg.mod2, pg.param("mod_b")))


C2 = 128
NCH = T // C2
TWO_SPANS = [(0, HALF), (HALF, T)]
HY_F = 33
TURN_HI = 6.28125
TURN_LO = 2.0 * math.pi - TURN_HI
ROUND = 1.5 * 2.0 ** 23


def linear_rows(pg, name, w, n_out, evac, engine):
    f0 = pg.fill
    g0 = pg.take_groups([f0 + 2])
    pg.fill += 2
    M = 64 * n_out

    def sync(e):
        pg.load(e, g0, w[0])

    def tensor(e):
        slot = pg.weights(e, g0)
        for s in range(2):
            f = f0 + s
            pg.bank_free(e, f)
            for k in range(KT):
                mm = e.matmul(pg.ps[0:M, f % 8, :], slot[:, k * M:(k + 1) * M], pg.h2[:, k, s * HALF:(s + 1) * HALF],
                              start=(k == 0), stop=(k == KT - 1))
            mm.then_inc(pg.ps_full, 1)

    def read(e):
        e.wait_ge(pg.ps_free, f0)
        for s in range(2):
            f = f0 + s
            e.wait_ge(pg.ps_full, f + 1)
            for t in range(n_out):
                ins = evac(e, t, s, pg.ps[64 * t:64 * t + 64, f % 8, :])
            ins.then_inc(pg.ps_free, 1)

    pg.stage(name=name, sync=sync, tensor=tensor, **{engine: read})


class Softplus:

    def __init__(self, pg, v, temps):
        self.v, self.t = v, temps
        self.asked, self.exps = pg.shared_sem("softplus_abs", 1), pg.shared_sem("softplus_exp", 1)
        self.ones, self.logs = pg.shared_sem("softplus_one_plus", 1), pg.shared_sem("softplus_log", 1)

    def scalar(self, e):
        a1, a2, a3, _ = self.t
        self.asked.wait(e, 1)
        e.activation(a1, a1, ACT.Exp, scale=-1.0).then_inc(self.exps.sem, 1)
        self.ones.wait(e, 1)
        e.activation(a3, a2, ACT.Ln).then_inc(self.logs.sem, 1)

    def vector(self, e, ch):
        v = self.v
        a1, a2, a3, a4 = self.t
        e.scalar_tensor_tensor(out=a1, in0=v, scalar=-1.0, in1=v, op0=ALU.mult, op1=ALU.max).then_inc(self.asked.sem, 1)
        self.exps.wait(e, 1)
        e.tensor_scalar(a2, a1, 1.0, None, ALU.add).then_inc(self.ones.sem, 1)
        self.logs.wait(e, 1)
        ch(e.tensor_scalar(a2, a2, -1.0, None, ALU.add))
        ch(e.tensor_scalar(a4, a2, 0.0, None, ALU.is_equal))
        ch(e.tensor_tensor(a2, a2, a4, ALU.add))
        ch(e.reciprocal(a2, a2))
        ch(e.tensor_tensor(a3, a3, a1, ALU.mult))
        ch(e.tensor_tensor(a3, a3, a2, ALU.mult))
        ch(e.tensor_tensor(a4, a4, a1, ALU.mult))
        ch(e.tensor_tensor(a3, a3, a4, ALU.add))
        ch(e.scalar_tensor_tensor(out=v, in0=v, scalar=0.0, in1=a3, op0=ALU.max, op1=ALU.add))


def row_of(pg, r):
    return pg.ident[0:64, r:r + 1].to_broadcast([64, P])


def both(lo, hi):
    return [(0, slice(0, 32), lo), (1, slice(32, 64), hi)]


def chunk_scan(e, ch, out, data, reset):
    ch(e.tensor_tensor_scan(out[0:32, :], reset[0:32, :], data[0:32, :], 0.0, ALU.mult, ALU.add))
    ch(e.tensor_tensor_scan(out[32:64, ::-1], reset[32:64, :], data[32:64, ::-1], 0.0, ALU.mult, ALU.add))


def dh_cols(v):
    return v.rearrange("p (d r) -> p d r", r=32)[:, :, 0:4]


def convolve(pg, e, ch, u, out, w, b, tile):
    n = 6
    ch(e.tensor_scalar(out[:, tile, :], u[:, tile, 1:T + 1], pg.col(w, n + tile), pg.col(b, tile), ALU.mult, ALU.add))
    ch(e.scalar_tensor_tensor(out=out[:, tile, :], in0=u[:, tile, 0:T], scalar=pg.col(w, tile), in1=out[:, tile, :],
                              op0=ALU.mult, op1=ALU.add))
    return e.scalar_tensor_tensor(out=out[:, tile, :], in0=u[:, tile, 2:T + 2], scalar=pg.col(w, 2 * n + tile),
                                  in1=out[:, tile, :], op0=ALU.mult, op1=ALU.add)


def to_fm(pg, name, y, tile0, gain=None, times=None, small=None, tokens=lambda c: slice(c * P, (c + 1) * P)):
    out = Mem(pg.big, M_Y2, M_W2)(KT, T)
    sums, roots, ready, turned, copied = (pg.shared_sem(f"to_fm_{n}", c) for n, c in (
        ("sums", 1 if gain else 0), ("roots", 1 if gain else 0), ("ready", NCH if gain else 0), ("turned", NCH),
        ("copied", NCH)))
    if gain:
        ss, rr, scr = small[:, 0:8], small[:, 8:16], small[:, 16:16 + 256]

    def vector(e):
        ch = pg.vchain(e)
        if gain:
            if times is not None:
                ch(e.tensor_tensor(y, y, times, ALU.mult))
            for c in range(NCH):
                ch(e.tensor_tensor_reduce(scr, y[:, c, :], y[:, c, :], 1.0, 0.0, ALU.mult, ALU.add, ss[:, c:c + 1]))
            e.drain().then_inc(sums.sem, 1)
            roots.wait(e, 1)
            ch(e.reciprocal(rr, rr))
            for c in range(NCH):
                e.scalar_tensor_tensor(out=y[:, c, :], in0=y[:, c, :], scalar=rr[:, c:c + 1], in1=pg.param(gain),
                                       op0=ALU.mult, op1=ALU.mult).then_inc(ready.sem, 1)

    def scalar(e):
        if gain:
            sums.wait(e, 1)
            e.activation(rr, ss, ACT.Sqrt, bias=pg.eps[:, 0:1], scale=1.0 / 256).then_inc(roots.sem, 1)
        for c in range(NCH):
            turned.wait(e, c + 1)
            e.activation(out[:, tile0:tile0 + 2, tokens(c)],
                         pg.ps[:, c % 2, 0:256].rearrange("p (a b) -> p a b", b=P), ACT.Copy).then_inc(copied.sem, 1)

    def tensor(e):
        for c in range(NCH):
            if gain:
                ready.wait(e, c + 1)
            if c >= 2:
                copied.wait(e, c - 1)
            for b in range(2):
                mm = e.transpose(pg.ps[:, c % 2, b * P:(b + 1) * P], y[:, c, b * P:(b + 1) * P], pg.ident)
            mm.then_inc(turned.sem, 1)

    pg.stage(name=name, vector=vector, scalar=scalar, tensor=tensor)


def ssd(pg):
    m = Mem(pg.big, M_W2, M_END)
    Z = m(NCH, 256)
    U = m(6, T + 2)
    XC = m(6, T)
    ST = m(2, NCH, 256)
    G = m(2, P)
    tri = m(2, P)
    acT, dtT, nac, ea, wc = (m(NCH, 8) for _ in range(5))
    cd, last = m(8, NCH), m(8, NCH)
    small = m(16)
    mu = Mem(pg.big, M_W2 + NCH * 256, M_END)
    XB = mu(NCH, 512)
    YT = mu(NCH, 256)
    mx_ = Mem(pg.big, M_W2 + NCH * 256 + 6 * (T + 2), M_END)
    Dd, Mm = mx_(8, P), mx_(8, P)
    my = Mem(pg.big, M_Y2 + 2 * T, M_W2)
    DT, A1, A2, A3, A4, reset = (my(T) for _ in range(6))
    rows = slice(0, 64)
    DTr, A1r, A2r, A3r, A4r, rr = (v[rows] for v in (DT, A1, A2, A3, A4, reset))
    xw = A2.rearrange("p (a b) -> p a b", a=4)
    off = A3[:, 0:512]
    off_d = A3[:, 512:768]
    scr = A4
    h = pg.h2
    k_at = len(pg.stages)
    tables = pg.sem("ssd_tables_loaded")

    linear_fm(pg, "ssd_in", pg.d["w_xbc"], KT, lambda k, a, b: h[:, k, a:b], 6, TWO_SPANS,
              lambda e, t, s, bank, ab: e.activation(U[:, t, 1 + ab[0]:1 + ab[1]], bank, ACT.Copy), "scalar")
    linear_rows(pg, "ssd_steps", pg.d["w_dt"], 1,
                lambda e, t, s, bank: e.activation(DTr[:, s * HALF:(s + 1) * HALF], bank, ACT.Identity,
                                                   bias=pg.col("dt_bias", parts=64)), "scalar")
    linear_tm(pg, "ssd_gate", pg.d["w_z"], lambda k, t: h[:, k, t * P:(t + 1) * P], list(range(NCH)), 256,
              lambda e, g, t, bank: e.activation(Z[:, t, :], bank, ACT.Silu), "scalar")

    sp = Softplus(pg, DTr, (A1r, A2r, A3r, A4r))
    conv, a_rd = pg.sem("ssd_convolved"), pg.sem("ssd_decay_rates")

    def pool(e):
        e.wait_ge(pg.stage_done, 3 * k_at)
        e.dma_start(tri, pg.d["tri_add"]).then_inc(tables, 16)
        e.dma_start(reset, pg.d["reset_128"]).then_inc(tables, 16)

    def vector(e):
        ch = pg.vchain(e)
        e.memset(U[:, :, 0:1], 0.0)
        ch(e.memset(U[:, :, T + 1:T + 2], 0.0))
        sp.vector(e, ch)
        e.wait_ge(a_rd, 1)
        ch(e.tensor_scalar(small[0:64, 1:2], small[0:64, 0:1], -1.0, None, ALU.mult))
        ch(e.tensor_scalar(A1r, DTr, small[0:64, 1:2], None, ALU.mult))
        e.wait_ge(tables, 32)
        chunk_scan(e, ch, A1r, A1r, rr)
        for t in range(6):
            convolve(pg, e, ch, U, XC, "cw", "cb", t).then_inc(conv, 1)

    def scalar(e):
        sp.scalar(e)
        e.activation(small[0:64, 0:1], pg.col("a_log", parts=64), ACT.Exp).then_inc(a_rd, 1)

    def scalar_after(e):
        for t in range(6):
            e.wait_ge(conv, t + 1)
            e.activation(XC[:, t, :], XC[:, t, :], ACT.Silu)

    pg.together("ssd_convolution", 1, gpsimd=pool, vector=vector, scalar=scalar, scalar_after=scalar_after)

    turned, copied, t_cols, c_cols = (pg.shared_sem(f"chunk_{n}", NCH) for n in (
        "turned", "turned_copied", "cols_turned", "cols_copied"))
    l_rd, l_cp, e_rd = pg.sem("ssd_ends"), pg.sem("ssd_ends_copied"), pg.sem("ssd_exps")

    def tensor(e):
        for c in range(NCH):
            if c >= 2:
                copied.wait(e, c - 1)
            for b in range(4):
                mm = e.transpose(pg.ps[:, c % 2, b * P:(b + 1) * P], XC[:, b, c * P:(c + 1) * P], pg.ident)
            mm.then_inc(turned.sem, 1)
            if c >= 2:
                c_cols.wait(e, c - 1)
            e.transpose(pg.ps[:, 2 + c % 2, 0:64], A1r[:, c * P:(c + 1) * P], pg.ident[0:64, 0:64])
            e.transpose(pg.ps[:, 2 + c % 2, 64:128], DTr[:, c * P:(c + 1) * P], pg.ident[0:64, 0:64]).then_inc(t_cols.sem, 1)
        for r in range(8):
            d, hh = divmod(r, 4)
            mm = e.matmul(pg.ps[:, 4, 8 * r:8 * r + 8], row_of(pg, 32 * d + hh),
                          A1r[:, (C2 - 1 if d == 0 else 0)::C2], start=True, stop=True)
        mm.then_inc(l_rd, 1)

    def scalar(e):
        for c in range(NCH):
            turned.wait(e, c + 1)
            e.activation(XB[:, c, :], pg.ps[:, c % 2, :], ACT.Copy).then_inc(copied.sem, 1)
        e.wait_ge(l_cp, 1)
        e.activation(ea, acT, ACT.Exp)
        e.activation(cd, last, ACT.Exp)
        e.activation(wc, wc, ACT.Exp).then_inc(e_rd, 1)

    def vector(e):
        ch = pg.vchain(e)
        for c in range(NCH):
            t_cols.wait(e, c + 1)
            e.tensor_copy(acT[:, c, :].rearrange("p (d r) -> p d r", d=2), dh_cols(pg.ps[:, 2 + c % 2, 0:64]))
            e.tensor_copy(dtT[:, c, :].rearrange("p (d r) -> p d r", d=2), dh_cols(pg.ps[:, 2 + c % 2, 64:128])).then_inc(c_cols.sem, 1)
        e.wait_ge(l_rd, 1)
        c_cols.wait(e, NCH)
        ch(e.tensor_copy(last, pg.ps[:, 4, 0:64].rearrange("p (r c) -> p r c", c=NCH)))
        ch(e.tensor_scalar(nac, acT, -1.0, None, ALU.mult))
        e.tensor_tensor(wc, last.rearrange("p r c -> p c r"), acT, ALU.subtract).then_inc(l_cp, 1)
        e.wait_ge(e_rd, 1)
        ch(e.tensor_tensor(wc, wc, dtT, ALU.mult))

    pg.stage(name="ssd_columns", tensor=tensor, scalar=scalar, vector=vector)

    order = [(s, d, s if d == 0 else NCH - 1 - s) for s in range(NCH - 1) for d in range(2)]
    w_rd, u_rd, s_rd = (pg.shared_sem(f"chunk_{n}", len(order)) for n in ("weighted", "updates", "states"))

    def tensor(e):
        for n, (s, d, c) in enumerate(order):
            w_rd.wait(e, n + 1)
            if n >= 2:
                s_rd.wait(e, n - 1)
            for b in range(2):
                mm = e.matmul(pg.ps[:, n % 2, b * P:(b + 1) * P], XB[:, c, 256 + b * P:256 + (b + 1) * P],
                              xw[:, n % 4, b * P:(b + 1) * P], start=True, stop=True)
            mm.then_inc(u_rd.sem, 1)

    def vector(e):
        ch = pg.vchain(e)
        e.memset(ST[:, 0, 0, :], 0.0)
        ch(e.memset(ST[:, 1, NCH - 1, :], 0.0))
        for n in range(len(order) + 2):
            if n < len(order):
                s, d, c = order[n]
                e.tensor_tensor(xw[:, n % 4, :].rearrange("p (h x) -> p h x", x=64),
                                XB[:, c, 0:256].rearrange("p (h x) -> p h x", x=64),
                                bc(wc[:, c, 4 * d:4 * d + 4], [P, 4, 64]), ALU.mult).then_inc(w_rd.sem, 1)
            if n >= 2:
                s, d, c = order[n - 2]
                nx = c + 1 if d == 0 else c - 1
                ch(e.tensor_tensor(ST[:, d, nx, :].rearrange("p (h x) -> p h x", x=64),
                                   ST[:, d, c, :].rearrange("p (h x) -> p h x", x=64),
                                   bc(cd[:, 4 * d:4 * d + 4, c], [P, 4, 64]), ALU.mult))
                u_rd.wait(e, n - 1)
                e.tensor_tensor(ST[:, d, nx, :], ST[:, d, nx, :], pg.ps[:, n % 2, 0:256], ALU.add).then_inc(s_rd.sem, 1)
                s_rd.wait(e, n - 1)

    pg.stage(name="ssd_states", tensor=tensor, vector=vector)

    p_rd, m_rd, x_rd, s2_rd, y_rd, y_cp = (pg.shared_sem(f"chunk_{n}", NCH) for n in (
        "products", "masked", "decays", "scores", "outputs", "summed"))
    g_cp = pg.sem("ssd_products_copied")

    def tensor(e):
        def pre(c):
            if c:
                e.wait_ge(g_cp, c)
                m_rd.wait(e, c)
            t = slice(c * P, c * P + P)
            for b in range(2):
                e.matmul(pg.ps[:, 0, b * P:(b + 1) * P], XC[:, 2 + b, t], XC[:, 4 + b, t], start=True, stop=True)
            for r in range(8):
                mm = e.matmul(pg.ps[:, 1 + r // 4, (r % 4) * P:(r % 4 + 1) * P], row_of(pg, 32 * (r // 4) + r % 4),
                              A1r[:, t], start=True, stop=True)
            mm.then_inc(p_rd.sem, 1)

        pre(0)
        for c in range(NCH):
            if c + 1 < NCH:
                pre(c + 1)
            s2_rd.wait(e, c + 1)
            if c:
                y_cp.wait(e, c)
            for hh in range(4):
                for d in range(2):
                    e.matmul(pg.ps[:, 3, hh * 64:hh * 64 + 64], Mm[:, 4 * d + hh, :], XB[:, c, hh * 64:hh * 64 + 64],
                             start=(d == 0), stop=(d == 1))
            for d in range(2):
                for b in range(2):
                    mm = e.matmul(pg.ps[:, 4, 256 * d + P * b:256 * d + P * b + P], XC[:, 4 + b, c * P:(c + 1) * P],
                                  ST[:, d, c, b * P:(b + 1) * P], start=True, stop=True)
            mm.then_inc(y_rd.sem, 1)

    def scalar(e):
        for c in range(NCH):
            p_rd.wait(e, c + 1)
            if c:
                s2_rd.wait(e, c)
            e.activation(G, pg.ps[:, 0, 0:256].rearrange("p (a b) -> p a b", b=P), ACT.Copy).then_inc(g_cp, 1)
            m_rd.wait(e, c + 1)
            for r in range(8):
                ins = e.activation(Dd[:, r, :], Dd[:, r, :], ACT.Exp, bias=nac[:, c, r:r + 1])
            ins.then_inc(x_rd.sem, 1)

    def vector(e):
        ch = pg.vchain(e)

        def masked(c):
            p_rd.wait(e, c + 1)
            for d in range(2):
                ins = e.tensor_tensor(Dd[:, 4 * d:4 * d + 4, :], pg.ps[:, 1 + d, :].rearrange("p (a b) -> p a b", b=P),
                                      tri[:, d:d + 1, :].to_broadcast([P, 4, P]), ALU.add)
            ins.then_inc(m_rd.sem, 1)

        masked(0)
        for c in range(NCH):
            x_rd.wait(e, c + 1)
            e.wait_ge(g_cp, c + 1)
            if c:
                y_rd.wait(e, c)
            for r in range(8):
                ins = e.scalar_tensor_tensor(out=Mm[:, r, :], in0=G[:, (r % 4) // 2, :], scalar=dtT[:, c, r:r + 1],
                                             in1=Dd[:, r, :], op0=ALU.mult, op1=ALU.mult)
            ins.then_inc(s2_rd.sem, 1)
            s2_rd.wait(e, c + 1)
            if c + 1 < NCH:
                masked(c + 1)
            ch(e.tensor_tensor(off_d.rearrange("p (h x) -> p h x", x=64), XB[:, c, 0:256].rearrange("p (h x) -> p h x", x=64),
                               bc(pg.param("ssd_d"), [P, 4, 64]), ALU.mult))
            y_rd.wait(e, c + 1)
            ch(e.tensor_tensor(off.rearrange("p (h x) -> p h x", x=64), pg.ps[:, 4, :].rearrange("p (h x) -> p h x", x=64),
                               bc(ea[:, c, :], [P, 8, 64]), ALU.mult))
            ch(e.tensor_tensor(YT[:, c, :], off_d, pg.ps[:, 3, 0:256], ALU.add))
            ch(e.tensor_tensor(YT[:, c, :], YT[:, c, :], off[:, 0:256], ALU.add))
            e.tensor_tensor(YT[:, c, :], YT[:, c, :], off[:, 256:512], ALU.add).then_inc(y_cp.sem, 1)
        y_cp.wait(e, NCH)

    pg.stage(name="ssd_outputs", tensor=tensor, scalar=scalar, vector=vector)
    to_fm(pg, "ssd_out", YT, 0, "ssd_g", Z, scr)


def neighbourhood(pg):
    m = Mem(pg.big, M_W2, M_END)
    kf = m(2, T)
    v, vs = m(NCH, 256), m(NCH - 1, 256)
    QD = m(2, 16, P)
    table, tmask = m(2, 15 * 64), m(2, 15 * 64)
    S = m(4, HALF)
    PT = m(2, 4, P)
    stat = m(4, 32)
    y = Mem(pg.big, M_Y2, M_W2)(KT, T)
    sq, rr = y[:, 4:6, :], y[:, 6, :]
    h = pg.h2
    k_at = len(pg.stages)
    tables, moved = pg.sem("na_tables_loaded"), pg.sem("na_values_moved")

    def pool(e):
        e.wait_ge(pg.stage_done, 3 * k_at)
        e.dma_start(table, pg.d["na_bias"]).then_inc(tables, 16)
        e.dma_start(tmask, pg.d["na_mask"]).then_inc(tables, 16)

    def vector(e):
        ch = pg.vchain(e)
        e.memset(QD, 0.0)
        e.wait_ge(tables, 32)
        ch(e.tensor_tensor(table, table, tmask, ALU.add))

    pg.stage(name="na_tables", gpsimd=pool, vector=vector)

    def q_out(e, t, s, bank, ab):
        for hh in range(2):
            r = slice(64 * hh, 64 * hh + 64)
            ins = e.activation(QD[r, t, 8 * s:8 * s + 8, 64 * hh:64 * hh + 64],
                               bank[r, :].rearrange("p (a b) -> p a b", b=64), ACT.Copy, scale=0.125)
        return ins
    linear_fm(pg, "na_q", pg.d["w_nq"], KT, lambda k, a, b: h[:, k, a:b], 2, TWO_SPANS, q_out, "scalar")
    linear_fm(pg, "na_k", pg.d["w_nk"], KT, lambda k, a, b: h[:, k, a:b], 2, TWO_SPANS,
              lambda e, t, s, bank, ab: e.activation(kf[:, t, ab[0]:ab[1]], bank, ACT.Copy), "scalar")
    linear_tm(pg, "na_v", pg.d["w_nv"], lambda k, t: h[:, k, t * P:(t + 1) * P], list(range(NCH)), 256,
              lambda e, g, t, bank: e.activation(v[:, t, :], bank, ACT.Copy), "scalar")
    k_mv = len(pg.stages)

    def pool(e):
        e.wait_ge(pg.stage_done, 3 * k_mv)
        e.dma_start(vs[0:64], v[64:128, 0:NCH - 1, :]).then_inc(moved, 16)
        e.dma_start(vs[64:128], v[0:64, 1:NCH, :]).then_inc(moved, 16)

    N = 32
    sc, sm, ex, pr, tr, pt, pv, yo = (pg.sem(f"na_{n}") for n in (
        "scores", "maxima", "exps", "probs", "turns", "turned", "outputs", "stored"))
    mx, nm, rs, ri = (stat[:, i, :] for i in range(4))

    def where(i):
        r, pair = divmod(i, 2)
        return r, pair, min(max(r - 4, 0), 8)

    def tensor(e):
        e.wait_ge(moved, 32)

        def scores(i):
            r, pair, base = where(i)
            if i >= 2:
                e.wait_ge(sm, i - 1)
            e.matmul(pg.ps[:, i % 2, :], QD[:, pair, r, :], kf[:, pair, base * 64:base * 64 + HALF],
                     start=True, stop=True).then_inc(sc, 1)

        def turn(i):
            e.wait_ge(pr, i + 1)
            if i >= 2:
                e.wait_ge(pt, i - 1)
            for b in range(4):
                mm = e.transpose(pg.ps[:, 2 + i % 2, b * P:(b + 1) * P], S[:, i % 4, b * P:(b + 1) * P], pg.ident)
            mm.then_inc(tr, 1)

        def values(i):
            r, pair, base = where(i)
            e.wait_ge(pt, i + 1)
            if i >= 2:
                e.wait_ge(yo, i - 1)
            for b in range(4):
                vv = v[:, base // 2 + b, :] if base % 2 == 0 else vs[:, base // 2 + b, :]
                mm = e.matmul(pg.ps[:, 4 + i % 2, 0:P], vv[:, pair * P:(pair + 1) * P], PT[:, i % 2, b, :],
                              start=(b == 0), stop=(b == 3))
            mm.then_inc(pv, 1)

        for i in range(N + 3):
            if i < N:
                scores(i)
            if 2 <= i < N + 2:
                turn(i - 2)
            if i >= 3:
                values(i - 3)

    def vector(e):
        ch = pg.vchain(e)
        for i in range(N + 1):
            if i < N:
                r, pair, base = where(i)
                e.wait_ge(sc, i + 1)
                if i >= 4:
                    e.wait_ge(tr, i - 3)
                dr = base - r + 7
                ch(e.tensor_tensor_reduce(S[:, i % 4, :], pg.ps[:, i % 2, :], table[:, pair, dr * 64:dr * 64 + HALF],
                                          1.0, -BIG, ALU.add, ALU.max, mx[:, i:i + 1]))
                e.tensor_scalar(nm[:, i:i + 1], mx[:, i:i + 1], -1.0, None, ALU.mult).then_inc(sm, 1)
            if i >= 1:
                q = i - 1
                e.wait_ge(ex, q + 1)
                ch(e.reciprocal(ri[:, q:q + 1], rs[:, q:q + 1]))
                e.tensor_scalar(S[:, q % 4, :], S[:, q % 4, :], ri[:, q:q + 1], None, ALU.mult).then_inc(pr, 1)

    def scalar(e):
        for i in range(N + 4):
            if i < N:
                e.wait_ge(sm, i + 1)
                e.activation(S[:, i % 4, :], S[:, i % 4, :], ACT.Exp, bias=nm[:, i:i + 1],
                             accum_out=rs[:, i:i + 1]).then_inc(ex, 1)
            if 2 <= i < N + 2:
                q = i - 2
                e.wait_ge(tr, q + 1)
                if q >= 2:
                    e.wait_ge(pv, q - 1)
                e.activation(PT[:, q % 2, :, :], pg.ps[:, 2 + q % 2, :].rearrange("p (a b) -> p a b", b=P),
                             ACT.Copy).then_inc(pt, 1)
            if i >= 4:
                q = i - 4
                r, pair, _ = where(q)
                e.wait_ge(pv, q + 1)
                for hh in range(2):
                    rw = slice(64 * hh, 64 * hh + 64)
                    ins = e.activation(y[rw, 2 + pair, r * 64:r * 64 + 64], pg.ps[rw, 4 + q % 2, 64 * hh:64 * hh + 64],
                                       ACT.Copy)
                ins.then_inc(yo, 1)

    pg.stage(name="na_attention", gpsimd=pool, tensor=tensor, vector=vector, scalar=scalar)

    squares, sums, roots = pg.sem("na_squares"), pg.sem("na_sums"), pg.sem("na_roots")

    def scalar(e):
        e.activation(sq, y[:, 2:4, :], ACT.Square).then_inc(squares, 1)
        e.wait_ge(sums, 1)
        pg.achain(e)(e.activation(rr, pg.ps[:, 0:2, :].rearrange("p a b -> p (a b)"), ACT.Ln, bias=pg.eps[:, 0:1],
                                  scale=1.0 / 256))
        e.activation(rr, rr, ACT.Exp, scale=-0.5).then_inc(roots, 1)

    def tensor(e):
        e.wait_ge(squares, 1)
        for s in range(2):
            for t in range(2):
                mm = e.matmul(pg.ps[:, s, :], pg.ones, sq[:, t, s * HALF:(s + 1) * HALF], start=(t == 0), stop=(t == 1))
        mm.then_inc(sums, 1)

    def vector(e):
        ch = pg.vchain(e)
        e.wait_ge(roots, 1)
        for t in range(2):
            ch(e.scalar_tensor_tensor(out=y[:, 2 + t, :], in0=y[:, 2 + t, :], scalar=pg.col("na_g", t), in1=rr,
                                      op0=ALU.mult, op1=ALU.mult))

    pg.stage(name="na_norm", tensor=tensor, vector=vector, scalar=scalar)


def mlstm(pg):
    m = Mem(pg.big, M_W2, M_END)
    qf, kf = m(2, T), m(2, T)
    KTm = m(NCH, 256)
    V1 = m(NCH, 4, 65)
    OG = m(NCH, 256)
    at = m.at
    YT = m(NCH, 256)
    ST = m(2, NCH, 2 * 65)
    Dd = m(8, P)
    cols = m(NCH, 4, 8)
    kw = m(4, 256)
    I2 = m(4, 65)
    H2 = m(256)
    cdb = m(4, NCH)
    tri = m(2, P)
    den = m(8)
    mp, rl, cdr = m(NCH), m(NCH), m(NCH)
    ssum, srt = m(32), m(32)
    reset = m(T)
    early = Mem(pg.big, at, M_END)
    A = [early(T)[0:64] for _ in range(4)]
    my = Mem(pg.big, M_Y2 + 4 * T, M_W2)
    LI, NB, R, WS = (my(T)[0:64] for _ in range(4))
    WI = Dd.rearrange("p a b -> p (a b)")[0:64]
    y_all = Mem(pg.big, M_Y2, M_W2)(KT, T)
    rr = reset[0:64]
    h = pg.h2
    k_at = len(pg.stages)
    tables = pg.sem("ml_tables_loaded")
    FM = lambda k, a, b: h[:, k, a:b]
    TM = lambda k, t: h[:, k, t * P:(t + 1) * P]

    def g_out(e, t, s, bank):
        a = slice(s * HALF, (s + 1) * HALF)
        if t == 0:
            return e.tensor_scalar(LI[:, a], bank, pg.col("ib", parts=64), None, ALU.add)
        return e.tensor_scalar(NB[:, a], bank, pg.col("fb", parts=64), -1.0, ALU.add, ALU.mult)
    linear_rows(pg, "ml_gates", pg.d["w_mg"], 2, g_out, "vector")
    linear_fm(pg, "ml_q", pg.d["w_mq"], KT, FM, 2, TWO_SPANS,
              lambda e, t, s, bank, ab: e.activation(qf[:, t, ab[0]:ab[1]], bank, ACT.Copy), "scalar")
    linear_fm(pg, "ml_k", pg.d["w_mk"], KT, FM, 2, TWO_SPANS,
              lambda e, t, s, bank, ab: e.activation(kf[:, t, ab[0]:ab[1]], bank, ACT.Copy, scale=0.125), "scalar")
    linear_tm(pg, "ml_v", pg.d["w_mv"], TM, list(range(NCH)), 256,
              lambda e, g, t, bank: e.activation(V1[:, t, :, 0:64], bank.rearrange("p (a b) -> p a b", b=64), ACT.Copy), "scalar")
    linear_tm(pg, "ml_o", pg.d["w_mo"], TM, list(range(NCH)), 256,
              lambda e, g, t, bank: e.activation(OG[:, t, :], bank, ACT.Sigmoid), "scalar")


    sp = Softplus(pg, NB, A)
    diff = pg.sem("ml_differences")

    def pool(e):
        e.wait_ge(pg.stage_done, 3 * k_at)
        e.dma_start(tri, pg.d["tri_add"]).then_inc(tables, 16)
        e.dma_start(reset, pg.d["reset_128"]).then_inc(tables, 16)

    def vector(e):
        ch = pg.vchain(e)
        ch(e.memset(V1[:, :, :, 64:65], 1.0))
        sp.vector(e, ch)
        e.wait_ge(tables, 32)
        chunk_scan(e, ch, A[0], NB, rr)
        ch(e.tensor_copy(NB, A[0]))
        ch(e.tensor_tensor(LI, LI, NB, ALU.add))
        ch(e.memset(mp, 0.0))
        for s in range(NCH):
            for d in range(2):
                c = s if d == 0 else NCH - 1 - s
                rw = slice(32 * d, 32 * d + 32)
                t = slice(c * C2, (c + 1) * C2)
                src, dst = LI[rw, t], R[rw, t]
                end = C2 - 1
                if d == 1:
                    src, dst, end = src[:, ::-1], dst[:, ::-1], 0
                ch(e.tensor_tensor_scan(dst, src, src, mp[rw, c:c + 1], ALU.max, ALU.max))
                e_at = c * C2 + end
                ch(e.tensor_copy(rl[rw, c:c + 1], R[rw, e_at:e_at + 1]))
                if s + 1 < NCH:
                    nx = c + 1 if d == 0 else c - 1
                    ch(e.tensor_tensor(mp[rw, nx:nx + 1], rl[rw, c:c + 1], NB[rw, e_at:e_at + 1], ALU.subtract))
        v3 = lambda v: v.rearrange("p (c t) -> p c t", t=C2)
        n64 = slice(0, 64)
        ch(e.tensor_tensor(v3(WI), bc(mp[n64], [64, NCH, C2]), v3(R), ALU.subtract))
        ch(e.tensor_tensor(NB, NB, R, ALU.subtract))
        ch(e.tensor_tensor(v3(WS), v3(LI), bc(rl[n64], [64, NCH, C2]), ALU.subtract))
        ch(e.tensor_scalar(R, R, -1.0, None, ALU.mult))
        e.tensor_tensor(cdr[n64], mp[n64], rl[n64], ALU.subtract).then_inc(diff, 1)

    def scalar_after(e):
        e.wait_ge(diff, 1)
        for v in (WI, NB, WS, cdr[0:64]):
            e.activation(v, v, ACT.Exp)

    pg.together("ml_rows", 4, gpsimd=pool, vector=vector, scalar=sp.scalar, scalar_after=scalar_after)

    turned, copied, t_cols, c_cols = (pg.shared_sem(f"chunk_{n}", NCH) for n in (
        "turned", "turned_copied", "cols_turned", "cols_copied"))
    c_rd = pg.sem("ml_carries")

    def tensor(e):
        for c in range(NCH):
            t = slice(c * P, (c + 1) * P)
            if c >= 2:
                copied.wait(e, c - 1)
            for b in range(2):
                mm = e.transpose(pg.ps[:, c % 2, b * P:(b + 1) * P], kf[:, b, t], pg.ident)
            mm.then_inc(turned.sem, 1)
            if c >= 2:
                c_cols.wait(e, c - 1)
            for n, v in enumerate((LI, WI, NB, WS)):
                mm = e.transpose(pg.ps[:, 2 + c % 2, 64 * n:64 * n + 64], v[:, t], pg.ident[0:64, 0:64])
            mm.then_inc(t_cols.sem, 1)
        for n in range(4):
            d, pair = divmod(n, 2)
            r = 32 * d + 2 * pair
            for j in range(2):
                mm = e.matmul(pg.ps[64 * j:64 * j + 64, 4, 8 * n:8 * n + 8],
                              pg.ident[0:64, r + j:r + j + 1].to_broadcast([64, 64]), cdr[0:64], start=True, stop=True)
        mm.then_inc(c_rd, 1)

    def scalar(e):
        for c in range(NCH):
            turned.wait(e, c + 1)
            e.activation(KTm[:, c, :], pg.ps[:, c % 2, 0:256], ACT.Copy).then_inc(copied.sem, 1)

    def vector(e):
        for c in range(NCH):
            t_cols.wait(e, c + 1)
            e.tensor_copy(cols[:, c, :, :].rearrange("p n (d r) -> p (n d) r", r=4),
                          pg.ps[:, 2 + c % 2, 0:256].rearrange("p (n r) -> p n r", r=32)[:, :, 0:4]).then_inc(c_cols.sem, 1)
        e.wait_ge(c_rd, 1)
        e.tensor_copy(cdb, pg.ps[:, 4, 0:32].rearrange("p (n c) -> p n c", c=NCH))

    pg.stage(name="ml_columns", tensor=tensor, scalar=scalar, vector=vector)

    order = [(s, d, s if d == 0 else NCH - 1 - s) for s in range(NCH - 1) for d in range(2)]
    w_rd, u_rd, s_rd = (pg.shared_sem(f"chunk_{n}", len(order)) for n in ("weighted", "updates", "states"))

    def tensor(e):
        for n, (s, d, c) in enumerate(order):
            w_rd.wait(e, n + 1)
            if n >= 2:
                s_rd.wait(e, n - 1)
            for hh in range(4):
                mm = e.matmul(pg.ps[64 * (hh % 2):64 * (hh % 2) + 64, n % 2, 65 * (hh // 2):65 * (hh // 2) + 65],
                              kw[:, n % 4, 64 * hh:64 * hh + 64], V1[:, c, hh, :], start=True, stop=True)
            mm.then_inc(u_rd.sem, 1)

    def vector(e):
        ch = pg.vchain(e)
        e.memset(ST[:, 0, 0, :], 0.0)
        ch(e.memset(ST[:, 1, NCH - 1, :], 0.0))
        for n in range(len(order) + 2):
            if n < len(order):
                s, d, c = order[n]
                e.tensor_tensor(kw[:, n % 4, :].rearrange("p (h x) -> p h x", x=64),
                                KTm[:, c, :].rearrange("p (h x) -> p h x", x=64),
                                bc(cols[:, c, 3, 4 * d:4 * d + 4], [P, 4, 64]), ALU.mult).then_inc(w_rd.sem, 1)
            if n >= 2:
                s, d, c = order[n - 2]
                nx = c + 1 if d == 0 else c - 1
                u_rd.wait(e, n - 1)
                for pair in range(2):
                    a = slice(65 * pair, 65 * pair + 65)
                    ins = e.scalar_tensor_tensor(out=ST[:, d, nx, a], in0=ST[:, d, c, a],
                                                 scalar=cdb[:, 2 * d + pair, c:c + 1], in1=pg.ps[:, n % 2, a],
                                                 op0=ALU.mult, op1=ALU.add)
                ins.then_inc(s_rd.sem, 1)
                s_rd.wait(e, n - 1)

    pg.stage(name="ml_states", tensor=tensor, vector=vector)

    q_cp = pg.shared_sem("chunk_turned_copied", NCH)
    QK = reset[:, 0:4 * P].rearrange("p (h t) -> p h t", t=P)
    DD = (Dd, kw.rearrange("p a (b c) -> p (a b) c", c=P))
    p_rd, m_rd, x2_rd, sc_rd, y_rd, y_cp = (pg.shared_sem(f"chunk_{n}", NCH) for n in (
        "products", "masked", "decays", "scores", "outputs", "summed"))

    def tensor(e):
        def pre(c):
            if c:
                m_rd.wait(e, c)
                q_cp.wait(e, c)
            t = slice(c * P, c * P + P)
            for hh in range(4):
                r = slice(64 * (hh % 2), 64 * (hh % 2) + 64)
                e.matmul(pg.ps[:, hh % 2, (hh // 2) * P:(hh // 2 + 1) * P], kf[r, hh // 2, t], qf[r, hh // 2, t], start=True, stop=True)
            for r in range(8):
                mm = e.matmul(pg.ps[:, 2 + r // 4, (r % 4) * P:(r % 4 + 1) * P], row_of(pg, 32 * (r // 4) + r % 4),
                              R[:, t], start=True, stop=True)
            mm.then_inc(p_rd.sem, 1)

        pre(0)
        for c in range(NCH):
            if c + 1 < NCH:
                pre(c + 1)
            sc_rd.wait(e, c + 1)
            if c:
                y_cp.wait(e, c)
            for d in range(2):
                for hh in range(4):
                    r = slice(64 * (hh % 2), 64 * (hh % 2) + 64)
                    a, at = slice(65 * hh, 65 * hh + 65), 65 * (2 * d + hh // 2)
                    e.matmul(pg.ps[:, 4 + d, a], DD[c % 2][:, 4 * d + hh, :], V1[:, c, hh, :], start=True, stop=True)
                    mm = e.matmul(pg.ps[:, 6 + hh % 2, at:at + 65], qf[r, hh // 2, c * P:(c + 1) * P],
                                  ST[r, d, c, 65 * (hh // 2):65 * (hh // 2) + 65], start=True, stop=True)
            mm.then_inc(y_rd.sem, 1)

    def scalar(e):
        for c in range(NCH):
            p_rd.wait(e, c + 1)
            if c:
                sc_rd.wait(e, c)
            e.activation(QK.rearrange("p (i j) t -> p i j t", j=2),
                         pg.ps[:, 0:2, 0:2 * P].rearrange("p j (i t) -> p i j t", t=P), ACT.Copy).then_inc(q_cp.sem, 1)
            m_rd.wait(e, c + 1)
            for r in range(8):
                ins = e.activation(DD[c % 2][:, r, :], DD[c % 2][:, r, :], ACT.Exp, bias=cols[:, c, 0, r:r + 1])
            ins.then_inc(x2_rd.sem, 1)

    def vector(e):
        ch = pg.vchain(e)

        def masked(c):
            p_rd.wait(e, c + 1)
            for d in range(2):
                ins = e.tensor_tensor(DD[c % 2][:, 4 * d:4 * d + 4, :], pg.ps[:, 2 + d, :].rearrange("p (a b) -> p a b", b=P),
                                      tri[:, d:d + 1, :].to_broadcast([P, 4, P]), ALU.add)
            ins.then_inc(m_rd.sem, 1)

        masked(0)
        for c in range(NCH):
            x2_rd.wait(e, c + 1)
            for d in range(2):
                ins = e.tensor_tensor(DD[c % 2][:, 4 * d:4 * d + 4, :], DD[c % 2][:, 4 * d:4 * d + 4, :], QK, ALU.mult)
            ins.then_inc(sc_rd.sem, 1)
            if c + 1 < NCH:
                masked(c + 1)
            y_rd.wait(e, c + 1)
            for d in range(2):
                four = slice(4 * d, 4 * d + 4)
                ch(e.tensor_tensor(I2.rearrange("p (i j) x -> p i j x", j=2),
                                   pg.ps[:, 6:8, 130 * d:130 * d + 130].rearrange("p j (i x) -> p i j x", x=65),
                                   bc(cols[:, c, 1, four].rearrange("p (i j) -> p i j", j=2), [P, 2, 2, 65]), ALU.mult))
                ch(e.tensor_tensor(I2, I2, pg.ps[:, 4 + d, 0:260].rearrange("p (a b) -> p a b", b=65), ALU.add))
                ch(e.scalar_tensor_tensor(out=den[:, four], in0=I2[:, :, 64], scalar=-1.0, in1=I2[:, :, 64],
                                          op0=ALU.mult, op1=ALU.max))
                ch(e.tensor_tensor(den[:, four], den[:, four], cols[:, c, 2, four], ALU.max))
                ch(e.reciprocal(den[:, four], den[:, four]))
                dst = YT[:, c, :] if d == 0 else H2
                ch(e.tensor_tensor(dst.rearrange("p (h x) -> p h x", x=64), I2[:, :, 0:64],
                                   bc(den[:, four], [P, 4, 64]), ALU.mult))
            e.tensor_tensor(YT[:, c, :], YT[:, c, :], H2, ALU.add).then_inc(y_cp.sem, 1)
        y_cp.wait(e, NCH)

    pg.stage(name="ml_outputs", tensor=tensor, scalar=scalar, vector=vector)

    sums, roots = pg.sem("ml_norm_sums"), pg.sem("ml_norm_roots")
    SQ = KTm

    def vector(e):
        ch = pg.vchain(e)
        heads = lambda v: v.rearrange("p c (h x) -> p (c h) x", x=64)
        ch(e.tensor_tensor(SQ, YT, YT, ALU.mult))
        e.tensor_reduce(ssum, heads(SQ), AX.X, ALU.add).then_inc(sums, 1)
        e.wait_ge(roots, 1)
        ch(e.reciprocal(srt, srt))
        ch(e.tensor_tensor(heads(YT), heads(YT), bc(srt, [P, 32, 64]), ALU.mult))
        ch(e.tensor_tensor(YT, YT, pg.param("ml_g").unsqueeze(1).to_broadcast([P, NCH, 256]), ALU.mult))
        ch(e.tensor_tensor(YT, YT, OG, ALU.mult))

    def scalar(e):
        e.wait_ge(sums, 1)
        e.activation(srt, ssum, ACT.Sqrt, bias=pg.eps[:, 0:1], scale=1.0 / 64).then_inc(roots, 1)

    pg.stage(name="ml_norm", vector=vector, scalar=scalar)
    to_fm(pg, "ml_out", YT, 4)


def hyena(pg):
    NF = KT
    m = Mem(pg.big, M_W2, M_END)
    U = Mem(pg.big, M_W2, M_END)(6, T + 2)
    FA, FB = m(NF, 512), m(NF, 512)
    Zt = m(3, NCH, 256)
    at = m.at
    SUM = m(NCH, 512)
    two = Mem(pg.big, at, M_END)
    YC, YS = two(KT, 256), two(KT, 256)
    alt = m(P + 1)
    odd_sums = m(512)
    small = Mem(pg.big, at, M_END)(16 + 256)
    XC = Mem(pg.big, M_H, M_HID)(6, T)
    HT = Mem(pg.big, M_H, M_HID)(NCH, 1024)
    early = Mem(pg.big, M_W2, M_END)
    feats, e1, e2, e3 = (early(T) for _ in range(4))
    w1, w2, w3 = early(64), early(64), early(1024)
    win = SUM.rearrange("p a b -> p (a b)")[:, 0:2048].rearrange("p (a b) -> p a b", b=256)
    scr = SUM.rearrange("p a b -> p (a b)")[:, 2048:4096].rearrange("p (a b) -> p a b", a=2)
    hy_norms = pg.perm_left(2 * 256)
    h = pg.h2
    tables = pg.sem("hy_tables_loaded")

    linear_fm(pg, "hy_in", pg.d["w_hy"], KT, lambda k, a, b: h[:, k, a:b], 6, TWO_SPANS,
              lambda e, t, s, bank, ab: e.activation(U[:, t, 1 + ab[0]:1 + ab[1]], bank, ACT.Copy), "scalar")
    conv = pg.sem("hy_convolved")
    turned, copied = pg.sem("hy_turned"), pg.sem("hy_turned_copied")

    def vector(e):
        ch = pg.vchain(e)
        e.memset(U[:, :, 0:1], 0.0)
        ch(e.memset(U[:, :, T + 1:T + 2], 0.0))
        for t in range(6):
            convolve(pg, e, ch, U, XC, "hcw", "hcb", t).then_inc(conv, 1)

    def tensor(e):
        n = 0
        for t in range(6):
            e.wait_ge(conv, t + 1)
            for half in range(2):
                if n >= 2:
                    e.wait_ge(copied, n - 1)
                for c in range(4):
                    mm = e.transpose(pg.ps[:, n % 2, c * P:(c + 1) * P], XC[:, t, 2 * c * P:2 * (c + 1) * P][:, half::2], pg.ident)
                mm.then_inc(turned, 1)
                n += 1

    def scalar(e):
        for n in range(12):
            t, half = divmod(n, 2)
            e.wait_ge(turned, n + 1)
            e.activation(Zt[:, t // 2, 4 * half:4 * half + 4, (t % 2) * P:(t % 2 + 1) * P],
                         pg.ps[:, n % 2, :].rearrange("p (a b) -> p a b", b=P), ACT.Copy).then_inc(copied, 1)

    pg.stage(name="hy_convolution", tensor=tensor, vector=vector, scalar=scalar)
    k_f = len(pg.stages)

    def pool(e):
        e.wait_ge(pg.stage_done, 3 * k_f)
        for dst, src in ((feats[0:HY_F], "hy_feats"), (w1[0:HY_F], "hy_w1"), (w2[0:64], "hy_w2"), (w3[0:64], "hy_w3"),
                         (win, "hy_window"), (alt, "alternate")):
            e.dma_start(dst, pg.d[src]).then_inc(tables, 16)

    a_rd, r_rd, s_rd, f_rd, f_cp = (pg.sem(f"hy_{n}") for n in ("layer", "angle", "sine", "filter", "filter_windowed"))
    r64 = slice(0, 64)

    def tensor(e):
        e.wait_ge(tables, 96)
        for layer in range(2):
            if layer:
                e.wait_ge(s_rd, 1)
            for s in range(2):
                mm = e.matmul(pg.ps[0:64, s, :], w1[0:HY_F] if layer == 0 else w2[r64],
                              (feats[0:HY_F] if layer == 0 else e1[r64])[:, s * HALF:(s + 1) * HALF], start=True, stop=True)
            mm.then_inc(a_rd, 1)
        e.wait_ge(s_rd, 2)
        for c in range(NCH):
            if c >= 2:
                e.wait_ge(f_cp, c - 1)
            for s in range(2):
                mm = e.matmul(pg.ps[:, 2 + 2 * (c % 2) + s, :], e1[r64, c * P:(c + 1) * P], w3[r64, s * HALF:(s + 1) * HALF],
                              start=True, stop=True)
            mm.then_inc(f_rd, 1)

    def scalar(e):
        for layer in range(2):
            e.wait_ge(r_rd, layer + 1)
            e.activation(e1[r64], e2[r64], ACT.Sin).then_inc(s_rd, 1)

    def vector(e):
        ch = pg.vchain(e)
        for layer in range(2):
            e.wait_ge(a_rd, layer + 1)
            x, k = e2[r64], e3[r64]
            ch(e.tensor_scalar(x, pg.ps[r64, 0:2, :].rearrange("p a b -> p (a b)"), pg.col("hb1" if layer == 0 else "hb2", parts=64),
                               pg.col("hfreq", layer, parts=64), ALU.add, ALU.mult))
            ch(e.tensor_scalar(k, x, 1.0 / (2.0 * math.pi), ROUND, ALU.mult, ALU.add))
            ch(e.tensor_scalar(k, k, -ROUND, None, ALU.add))
            ch(e.scalar_tensor_tensor(out=x, in0=k, scalar=-TURN_HI, in1=x, op0=ALU.mult, op1=ALU.add))
            ch(e.scalar_tensor_tensor(out=x, in0=k, scalar=-TURN_LO, in1=x, op0=ALU.mult, op1=ALU.add))
            e.tensor_scalar(x, x, 3.1415925, -3.1415925, ALU.min, ALU.max).then_inc(r_rd, 1)
        for c in range(NCH):
            e.wait_ge(f_rd, c + 1)
            for s in range(2):
                ins = e.tensor_tensor(HT[:, c, s * HALF:(s + 1) * HALF].rearrange("p (d x) -> p d x", d=2),
                                      pg.ps[:, 2 + 2 * (c % 2) + s, :].rearrange("p (d x) -> p d x", d=2),
                                      win[:, c:c + 1, :].to_broadcast([P, 2, 256]), ALU.mult)
            ins.then_inc(f_cp, 1)

    pg.stage(name="hy_network", gpsimd=pool, tensor=tensor, vector=vector, scalar=scalar)

    sq_rd, ss_rd, rt_rd = pg.sem("hy_squares"), pg.sem("hy_square_sums"), pg.sem("hy_roots")

    def tensor(e):
        for c in range(NCH):
            e.wait_ge(sq_rd, c + 1)
            for o in range(2):
                for d in range(2):
                    mm = e.matmul(pg.ps[:, o, 0:256], pg.ones, scr[:, c % 2, 512 * o + 256 * d:512 * o + 256 * d + 256],
                                  start=(c == 0 and d == 0), stop=(c == NCH - 1 and d == 1))
            mm.then_inc(ss_rd, 1)

    rn = hy_norms.rearrange("p (o x) -> p o x", o=2)

    def scalar(e):
        for c in range(NCH):
            if c >= 2:
                e.wait_ge(ss_rd, c - 1)
            e.activation(scr[:, c % 2, :], HT[:, c, :], ACT.Square).then_inc(sq_rd, 1)
        e.wait_ge(ss_rd, NCH)
        e.activation(rn, pg.ps[:, 0:2, 0:256], ACT.Sqrt, bias=pg.eps[:, 0:1]).then_inc(rt_rd, 1)

    def vector(e):
        ch = pg.vchain(e)
        for c in range(NCH):
            e.wait_ge(sq_rd, c + 1)
            if c == NCH // 2:
                e.wait_ge(ss_rd, NCH)
            if c == 0:
                ch(e.memset(HT[0:1, 0, :].rearrange("p (o d x) -> p o d x", o=2, d=2)[:, :, 1, :], 0.0))
            v = HT[:, c, :].rearrange("p (o d x) -> p o d x", o=2, d=2)
            s = SUM[:, c, :].rearrange("p (o x) -> p o x", o=2)
            ch(e.tensor_tensor(s, v[:, :, 0, :], v[:, :, 1, :], ALU.add))
            ch(e.tensor_tensor(v[:, :, 0, :], v[:, :, 0, :], v[:, :, 1, :], ALU.subtract))
        e.wait_ge(rt_rd, 1)
        ch(e.reciprocal(rn, rn))

    pg.stage(name="hy_filters", tensor=tensor, vector=vector, scalar=scalar)

    def groups(fills_of_group, n):
        g = pg.take_groups([pg.fill + fills_of_group * (i + 1) for i in range(n)])
        f = pg.fill
        pg.fill += fills_of_group * n
        return g, f

    def sync_of(g0, table):
        def sync(e):
            for n in range(4):
                pg.load(e, g0 + n, pg.d[table][n])
        return sync

    DIFF = HT.rearrange("p c (o d x) -> p c o d x", o=2, d=2)[:, :, :, 0, :]
    def forward(e, g0, f0, width, rhs, middle):
        for n in range(4):
            slot = pg.weights(e, g0 + n)
            for q in range(4):
                t, odd = divmod(q, 2)
                f = f0 + 4 * n + q
                pg.bank_free(e, f)
                for k in range(4 * odd, 4 * odd + 4):
                    mm = e.matmul(pg.ps[:, f % 8, 0:width], slot[:, (2 * k + t) * P:(2 * k + t + 1) * P], rhs(t, k),
                                  start=(k % 4 == 0), stop=(k % 4 == 3))
                mm.then_inc(pg.ps_full, 1)
        e.wait_ge(pg.ps_free, f0 + 16)
        for t in range(2):
            for k in range(4 * t, 4 * t + 4):
                mm = e.matmul(pg.ps[0:1, t, 0:width], alt[:, 0:1], rhs(t, k), start=(k % 4 == 0), stop=(k % 4 == 3))
        mm.then_inc(middle, 1)

    gF, fF = groups(4, 4)
    nyq = pg.sem("hy_middle_frequency")
    row_a, row_b = pg.spare[0:1, 0, :], pg.spare[0:1, 1, :]
    fM = row_a
    zM, rows = row_b[:, 0:512], row_b[:, 512:1024]

    def tensor(e):
        forward(e, gF, fF, 512, lambda t, k: SUM[:, k, :] if t == 0 else DIFF[:, k, :, :], nyq)

    odd_part = odd_sums

    def vector(e):
        ch = pg.vchain(e)
        e.wait_ge(pg.ps_free, fF)
        scaled = lambda out, bank: e.scalar_tensor_tensor(out=out, in0=bank, scalar=2.0 / (2 * T), in1=hy_norms[0:out.shape[0]],
                                                          op0=ALU.mult, op1=ALU.mult)
        for n in range(4):
            for t in range(2):
                F = (FA, FB)[t]
                f = fF + 4 * n + 2 * t
                e.wait_ge(pg.ps_full, f + 2)
                ch(scaled(F[:, n, :], pg.ps[:, f % 8, :]))
                scaled(odd_part, pg.ps[:, (f + 1) % 8, :]).then_inc(pg.ps_free, 2)
                e.wait_ge(pg.ps_free, f + 2)
                even_odd = (F[:, n, :], odd_part) if t == 0 else (odd_part, F[:, n, :])
                ch(e.tensor_tensor(F[:, 4 + n, :], even_odd[0], even_odd[1], ALU.subtract))
                ch(e.tensor_tensor(F[:, n, :], F[:, n, :], odd_part, ALU.add))
        ch(e.tensor_scalar(FA[0:1, 0, :], FA[0:1, 0, :], 0.5, None, ALU.mult))
        ch(e.tensor_scalar(FA[0:1, 4, :], FA[0:1, 4, :], 0.5, None, ALU.mult))
        e.wait_ge(nyq, 1)
        scaled(fM[:, 0:512], pg.ps[0:1, 0, :])
        ch(scaled(fM[:, 512:1024], pg.ps[0:1, 1, :]))

    pg.stage(name="hy_filter_dft", sync=sync_of(gF, "dft"), tensor=tensor, vector=vector)

    sums = Mem(pg.big, M_H, M_HID)(2, 4 * 256)
    work = Mem(pg.big, M_H + 2048, M_HID)
    PC, QS, C, S, W = (work(2, 256) for _ in range(5))
    for o in range(2):
        z, gate = Zt[:, 0, :, :], Zt[:, 1 + o, :, :]
        ch_o = slice(256 * o, 256 * o + 256)
        g1, f1 = groups(4, 4)
        nq, s_used = pg.shared_sem("hy_middle_of_z", 1), pg.shared_sem("hy_sums_used", 4)

        def tensor(e, g1=g1, f1=f1, z=z, nq=nq):
            forward(e, g1, f1, 256, lambda t, k: z[:, k, :], nq.sem)

        def scalar(e, f1=f1, s_used=s_used):
            e.wait_ge(pg.ps_free, f1)
            for n in range(4):
                if n >= 2:
                    s_used.wait(e, n - 1)
                for q in range(4):
                    f = f1 + 4 * n + q
                    e.wait_ge(pg.ps_full, f + 1)
                    e.activation(sums[:, n % 2, 256 * q:256 * q + 256], pg.ps[:, f % 8, 0:256], ACT.Copy).then_inc(pg.ps_free, 1)

        def vector(e, f1=f1, ch_o=ch_o, nq=nq, s_used=s_used):
            ch = pg.vchain(e)

            def product(C, S, W, fa, fb, pc, qs):
                ch(e.tensor_tensor(C, fa, pc, ALU.mult))
                ch(e.tensor_tensor(W, fb, qs, ALU.mult))
                ch(e.tensor_tensor(C, C, W, ALU.subtract))
                ch(e.tensor_tensor(S, fb, pc, ALU.mult))
                ch(e.tensor_tensor(W, fa, qs, ALU.mult))
                ch(e.tensor_tensor(S, S, W, ALU.add))

            for n in range(4):
                e.wait_ge(pg.ps_free, f1 + 4 * n + 4)
                ce, co, se, so = (sums[:, n % 2, 256 * q:256 * q + 256] for q in range(4))
                e.tensor_tensor(PC[:, 0, :], ce, co, ALU.add)
                e.tensor_tensor(PC[:, 1, :], ce, co, ALU.subtract)
                e.tensor_tensor(QS[:, 0, :], se, so, ALU.add)
                e.tensor_tensor(QS[:, 1, :], so, se, ALU.subtract).then_inc(s_used.sem, 1)
                s_used.wait(e, n + 1)
                product(C, S, W, FA[:, n::4, ch_o], FB[:, n::4, ch_o], PC, QS)
                e.tensor_tensor(YC[:, n, :], C[:, 0, :], C[:, 1, :], ALU.add)
                e.tensor_tensor(YC[:, 4 + n, :], C[:, 0, :], C[:, 1, :], ALU.subtract)
                e.tensor_tensor(YS[:, n, :], S[:, 0, :], S[:, 1, :], ALU.subtract)
                ch(e.tensor_tensor(YS[:, 4 + n, :], S[:, 0, :], S[:, 1, :], ALU.add))
            nq.wait(e, 1)
            ch(e.tensor_copy(rows.rearrange("p (a b) -> p a b", a=2), pg.ps[0:1, 0:2, 0:256]))
            fc, fs = fM[:, ch_o], fM[:, 512 + ch_o.start:512 + ch_o.stop]
            product(zM[:, 0:256], zM[:, 256:512], W[0:1, 0, :], fc, fs, rows[:, 0:256], rows[:, 256:512])

        pg.stage(name=f"hy_dft_{o}", sync=sync_of(g1, "dft"), tensor=tensor, scalar=scalar, vector=vector)

        g2, f2 = groups(2, 4)

        def tensor(e, g2=g2, f2=f2):
            for c in range(NCH):
                slot = pg.weights(e, g2 + c // 2)
                odd = c // 4
                f = f2 + c
                pg.bank_free(e, f)
                bank = pg.ps[:, f % 8, 0:256]
                for n in range(4):
                    for t in range(2):
                        at = (8 * (c % 2) + 2 * n + t) * P
                        e.matmul(bank, slot[:, at:at + P], (YC, YS)[t][:, 4 * odd + n, :], start=(n == 0 and t == 0), stop=False)
                e.matmul(bank, alt[0:1, 1:P + 1], zM[:, 256 * odd:256 * odd + 256], start=False, stop=True).then_inc(pg.ps_full, 1)

        def vector(e, f2=f2, z=z, gate=gate, o=o):
            ch = pg.vchain(e)
            e.wait_ge(pg.ps_free, f2)
            for n in range(NCH):
                f = f2 + n
                ch(e.tensor_tensor(z[:, n, :], z[:, n, :], pg.param("hskip")[:, 256 * o:256 * o + 256], ALU.mult))
                e.wait_ge(pg.ps_full, f + 1)
                e.tensor_tensor(z[:, n, :], z[:, n, :], pg.ps[:, f % 8, 0:256], ALU.add).then_inc(pg.ps_free, 1)
                e.wait_ge(pg.ps_free, f + 1)
                ch(e.tensor_tensor(z[:, n, :], z[:, n, :], gate[:, n, :], ALU.mult))

        pg.stage(name=f"hy_inverse_{o}", sync=sync_of(g2, "dft_inverse"), tensor=tensor, vector=vector)

    to_fm(pg, "hy_out", Zt[:, 0, :, :], 6, "hy_g", None, small,
          lambda c: slice(2 * P * (c % 4) + c // 4, 2 * P * (c % 4 + 1), 2))


def block_2(pg):
    x, h = pg.x, pg.h2

    def vector(e):
        ch = pg.vchain(e)
        ch(e.tensor_scalar(pg.sc2a, pg.mod2[:, 8:16], 1.0, None, ALU.add))
        ch(e.tensor_scalar(pg.sc2b, pg.mod2[:, 32:40], 1.0, None, ALU.add))
    pg.stage(name="scales_2", vector=vector)
    half = lambda v: (lambda s: v[:, :, s * HALF:(s + 1) * HALF])
    norm(pg, "norm_mix_2", half(x), half(h), [HALF, HALF], lambda s, k: pg.sc2a[:, k:k + 1], lambda s, k: pg.mod2[:, k:k + 1])
    ssd(pg)
    neighbourhood(pg)
    mlstm(pg)
    hyena(pg)
    y = Mem(pg.big, M_Y2, M_W2)(KT, T)

    def out(e, tile, s, bank, ab):
        xs = x[:, tile, ab[0]:ab[1]]
        return e.scalar_tensor_tensor(out=xs, in0=bank, scalar=pg.mod2[:, 16 + tile:17 + tile], in1=xs,
                                      op0=ALU.mult, op1=ALU.add)
    linear_split(pg, "merge_2", pg.d["w_out2"], out, act=y)
    norm(pg, "norm_ffn_2", half(x), half(pg.whole), [HALF, HALF], lambda s, k: pg.sc2b[:, k:k + 1], lambda s, k: pg.mod2[:, 24 + k:25 + k],
         parts=pg.h_parts)
    ffn(pg, "ffn_2", pg.d["w_gu2"], pg.d["w_down2"], lambda t: pg.mod2[:, 40 + t:41 + t])
    norm(pg, "norm_final", half(x), half(h), [HALF, HALF], lambda s, k: pg.col("final_g", k), None)
    pg.result = h


def block_2_layout(l0, o, gu):
    f = np.float32
    w = l0["w_in_2"]
    o["mod_w"] = row_groups(l0["mod_w_2"])
    o["w_z"] = tm_groups(w[:, 0:256], 256)
    o["w_xbc"] = fm_groups(w[:, 256:1024], 2)

    def rows(cols):
        k, n = cols.shape[:2]
        v = np.zeros((k, n, 2, 32), f)
        v[:, :, :, 0:4] = cols
        return v.reshape(KT, P, n * 64).transpose(1, 0, 2).reshape(1, P, -1)
    o["w_dt"] = rows(w[:, 1024:1032].reshape(D, 1, 2, 4))
    na = w[:, 1032:1800]
    o["w_nq"], o["w_nk"] = fm_groups(na[:, 0:256], 2), fm_groups(na[:, 256:512], 2)
    o["w_nv"] = tm_groups(na[:, 512:768], 256)
    ml = w[:, 1800:2840]
    o["w_mq"], o["w_mk"] = fm_groups(ml[:, 0:256], 2), fm_groups(ml[:, 256:512], 2)
    o["w_mv"], o["w_mo"] = tm_groups(ml[:, 512:768], 256), tm_groups(ml[:, 768:1024], 256)
    o["w_mg"] = rows(ml[:, 1024:1040].reshape(D, 2, 2, 4))
    o["w_hy"] = fm_groups(w[:, 2840:3608], 2)
    o["w_out2"] = fm_groups(l0["w_out_2"], 2)
    o["w_gu2"] = gu(l0["ffn_w_gate_2"], l0["ffn_w_up_2"])
    o["w_down2"] = down_groups(l0["ffn_w_down_2"])
    o["hy_w1"], o["hy_w2"], o["hy_w3"] = l0["hy_w1_2"], l0["hy_w2_2"], l0["hy_w3_2"]

    rpb = l0["na_rpb_2"]
    q, k = np.arange(64)[:, None], np.arange(64)[None]
    first = np.clip(q - 8, 0, 48)
    valid = (k >= first) & (k < first + 16)
    dist = np.where(valid, k - q + 15, 0)
    bias = np.where(valid[None, None], rpb[:, :, dist], f(0.0))
    o["na_bias"] = bias.transpose(0, 2, 1, 3).reshape(2, P, 15 * 64).transpose(1, 0, 2)
    mask = np.where(valid, 0, -BIG).astype(f)
    mask = np.broadcast_to(mask[None, :, None], (2, 64, 15, 64)).reshape(P, 1, 960)
    o["na_mask"] = np.broadcast_to(mask, (P, 2, 960))

    s, t = np.arange(P)[:, None], np.arange(P)[None]
    o["tri_add"] = np.stack([np.where(s <= t, 0, -BIG), np.where(s >= t, 0, -BIG)], 1).astype(f)
    o["reset_128"] = np.broadcast_to((np.arange(T) % C2 != 0).astype(f), (P, T))

    bands = (HY_F - 1) // 2
    tt = np.linspace(0.0, 1.0, T, dtype=f)
    ff = np.linspace(1e-4, bands - 1, bands, dtype=f)
    ang = (f(2.0 * math.pi) * (np.arange(T, dtype=f) / f(T))[:, None] * ff[None]).astype(f)
    n = np.arange(T)
    order = np.concatenate([n[0::2], n[1::2]])
    o["hy_feats"] = np.concatenate([tt[:, None], np.cos(ang), -np.sin(ang)], 1).astype(f)[order].T
    deltas = np.abs(np.linspace(math.log(1e-2) / 1.5, math.log(1e-2) / 0.3, 256, dtype=f))
    o["hy_window"] = np.exp(-tt[:, None] * deltas[None]).astype(f)[order].reshape(NCH, P, 256).transpose(1, 0, 2)
    turns = (order[:, None] * n[None, 0:T // 2]) % (2 * T) * (np.pi / T)
    waves = np.stack([np.cos(turns), np.sin(turns)]).astype(f).reshape(2, KT, P, KT // 2, P)
    o["dft"] = waves.transpose(3, 2, 1, 0, 4).reshape(KT // 2, P, 2 * D)
    o["dft_inverse"] = waves.reshape(2, KT // 2, 2, P, KT // 2, P).transpose(1, 5, 2, 4, 0, 3).reshape(KT // 2, P, 2 * D)
    alt = np.zeros((P, P + 1), f)
    alt[:, 0] = (-1.0) ** np.arange(P)
    alt[0, 1:] = (-1.0) ** np.arange(P)
    o["alternate"] = alt


def build_program(nc, dram, out):
    with ExitStack() as ctx:
        pg = Program(nc, ctx, dram)
        block_1(pg)
        block_2(pg)
        stages = pg.stages
        stored = pg.sem("output_stored")
        block = ctx.enter_context(nc.Block())

        def compute(e, engine):
            for n, st in enumerate(stages):
                if engine in st:
                    st[engine](e)
                e.drain().then_inc(pg.stage_done, 1)
                e.wait_ge(pg.stage_done, 3 * (n + 1))

        @block.sync
        def _(e):
            for st in stages:
                if "sync" in st:
                    st["sync"](e)
            e.wait_ge(pg.stage_done, 3 * len(stages))
            e.dma_start(out, pg.result).then_inc(stored, 16)
            e.wait_ge(stored, 16)

        @block.gpsimd
        def _(e):
            for st in stages:
                if "gpsimd" in st:
                    st["gpsimd"](e)

        @block.tensor
        def _(e):
            compute(e, "tensor")

        @block.scalar
        def _(e):
            compute(e, "scalar")

        @block.vector
        def _(e):
            compute(e, "vector")
        return pg


def fm_groups(w, per):
    k, n = w.shape
    return w.reshape(k // P, P, n // (per * P), per, P).transpose(2, 1, 0, 3, 4).reshape(n // (per * P), P, -1)


def row_groups(w):
    return w.T.reshape(-1, 2, P, D).transpose(0, 2, 1, 3).reshape(-1, P, 2 * D)


def down_groups(w):
    return w.reshape(FT // 2, 2, P, D).transpose(0, 2, 1, 3).reshape(FT // 2, P, 2 * D)


def tm_groups(w, cols):
    k, n = w.shape
    return w.reshape(k // P, P, n // cols, cols).transpose(2, 1, 0, 3).reshape(n // cols, P, -1)


def column(v):
    return v.reshape(-1, P).T


def rows_of(v, n=4):
    c = np.zeros((P, 1), v.dtype)
    c[0:n, 0] = v[0]
    c[32:32 + n, 0] = v[1]
    return c


def constants():
    f = np.float32
    c = {"ident": np.eye(P, dtype=f), "ones_64": np.kron(np.eye(2), np.ones((64, 64))).astype(f)}
    pos = np.arange(T)
    inv = (f(10000.0) ** (-np.arange(0, 32, 2, dtype=f) / f(32))).astype(f)
    d = np.arange(P) % 64
    at = np.where((d < 32)[:, None], (pos // 64)[None], (pos % 64)[None]).astype(f)
    ang = at * inv[d % 16][:, None]
    c["rope_cos"], c["rope_sin"] = np.cos(ang).astype(f), np.sin(ang).astype(f)
    turn = np.zeros((P, P), f)
    for m in range(P):
        turn[m + 16 if m % 32 < 16 else m - 16, m] = -1.0 if m % 32 < 16 else 1.0
    c["rope_turn"] = turn
    qi, kj = np.arange(P)[:, None], np.arange(P)[None]
    masks = np.zeros((P, 3, 640), f)
    masks[:, :, 256:384] = np.where(kj >= qi, 0, -BIG)[:, None]
    masks[:, :, 512:640] = np.where(kj <= qi, 0, -BIG)[:, None]
    masks[:, 1, 256:384] = -BIG
    masks[:, 2, 512:640] = -BIG
    c["window_masks"] = masks
    same = qi // 32 == kj // 32
    c["tri_32"] = np.stack([same & (qi <= kj), same & (qi >= kj)], 1).astype(np.int32)
    c["reset_32"] = np.broadcast_to((np.arange(TA) % 32 != 0).astype(f), (P, TA)).copy()
    return c


def lay_out(i):
    g = {k: np.asarray(v) for k, v in i.items()}
    l0 = {k: v[0] for k, v in g.items() if k not in ("hgrn_lb_logits", "c_ctx", "final_norm_g_2")}
    o = constants()
    w = l0["w_in"]
    o["x_t"] = l0["x"].T.reshape(KT, P, T).transpose(1, 0, 2)
    o["ctx_t"] = l0["ctx"].T.reshape(KT, P, TC).transpose(1, 0, 2)
    o["w_ada"] = fm_groups(l0["w_ada"][:, 0:P * MOD_FIRST], 2)
    o["w_ada_rest"] = row_groups(l0["w_ada"][:, P * MOD_FIRST:])
    o["cond_rows"] = np.stack([np.broadcast_to(v.reshape(1, D), (P, D)) for v in (l0["c"], l0["c_2"], g["c_ctx"])])
    heads = [h * 64 + n for j in range(4) for h in (j, 4 + j) for n in range(64)]
    o["w_q"] = fm_groups(w[:, 2816:3328][:, heads], 2)
    o["w_k"] = fm_groups(w[:, 1536:1664], 1)
    o["w_v"] = tm_groups(w[:, 1664:1792], P)
    o["w_inp"] = tm_groups(w[:, 1024:1536], 256)
    hg = []
    for h in range(4):
        c = slice(h * P, h * P + P)
        hg.append(fm_groups(np.concatenate([w[:, 0:512][:, c], w[:, 512:1024][:, c]], 1), 2)[0])
        hg.append(fm_groups(np.concatenate([w[:, 1792:2304][:, c], w[:, 2304:2816][:, c]], 1), 2)[0])
    o["w_hgrn"] = np.stack(hg)
    gates = w[:, 3328:5376]
    o["w_merge"] = np.concatenate([fm_groups(l0["w_branch_hgrn"], 1), fm_groups(l0["w_branch_attn"][heads], 1),
                                   fm_groups(gates[:, 0:D], 1), fm_groups(gates[:, D:], 1)], 2)
    o["w_out1"] = fm_groups(l0["w_out"], 2)

    def gu(a, b):
        k, n = a.shape
        return fm_groups(np.stack([a.reshape(k, n // P, P), b.reshape(k, n // P, P)], 2).reshape(k, 2 * n), 2)
    o["w_gu1"] = gu(l0["w_ffn_gate"], l0["w_ffn_up"])
    o["w_down1"] = down_groups(l0["w_ffn_down"])
    block_2_layout(l0, o, gu)

    pp = np.zeros((P, NPP), np.float32)

    def put(name, v):
        at, n = PP[name]
        pp[:, at:at + n] = v

    def wide(v):
        return np.broadcast_to(v.reshape(1, -1), (P, v.size))
    put("cond", np.stack([column(l0["c"]), column(g["c_ctx"]), column(l0["c_2"])], 2).reshape(P, -1))
    put("b_ada", column(l0["b_ada"]))
    put("mod_b", column(l0["mod_b_2"]))
    put("norm_mix", column(l0["norm_mix_w"]))
    put("norm_ffn", column(l0["norm_ffn_w"]))
    put("final_g", column(g["final_norm_g_2"]))
    put("lb", column(g["hgrn_lb_logits"]))
    put("hg_norm", column(l0["hgrn_norm_w"]))
    put("q_norm", column(np.concatenate([l0["q_norm_w"]] * 2)))
    put("k_norm", column(np.concatenate([l0["k_norm_w"]] * 2)))
    put("sink", wide(l0["attn_sinks"]))
    put("cw", column(l0["ssd_conv_w_2"]))
    put("cb", column(l0["ssd_conv_b_2"]))
    put("dt_bias", rows_of(l0["ssd_dt_bias_2"]))
    put("a_log", rows_of(l0["ssd_a_log_2"]))
    put("ssd_d", wide(l0["ssd_d_2"]))
    put("ssd_g", wide(l0["ssd_norm_g_2"]))
    put("na_g", column(l0["na_norm_g_2"]))
    put("ib", rows_of(l0["ml_i_bias_2"]))
    put("fb", rows_of(l0["ml_f_bias_2"]))
    put("ml_g", wide(l0["ml_norm_g_2"]))
    put("hcw", column(l0["hy_conv_w_2"]))
    put("hcb", column(l0["hy_conv_b_2"]))
    pad = np.zeros(64, np.float32)
    put("hb1", column(np.concatenate([l0["hy_b1_2"], pad])))
    put("hb2", column(np.concatenate([l0["hy_b2_2"], pad])))
    put("hfreq", column(np.stack([np.concatenate([l0["hy_freq_2"][n], pad]) for n in range(2)])))
    put("hskip", wide(l0["hy_skip_2"]))
    put("hy_g", wide(l0["hy_norm_g_2"]))
    o["params"] = pp
    return {k: np.ascontiguousarray(v) for k, v in o.items()}


def kernel(**inputs):
    import concourse.bacc as _bacc
    from concourse.bass_utils import run_bass_kernel_spmd as _run

    nc = _bacc.Bacc("TRN2", target_bir_lowering=False, num_devices=1)
    arrays = lay_out(inputs)
    dram = {n: nc.dram_tensor(f"in_{n}", list(a.shape), mybir.dt.from_np(a.dtype), kind="ExternalInput").ap()
            for n, a in arrays.items()}
    out = nc.dram_tensor("out_x", [P, KT, T], F32, kind="ExternalOutput").ap()
    build_program(nc, dram, out)
    r = _run(nc, [{f"in_{n}": a for n, a in arrays.items()}], core_ids=[0])
    got = r.results[0]["out_x"]
    return got.transpose(1, 0, 2).reshape(1, D, T).transpose(0, 2, 1)
```
